# Optimizing a Trainium2 kernel written in Bass

```python
import functools
import jax, jax.numpy as jnp
from jax import lax
import numpy as np

D_MODEL = 1024
BATCH = 1
SEQ = 512
DEPTH = 1
DEC_BATCH = 8
DEC_SEQ = 1
PAST_LEN = 256
PAGE_SIZE = 128

HEAD_DIM = 64
N_HEADS_A = 8
N_HEADS_B = 8
N_IDX_HEADS = 8
IDX_DIM = 64
TOPK_MAX = 256
D_FF = 4 * D_MODEL
Q_BLOCK = 128
FORGET_BIAS = 2.0
EPS = 1e-6
MASK_VALUE = -1e30
WIDTH_A = N_HEADS_A * HEAD_DIM
WIDTH_B = N_HEADS_B * HEAD_DIM
IN_SIZES = (WIDTH_A, WIDTH_A, WIDTH_A, WIDTH_B, WIDTH_B, WIDTH_B, N_IDX_HEADS * IDX_DIM, IDX_DIM, N_IDX_HEADS, N_HEADS_B, D_MODEL, D_MODEL)
D_IN = 3 * WIDTH_A + 3 * WIDTH_B + N_IDX_HEADS * IDX_DIM + IDX_DIM + N_IDX_HEADS + N_HEADS_B + 2 * D_MODEL

kernel_name = 'hybrid_dsa_fox_decode_step'

def rms_norm(x, g):
    xf = x.astype(jnp.float32)
    y = xf * lax.rsqrt(jnp.mean(xf * xf, axis=-1, keepdims=True) + EPS)
    return (y * g.astype(jnp.float32)).astype(x.dtype)

def topk_count(n_keys):
    return max(1, min(TOPK_MAX, n_keys // 4))

def alibi_slopes():
    return jnp.exp2(-8.0 * jnp.arange(1, N_HEADS_A + 1, dtype=jnp.float32) / N_HEADS_A)

def take_rows(a, idx):
    return jax.vmap(lambda ab, ib: ab[ib])(a, idx)

def project(h, w_in, b_forget, g_qa, g_ka, g_qb, g_kb):
    B, T, _ = h.shape
    z = h @ w_in
    cuts = [int(i) for i in np.cumsum(IN_SIZES)[:-1]]
    qa, ka, va, qb, kb, vb, qi, ki, wi, fl, ga, gb = jnp.split(z, cuts, axis=-1)
    heads = lambda a, n: a.reshape(B, T, n, HEAD_DIM)
    qa = rms_norm(heads(qa, N_HEADS_A), g_qa)
    ka = rms_norm(heads(ka, N_HEADS_A), g_ka)
    va = heads(va, N_HEADS_A)
    qb = rms_norm(heads(qb, N_HEADS_B), g_qb)
    kb = rms_norm(heads(kb, N_HEADS_B), g_kb)
    vb = heads(vb, N_HEADS_B)
    qi = qi.reshape(B, T, N_IDX_HEADS, IDX_DIM)
    wi = wi * (N_IDX_HEADS ** -0.5)
    logf = jax.nn.log_sigmoid((fl + b_forget).astype(jnp.float32)).astype(h.dtype)
    return qa, ka, va, qb, kb, vb, qi, ki, wi, logf, ga, gb

def index_scores(qi, wi, ki, qpos, kpos):
    s = jnp.einsum('bthd,bsd->bths', qi, ki).astype(jnp.float32) * (IDX_DIM ** -0.5)
    s = jnp.einsum('bths,bth->bts', jax.nn.relu(s), wi.astype(jnp.float32))
    return jnp.where(kpos[None, None, :] <= qpos[None, :, None], s, MASK_VALUE)

def sparse_attend(q, k_sel, v_sel, qpos, sel):
    logits = jnp.einsum('bthd,btkhd->bhtk', q, k_sel).astype(jnp.float32) * (HEAD_DIM ** -0.5)
    dist = (qpos[None, :, None] - sel).astype(jnp.float32)
    logits = logits - alibi_slopes()[None, :, None, None] * dist[:, None]
    logits = jnp.where((dist >= 0)[:, None], logits, MASK_VALUE)
    p = jax.nn.softmax(logits, axis=-1).astype(v_sel.dtype)
    return jnp.einsum('bhtk,btkhd->bthd', p, v_sel)

def forget_attend(q, k, v, Fq, Fk, qpos, kpos):
    logits = jnp.einsum('bthd,bshd->bhts', q, k).astype(jnp.float32) * (HEAD_DIM ** -0.5)
    logits = logits + (jnp.transpose(Fq, (0, 2, 1))[:, :, :, None] - jnp.transpose(Fk, (0, 2, 1))[:, :, None, :])
    logits = jnp.where((kpos[None, :] <= qpos[:, None])[None, None], logits, MASK_VALUE)
    p = jax.nn.softmax(logits, axis=-1).astype(v.dtype)
    return jnp.einsum('bhts,bshd->bthd', p, v)

def prompt_mix(qa, ka, va, qb, kb, vb, qi, ki, wi, logf):
    B, S = qa.shape[:2]
    n_blk = S // Q_BLOCK
    k_top = topk_count(S)
    pos = jnp.arange(S)
    F = jnp.cumsum(logf.astype(jnp.float32), axis=1)

    def blocks(a):
        return jnp.moveaxis(a.reshape(B, n_blk, Q_BLOCK, *a.shape[2:]), 1, 0)

    def one_block(args):
        qa_b, qi_b, wi_b, qb_b, F_b, qpos = args
        scores = index_scores(qi_b, wi_b, ki, qpos, pos)
        _, sel = lax.top_k(scores, k_top)
        oa_b = sparse_attend(qa_b, take_rows(ka, sel), take_rows(va, sel), qpos, sel)
        ob_b = forget_attend(qb_b, kb, vb, F_b, F, qpos, pos)
        return oa_b, ob_b

    oa, ob = lax.map(one_block, (blocks(qa), blocks(qi), blocks(wi), blocks(qb), blocks(F), pos.reshape(n_blk, Q_BLOCK)))
    unblock = lambda a: jnp.moveaxis(a, 0, 1).reshape(B, S, *a.shape[3:])
    return unblock(oa), unblock(ob)

def sample_mix(layer, cache_k_a, cache_v_a, cache_k_idx, cache_k_b, cache_v_b, cache_logf_b, page_table,
               qa, ka, va, qb, kb, vb, qi, ki, wi, logf):
    DB, T = qa.shape[:2]
    page = cache_k_a.shape[2]
    past = page_table.shape[1] * page
    L = past + T
    qpos = past + jnp.arange(T)
    kpos = jnp.arange(L)

    def paged_rows(pool):
        return pool[layer, page_table].reshape(DB, past, *pool.shape[3:])

    def gather_selected(pool, new, sel):
        in_past = sel < past
        ps = jnp.minimum(sel, past - 1)
        phys = jax.vmap(lambda pt, i: pt[i])(page_table, ps // page)
        rows_past = pool[layer, phys, ps % page]
        rows_new = take_rows(new, jnp.clip(sel - past, 0, T - 1))
        return jnp.where(in_past[..., None, None], rows_past, rows_new)

    ki_all = jnp.concatenate([paged_rows(cache_k_idx), ki], axis=1)
    scores = index_scores(qi, wi, ki_all, qpos, kpos)
    _, sel = lax.top_k(scores, topk_count(L))
    oa = sparse_attend(qa, gather_selected(cache_k_a, ka, sel), gather_selected(cache_v_a, va, sel), qpos, sel)
    kb_all = jnp.concatenate([paged_rows(cache_k_b), kb], axis=1)
    vb_all = jnp.concatenate([paged_rows(cache_v_b), vb], axis=1)
    F = jnp.cumsum(jnp.concatenate([paged_rows(cache_logf_b), logf], axis=1).astype(jnp.float32), axis=1)
    ob = forget_attend(qb, kb_all, vb_all, F[:, past:], F, qpos, kpos)
    return oa, ob

def run_layer(x, c, mix, w_ada, b_ada, g_norm1, w_in, b_forget, g_qa, g_ka, g_qb, g_kb,
              w_o_a, w_o_b, w_out, g_norm2, w_up, w_down):
    B, T, _ = x.shape
    mod = (jax.nn.silu(c) @ w_ada + b_ada)[:, None, :]
    shift1, scale1, gate1, shift2, scale2, gate2 = jnp.split(mod, 6, axis=-1)
    h = rms_norm(x, g_norm1) * (1.0 + scale1) + shift1
    qa, ka, va, qb, kb, vb, qi, ki, wi, logf, ga, gb = project(h, w_in, b_forget, g_qa, g_ka, g_qb, g_kb)
    oa, ob = mix(qa, ka, va, qb, kb, vb, qi, ki, wi, logf)
    merged = (jax.nn.sigmoid(ga) * (oa.reshape(B, T, WIDTH_A) @ w_o_a)
              + jax.nn.sigmoid(gb) * (ob.reshape(B, T, WIDTH_B) @ w_o_b))
    x = x + gate1 * (merged @ w_out)
    h2 = rms_norm(x, g_norm2) * (1.0 + scale2) + shift2
    x = x + gate2 * (jnp.square(jax.nn.relu(h2 @ w_up)) @ w_down)
    return x, (ka, va, ki, kb, vb, logf)

def setup_inputs(seed: int = 0) -> dict:
    key = jax.random.key(seed)
    ks = jax.random.split(key, 32)
    n_pages = PAST_LEN // PAGE_SIZE
    n_pool = (5 * DEC_BATCH * n_pages) // 4
    f32 = jnp.float32
    nrm = lambda k, shape, s=1.0: (s * jax.random.normal(k, shape)).astype(f32)
    gain = lambda k, shape: (1.0 + 0.05 * jax.random.normal(k, shape)).astype(f32)
    x_prompt = nrm(ks[0], (BATCH, SEQ, D_MODEL))
    x_sample = nrm(ks[1], (DEC_BATCH, DEC_SEQ, D_MODEL))
    cache_k_a = nrm(ks[2], (DEPTH, n_pool, PAGE_SIZE, N_HEADS_A, HEAD_DIM))
    cache_v_a = nrm(ks[3], (DEPTH, n_pool, PAGE_SIZE, N_HEADS_A, HEAD_DIM))
    cache_k_idx = nrm(ks[4], (DEPTH, n_pool, PAGE_SIZE, IDX_DIM))
    cache_k_b = nrm(ks[5], (DEPTH, n_pool, PAGE_SIZE, N_HEADS_B, HEAD_DIM))
    cache_v_b = nrm(ks[6], (DEPTH, n_pool, PAGE_SIZE, N_HEADS_B, HEAD_DIM))
    cache_logf_b = jax.nn.log_sigmoid(FORGET_BIAS + jax.random.normal(ks[7], (DEPTH, n_pool, PAGE_SIZE, N_HEADS_B))).astype(f32)
    page_table = jax.random.permutation(ks[8], n_pool)[:DEC_BATCH * n_pages].reshape(DEC_BATCH, n_pages).astype(jnp.int32)
    c_prompt = nrm(ks[9], (BATCH, D_MODEL))
    c_sample = nrm(ks[10], (DEC_BATCH, D_MODEL))
    w_ada = nrm(ks[11], (DEPTH, D_MODEL, 6 * D_MODEL), 0.5 * D_MODEL ** -0.5)
    b_ada = nrm(ks[12], (DEPTH, 6 * D_MODEL), 0.02)
    g_norm1 = gain(ks[13], (DEPTH, D_MODEL))
    w_in = nrm(ks[14], (DEPTH, D_MODEL, D_IN), D_MODEL ** -0.5)
    b_forget = (FORGET_BIAS + 0.1 * jax.random.normal(ks[15], (DEPTH, N_HEADS_B))).astype(f32)
    g_qa = gain(ks[16], (DEPTH, HEAD_DIM))
    g_ka = gain(ks[17], (DEPTH, HEAD_DIM))
    g_qb = gain(ks[18], (DEPTH, HEAD_DIM))
    g_kb = gain(ks[19], (DEPTH, HEAD_DIM))
    w_o_a = nrm(ks[20], (DEPTH, WIDTH_A, D_MODEL), WIDTH_A ** -0.5)
    w_o_b = nrm(ks[21], (DEPTH, WIDTH_B, D_MODEL), WIDTH_B ** -0.5)
    w_out = nrm(ks[22], (DEPTH, D_MODEL, D_MODEL), D_MODEL ** -0.5)
    g_norm2 = gain(ks[23], (DEPTH, D_MODEL))
    w_up = nrm(ks[24], (DEPTH, D_MODEL, D_FF), D_MODEL ** -0.5)
    w_down = nrm(ks[25], (DEPTH, D_FF, D_MODEL), D_FF ** -0.5)
    return {'x_prompt': x_prompt, 'x_sample': x_sample,
            'cache_k_a': cache_k_a, 'cache_v_a': cache_v_a, 'cache_k_idx': cache_k_idx,
            'cache_k_b': cache_k_b, 'cache_v_b': cache_v_b, 'cache_logf_b': cache_logf_b,
            'page_table': page_table, 'c_prompt': c_prompt, 'c_sample': c_sample,
            'w_ada': w_ada, 'b_ada': b_ada, 'g_norm1': g_norm1, 'w_in': w_in, 'b_forget': b_forget,
            'g_qa': g_qa, 'g_ka': g_ka, 'g_qb': g_qb, 'g_kb': g_kb,
            'w_o_a': w_o_a, 'w_o_b': w_o_b, 'w_out': w_out,
            'g_norm2': g_norm2, 'w_up': w_up, 'w_down': w_down}

def reference(x_prompt, x_sample, cache_k_a, cache_v_a, cache_k_idx, cache_k_b, cache_v_b, cache_logf_b,
              page_table, c_prompt, c_sample, w_ada, b_ada, g_norm1, w_in, b_forget, g_qa, g_ka, g_qb, g_kb,
              w_o_a, w_o_b, w_out, g_norm2, w_up, w_down):
    y_p, y_s = x_prompt, x_sample
    states_p, states_s = [], []
    for l in range(DEPTH):
        lw = (w_ada[l], b_ada[l], g_norm1[l], w_in[l], b_forget[l], g_qa[l], g_ka[l], g_qb[l], g_kb[l],
              w_o_a[l], w_o_b[l], w_out[l], g_norm2[l], w_up[l], w_down[l])
        y_p, st_p = run_layer(y_p, c_prompt, prompt_mix, *lw)
        mix_s = functools.partial(sample_mix, l, cache_k_a, cache_v_a, cache_k_idx, cache_k_b, cache_v_b,
                                  cache_logf_b, page_table)
        y_s, st_s = run_layer(y_s, c_sample, mix_s, *lw)
        states_p.append(st_p)
        states_s.append(st_s)
    k_a_p, v_a_p, k_idx_p, k_b_p, v_b_p, logf_p = (jnp.stack(s) for s in zip(*states_p))
    k_a_s, v_a_s, k_idx_s, k_b_s, v_b_s, logf_s = (jnp.stack(s) for s in zip(*states_s))
    return (y_p, y_s, k_a_p, v_a_p, k_idx_p, k_b_p, v_b_p, logf_p, k_a_s, v_a_s, k_idx_s, k_b_s, v_b_s, logf_s)


_drawn_inputs = setup_inputs


def setup_inputs(seed=0):
    import zlib

    import numpy as np

    out = dict(_drawn_inputs(seed))
    spreads = {}
    factors = {'cache_logf_b': 3.36, 'g_qa': 8.0, 'g_qb': 27.516, 'g_norm2': 2.673}
    for name, (base, spread) in spreads.items():
        noise = np.random.default_rng([zlib.crc32(name.encode()), seed]).standard_normal(out[name].shape)
        drawn = base * np.exp(spread * noise) if base else spread * noise
        out[name] = __import__('jax').numpy.asarray(drawn.astype(out[name].dtype))
    for name, factor in factors.items():
        out[name] = (out[name] * factor).astype(out[name].dtype)
    return out
```

```python
from contextlib import ExitStack

import numpy as np

import concourse.bass as bass
from concourse import mybir

ALU = mybir.AluOpType
ACT = mybir.ActivationFunctionType
F32 = mybir.dt.float32
F32R = mybir.dt.float32r
I32 = mybir.dt.int32
AX_X = mybir.AxisListType.X

P = 128
DM = 1024
SEQ = 512
NS = 8
T = SEQ + NS
HALF = T // 2
H = 8
HD = 64
NCH = DM // P
QB = SEQ // P
PAGE = 128
NPAGE = 2
PAST = PAGE * NPAGE
L = PAST + 1
TOPK_P = 128
TOPK_S = L // 4
FF = 4 * DM
EPS = 1e-6
MASK = -1e30
TAKEN = -3e38
QK_SCALE = HD ** -0.5
SLOPES = [2.0 ** (-8.0 * (h + 1) / H) for h in range(H)]

QA, KA, VA, QBC, KBC, VBC, QI, KI, WI, FL, GA, GB = np.cumsum(
    [0, 512, 512, 512, 512, 512, 512, 512, 64, 8, 8, 1024]).tolist()

N_PAIRS = 8
T_SMALL, T_QI = 0, 1
T_PAIR = T_QI + 4
T_GATE = T_PAIR + 3 * N_PAIRS
T_WO = T_GATE + 2 * NCH
T_OUT = T_WO + NCH
T_MLP = T_OUT + NCH
RAW = 4
SPL = 2
ADA_BLOCKS = 12
ROW_FL = 96


def pair_mixer(p):
    return p // 4, p % 4


def dma_count(i):
    if i == T_SMALL:
        return 3
    return 2 if T_WO <= i < T_OUT else 1


def landed_value(i):
    return 16 * sum(dma_count(j) for j in range(i % RAW, i + 1, RAW))


def par(i):
    return 0 if i < T_GATE + 4 else i % 2


def act_evac_value(i, half):
    return 2 * i + half + 1


def layer(nc, a):
    ctx = ExitStack()
    with ctx:
        def sem(name):
            return ctx.enter_context(nc.semaphore(name))

        place = {"at": nc.sbuf_base + 32}
        place["at"] -= place["at"] % 32

        def sb(name, shape, dt=F32, at=None):
            size = int(np.prod(shape[1:])) * 4
            size += -size % 32
            if at is None:
                at = place["at"]
                place["at"] += size
            return nc.alloc_sbuf_tensor_at(name, list(shape), dt, offset=at), at, at + size

        def new(name, shape, dt=F32):
            return sb(name, shape, dt)[0]

        ident = new("ident", [P, P])
        ones = new("ones", [P, P])
        dist = new("dist", [P, SEQ])
        cmask = new("cmask", [P, P])
        vec_t = new("vec_t", [P, 64])
        mod_t = new("mod_t", [P, 48, 9])
        amul = new("amul", [P, NCH, 9])
        cond_t = new("cond_t", [P, NCH, 9])
        g_col = new("g_col", [P, 2])
        gq = new("gq", [P, 2])
        gk_row = new("gk_row", [P, 2, HD])
        bforget = new("bforget", [P, 1])
        wi_tok = new("wi_tok", [P, QB, H])
        stat = new("stat", [P, 40])
        m8 = new("m8", [P, 8])
        ms8 = new("ms8", [P, 8])
        rs8 = new("rs8", [P, 8])
        neghalf = new("neghalf", [P, 8])
        sm_tok_s = new("sm_tok_s", [NS, P])
        page_row = new("page_row", [1, NS * NPAGE], I32)

        x_t = new("x_t", [P, NCH, T])
        raw = new("raw", [P, RAW, NCH, P])
        w_hi = new("w_hi", [P, SPL, NCH, P], F32R)
        w_lo = new("w_lo", [P, SPL, NCH, P], F32R)
        h_hi = new("h_hi", [P, NCH, T], F32R)
        h_lo = new("h_lo", [P, NCH, T], F32R)
        o_at = place["at"]
        o_hi = new("o_hi", [P, 8, T], F32R)
        o_lo = new("o_lo", [P, 8, T], F32R)
        z_s = new("z_s", [P, 29, NS])

        base = place["at"]
        rbuf = new("rbuf", [P, 2, SEQ])
        sq = new("sq", [P, SEQ])
        tok = new("tok", [P, 2, SEQ])
        z = new("z", [P, 3, SEQ])
        q_pad = new("q_pad", [P, 2, 2, SEQ])
        k_fm = new("k_fm", [P, 2, SEQ])
        v_tok = new("v_tok", [P, 2, QB, P])
        ki2 = new("ki2", [P, SEQ])
        sel = new("sel", [P, 1152])
        fbc = new("fbc", [P, 2, 2, SEQ])
        fd_at = place["at"]
        fdiag = new("fdiag", [P, 2, SEQ])
        lg = new("lg", [P, 3, SEQ])
        abias = new("abias", [P, SEQ])
        pt_at = place["at"]
        p_t = new("p_t", [P, 2, QB, SEQ])
        assert place["at"] <= nc.sbuf_usable_end
        q_idx = sb("q_idx", [P, H, SEQ], F32, pt_at)[0]

        gate = sb("gate", [P, 2 * NCH, T], F32, base)[0]
        at = base + 2 * NCH * T * 4

        def area(name, shape, dt=F32):
            nonlocal at
            tile_, _, at = sb(name, shape, dt, at)
            return tile_

        ts = area("ts", [NS, 7, SEQ])
        kv_at = at
        kv = area("kv", [P, 2, NPAGE, SEQ])
        prod = area("prod", [P, 2, NPAGE, SEQ])
        qbc = area("qbc", [P, 2, SEQ])
        ki_pg, _, ki_end = sb("ki_pg", [P, NS * NPAGE, 2, HD], F32, kv_at)
        ki_pt = sb("ki_pt", [P, NS * NPAGE, P], F32, ki_end)[0]
        lgs = area("lgs", [P, 2, NPAGE, NS * H])
        pts = area("pts", [P, 2, NPAGE, NS * H])
        lfp = area("lfp", [P, NPAGE, NS * H])
        qzs = area("qzs", [P, NS, 4, 2])
        wbc = area("wbc", [P, NS, H])
        isr = area("isr", [P, NS, NPAGE, H])
        iss = area("iss", [P, NS, NPAGE])
        onehot = area("onehot", [P, NS, NS])
        rows_l = area("rows_l", [64, 2, L])
        rows_f = area("rows_f", [64, L])
        srow = area("srow", [NS, L])
        dist_s = area("dist_s", [NS, L])
        spread = area("spread", [NS, 64])
        gather = area("gather", [64, NS])
        pick = area("pick", [64, H])
        slope_rows = area("slope_rows", [64, H])
        pself = area("pself", [64, 2, H])
        col64 = area("col64", [64, 16])
        s8 = area("s8", [NS, 12, 8])
        gq_row = area("gq_row", [NS, 2, HD])
        samples_end = at
        assert samples_end <= nc.sbuf_usable_end, (samples_end, nc.sbuf_usable_end)
        mix, _, at2 = sb("mix", [P, 2, 3, HALF], F32, samples_end)
        assert at2 <= nc.sbuf_usable_end, (at2, nc.sbuf_usable_end)
        u_hi, _, at2 = sb("u_hi", [P, 16, T], F32R, o_at)
        u_lo, _, at2 = sb("u_lo", [P, 16, T], F32R, at2)
        u_f, _, at2 = sb("u_f", [P, 4, HALF], F32, at2)
        xs8, _, at2 = sb("xs8", [P, 2, NS], F32, at2)
        y_tok, _, at2 = sb("y_tok", [P, QB, DM], F32, at2)
        y_stok, _, at2 = sb("y_stok", [NS, DM], F32, at2)
        assert at2 <= nc.sbuf_usable_end, (at2, nc.sbuf_usable_end)
        x_tok, _, e1 = sb("x_tok", [P, QB, DM], F32, base)
        x_stok, _, e1 = sb("x_stok", [NS, DM], F32, e1)
        cond, _, e1 = sb("cond", [9, DM], F32, e1)
        vec_rows, _, e1 = sb("vec_rows", [64, P], F32, e1)
        sig, _, e1 = sb("sig", [P, NCH * 9], F32, e1)
        nbuf, _, e1 = sb("nbuf", [P, 4, T], F32, e1)
        nrm, _, e1 = sb("nrm", [P, 2, T], F32, e1)
        nsm, _, e1 = sb("nsm", [P, 2, NCH, NS], F32, e1)
        mod_row, _, e1 = sb("mod_row", [9, 2, SEQ], F32, e1)
        ada, _, e1 = sb("ada", [P, 2, NCH, SEQ], F32, o_at)
        assert e1 <= nc.sbuf_usable_end
        del e1
        zsm, _, e2 = sb("zsm", [P, T], F32, base)
        assert e2 <= base + 4096
        lf, _, e2 = sb("lf", [P, 4, T], F32, fd_at)
        assert e2 <= fd_at + 5 * 4 * SEQ

        bank = [ctx.enter_context(nc.psum_tensor(f"bank{i}", [P, SEQ], F32)) for i in range(8)]
        negf_d = nc.dram_tensor("negf_d", (H, SEQ), F32).ap()
        q_d = nc.dram_tensor("q_d", (2, NS, SEQ), F32).ap()
        wi_d = nc.dram_tensor("wi_d", (NS, H), F32).ap()


        small_landed = sem("small_landed")
        x_landed = sem("x_landed")
        ada_landed = [sem("ada_landed0"), sem("ada_landed1")]
        raw_landed = [sem(f"raw_landed{i}") for i in range(RAW)]
        fbc_landed = [sem("fbc_landed0"), sem("fbc_landed1")]
        consts = sem("consts")
        zeroed = sem("zeroed")
        vec_done = sem("vec_done")
        vec_ready = sem("vec_ready")
        cond_ready = sem("cond_ready")
        xt_done = sem("xt_done")
        xt_act = sem("xt_act")
        xt_dve = sem("xt_dve")
        sq_ready = sem("sq_ready")
        sq_used = sem("sq_used")
        ms_ready = sem("ms_ready")
        rs_ready = sem("rs_ready")
        mod_done = sem("mod_done")
        mod_row_ready = sem("mod_row_ready")
        mod_turned = sem("mod_turned")
        mod_ready = sem("mod_ready")
        nf_ready = sem("nf_ready")
        h_hi_ready = sem("h_hi_ready")
        h_lo_ready = sem("h_lo_ready")
        hi_ready = sem("hi_ready")
        lo_ready = sem("lo_ready")
        proj_done = sem("proj_done")
        act_evac = sem("act_evac")
        xs_ready = sem("xs_ready")
        dve_evac = sem("dve_evac")
        tok_done = sem("tok_done")
        tok_sq = sem("tok_sq")
        ms_tok = sem("ms_tok")
        rstd_tok = sem("rstd_tok")
        tok_ready = sem("tok_ready")
        tok_read = sem("tok_read")
        v_ready = sem("v_ready")
        back_done = sem("back_done")
        back_read = sem("back_read")
        s_done = sem("s_done")
        lg_ready = sem("lg_ready")
        e_ready = sem("e_ready")
        p_ready = sem("p_ready")
        pt_done = sem("pt_done")
        pt_ready = sem("pt_ready")
        pv_done = sem("pv_done")
        o_hi_ready = sem("o_hi_ready")
        o_lo_ready = sem("o_lo_ready")
        idx_done = sem("idx_done")
        idx_relu = sem("idx_relu")
        idx_sum = sem("idx_sum")
        sel_ready = sem("sel_ready")
        sm_ready = sem("sm_ready")
        lf_step = sem("lf_step")
        smt_done = sem("smt_done")
        smt_ready = sem("smt_ready")
        negf_ready = sem("negf_ready")
        negf_stored = sem("negf_stored")
        fd_ready = sem("fd_ready")
        pages_landed = sem("pages_landed")
        ts_turned = sem("ts_turned")
        ts_ready = sem("ts_ready")
        ts_sq = sem("ts_sq")
        ts_ms = sem("ts_ms")
        ts_rs = sem("ts_rs")
        ts_norm = sem("ts_norm")
        q_stored = sem("q_stored")
        wbc_landed = sem("wbc_landed")
        gq_landed = sem("gq_landed")
        s_consts = sem("s_consts")
        kip_landed = sem("kip_landed")
        lfp_landed = sem("lfp_landed")
        kip_turned = sem("kip_turned")
        kip_ready = sem("kip_ready")
        qzs_ready = sem("qzs_ready")
        is_done = sem("is_done")
        is_relu = sem("is_relu")
        is_sum = sem("is_sum")
        is_turned = sem("is_turned")
        srow_ready = sem("srow_ready")
        dist_ready = sem("dist_ready")
        dist_spread = sem("dist_spread")
        kv_landed = [sem("kv_landed0"), sem("kv_landed1")]
        prod_pool = sem("prod_pool")
        prod_dve = sem("prod_dve")
        prod_used = sem("prod_used")
        pv_used = sem("pv_used")
        lgs_ready = sem("lgs_ready")
        rows_turned = sem("rows_turned")
        rows_lg = sem("rows_lg")
        rows_e = sem("rows_e")
        rows_p = sem("rows_p")
        pts_turned = sem("pts_turned")
        pts_ready = sem("pts_ready")
        os_ready = sem("os_ready")
        os_turned = sem("os_turned")
        os_hi = sem("os_hi")
        os_lo = sem("os_lo")
        gates_ready = sem("gates_ready")
        mf_ready = sem("mf_ready")
        mf_hi = sem("mf_hi")
        mf_lo = sem("mf_lo")
        u_relu = sem("u_relu")
        u_sq = sem("u_sq")
        u_hi_ready = sem("u_hi_ready")
        u_lo_ready = sem("u_lo_ready")
        y_done = sem("y_done")
        y_act = sem("y_act")
        y_dve = sem("y_dve")
        act_self = sem("act_self")
        dve_self = sem("dve_self")
        pool_self = sem("pool_self")
        k_stored = sem("k_stored")
        v_stored = sem("v_stored")
        stored = sem("stored")

        w_in_v = a["w_in"][0].rearrange("(k p) n -> p k n", p=P)
        ada_v = a["w_ada"][0].rearrange("(k p) n -> p k n", p=P)

        def tile_dmas(i):
            dst = raw[:, i % RAW]
            if i == T_SMALL:
                return [(dst[:, :, 0:HD], w_in_v[:, :, KI:KI + HD]), (dst[:, :, 64:64 + H], w_in_v[:, :, WI:WI + H]),
                        (dst[:, :, ROW_FL:ROW_FL + H], w_in_v[:, :, FL:FL + H])]
            if i < T_PAIR:
                col = QI + (i - T_QI) * P
            elif i < T_GATE:
                p, kd = (i - T_PAIR) // 3, (i - T_PAIR) % 3
                m, c = pair_mixer(p)
                col = [[QBC, KBC, VBC], [QA, KA, VA]][m][kd] + c * P
            elif i < T_WO:
                m, g = (i - T_GATE) // 2, (i - T_GATE) % 2
                col = [GA, GB][g] + m * P
            elif i < T_OUT:
                m = i - T_WO
                return [(dst[:, 0:4], wob_v[:, :, m * P:(m + 1) * P]), (dst[:, 4:8], woa_v[:, :, m * P:(m + 1) * P])]
            else:
                m = i - T_OUT
                return [(dst, wout_v[:, :, m * P:(m + 1) * P])]
            return [(dst, w_in_v[:, :, col:col + P])]

        wob_v = a["w_o_b"][0].rearrange("(k p) n -> p k n", p=P)
        woa_v = a["w_o_a"][0].rearrange("(k p) n -> p k n", p=P)
        wout_v = a["w_out"][0].rearrange("(k p) n -> p k n", p=P)

        N_SMALL = 12
        n_pool = a["cache_k_a"].shape[1]
        wup_v = a["w_up"][0].rearrange("(k p) n -> p k n", p=P)
        wdn_v = a["w_down"][0].rearrange("(k p) n -> p k n", p=P)
        sel_at = [0, 0, 256, 640]

        def width(qb):
            return (qb + 1) * P

        block = ctx.enter_context(nc.Block())

        @block.sync
        def _(sp):
            def small(dst, src):
                sp.dma_start(dst, src).then_inc(small_landed, 16)

            small(cond[0:1, :], a["c_prompt"])
            small(cond[1:9, :], a["c_sample"])
            small(vec_rows[0:48, :], a["b_ada"][0].rearrange("(r c) -> r c", c=P))
            small(vec_rows[48:56, :], a["g_norm1"][0].rearrange("(r c) -> r c", c=P))
            small(vec_rows[56:64, :], a["g_norm2"][0].rearrange("(r c) -> r c", c=P))
            for half in range(2):
                small(g_col[64 * half:64 * half + 64, 0:1], a["g_qb"][0].rearrange("(d o) -> d o", o=1))
                small(g_col[64 * half:64 * half + 64, 1:2], a["g_qa"][0].rearrange("(d o) -> d o", o=1))
            small(gk_row[:, 0, :], a["g_kb"][0].partition_broadcast(P))
            small(gk_row[:, 1, :], a["g_ka"][0].partition_broadcast(P))
            small(bforget[ROW_FL:ROW_FL + H, :], a["b_forget"][0].rearrange("(d o) -> d o", o=1))
            sp.dma_start(page_row[:, :], a["page_table"].rearrange("(o b) n -> o (b n)", o=1)).then_inc(pages_landed, 16)
            sp.dma_start(x_tok[:, :, :], a["x_prompt"][0].rearrange("(t p) n -> p t n", p=P)).then_inc(x_landed, 16)
            sp.dma_start(x_stok[:, :], a["x_sample"][:, 0, :]).then_inc(x_landed, 16)
            for b in range(2):
                sp.dma_start(ada[:, b], ada_v[:, :, b * SEQ:(b + 1) * SEQ]).then_inc(ada_landed[b], 16)
            with sp.Fori(1, ADA_BLOCKS // 2) as it:
                for b in range(2):
                    sp.wait_ge(mod_done, it * 2 + (b - 1))
                    sp.dma_start(ada[:, b], ada_v[:, :, bass.ds((it * 2 + b) * SEQ, SEQ)]).then_inc(ada_landed[b], 16)

            def load(i):
                if i == T_SMALL:
                    sp.wait_ge(zeroed, 1)
                if i >= RAW:
                    sp.wait_ge(lo_ready, i - RAW + 1)
                for dst, src in tile_dmas(i):
                    sp.dma_start(dst, src).then_inc(raw_landed[i % RAW], 16)

            for i in range(RAW):
                load(i)
            for i in range(RAW, T_PAIR + 2 + RAW - 1):
                load(i)
            sp.wait_ge(negf_ready, 1)
            sp.dma_start(negf_d, lf[ROW_FL:ROW_FL + H, 1, 0:SEQ]).then_inc(negf_stored, 16)
            sp.wait_ge(smt_ready, 1)
            smt = abias[:, :].rearrange("p (t c) -> p t c", t=QB)
            sp.dma_start(a["k_idx_p"][0, 0].rearrange("(t p) d -> p t d", p=P), smt[:, :, 0:HD]).then_inc(stored, 16)
            sp.dma_start(a["logf_p"][0, 0].rearrange("(t p) d -> p t d", p=P), smt[:, :, ROW_FL:ROW_FL + H]).then_inc(stored, 16)
            sp.dma_start(a["k_idx_s"][0, :, 0, :], sm_tok_s[:, 0:HD]).then_inc(stored, 16)
            sp.dma_start(a["logf_s"][0, :, 0, :], sm_tok_s[:, ROW_FL:ROW_FL + H]).then_inc(stored, 16)
            sp.wait_ge(negf_stored, 16)
            def sample_stores():
                sp.wait_ge(ts_norm, 4)
                sp.wait_ge(ts_ready, 7)
                for j, name in ((1, "k_b_s"), (2, "v_b_s"), (4, "k_a_s"), (5, "v_a_s")):
                    sp.dma_start(a[name][0, :, 0].rearrange("b h d -> b (h d)"), ts[:, j, :]).then_inc(stored, 16)

            for p in range(N_PAIRS):
                m, c = pair_mixer(p)
                first = T_PAIR + 3 * p
                if m == 0:
                    if p >= 2:
                        sp.wait_ge(lg_ready, 8 * (p - 1))
                    for hh in range(2):
                        sp.dma_start(fbc[:, p % 2, hh, :], negf_d[2 * c + hh].partition_broadcast(P)).then_inc(fbc_landed[p % 2], 16)
                load(first + 1 + RAW)
                load(first + 2 + RAW)
                sp.wait_ge(tok_ready, p + 1)
                dst = a[["k_b_p", "k_a_p"][m]][0, 0].rearrange("(t p) h d -> p t (h d)", p=P)
                sp.dma_start(dst[:, :, c * P:(c + 1) * P], tok[:, 1, :].rearrange("p (t c) -> p t c", t=QB)).then_inc(k_stored, 16)
                load(first + 3 + RAW)
                sp.wait_ge(v_ready, p + 1)
                dst = a[["v_b_p", "v_a_p"][m]][0, 0].rearrange("(t p) h d -> p t (h d)", p=P)
                sp.dma_start(dst[:, :, c * P:(c + 1) * P], v_tok[:, p % 2]).then_inc(v_stored, 16)
            for i in range(T_PAIR + 3 * N_PAIRS + RAW + 1, T_MLP):
                if i == T_GATE + 11:
                    sample_stores()
                load(i)
            for q in range(2):
                with sp.Fori(0, 4) as it:
                    for b in range(4):
                        i = T_MLP + 32 * q + b
                        sp.wait_ge(lo_ready, it * 4 + (i - RAW + 1))
                        sp.dma_start(raw[:, i % RAW], wup_v[:, :, bass.ds((it * 4 + (16 * q + b)) * P, P)])\
                            .then_inc(raw_landed[i % RAW], 16)
                with sp.Fori(0, 4) as it:
                    for b in range(4):
                        i = T_MLP + 32 * q + 16 + b
                        k0 = 16 * q + 8 * (b % 2)
                        sp.wait_ge(lo_ready, it * 4 + (i - RAW + 1))
                        sp.dma_start(raw[:, i % RAW], wdn_v[:, k0:k0 + NCH, bass.ds((it * 2 + b // 2) * P, P)])\
                            .then_inc(raw_landed[i % RAW], 16)
            y_v = a["y_p"][0].rearrange("(t p) n -> p t n", p=P)
            for g in range(4):
                sp.wait_ge(y_act, g + 1)
                sp.wait_ge(y_dve, g + 1)
                sp.dma_start(y_v[:, :, 256 * g:256 * g + 256], y_tok[:, :, 256 * g:256 * g + 256]).then_inc(stored, 16)
            sp.wait_ge(y_act, 5)
            sp.dma_start(a["y_s"][:, 0, :], y_stok[:, :]).then_inc(stored, 16)
            sp.wait_ge(stored, 16 * (4 + 4 + 5))
            sp.wait_ge(k_stored, 16 * N_PAIRS)
            sp.wait_ge(v_stored, 16 * N_PAIRS)

        @block.gpsimd
        def _(pool):
            steps = [0]

            def link(ins):
                steps[0] += 1
                ins.then_inc(pool_self, 1)
                pool.wait_ge(pool_self, steps[0])

            link(pool.memset(ident[:, :], 0.0))
            pool.affine_select(out=ident[:, :], in_=ident[:, :], compare_op=ALU.not_equal, fill=1.0, base=0,
                               pattern=[[-1, P]], channel_multiplier=1).then_inc(consts, 1)
            pool.memset(ones[:, :], 1.0)
            pool.memset(neghalf[:, :], -0.5)
            link(pool.iota(dist[:, :], pattern=[[1, SEQ]], base=-(SEQ - P), channel_multiplier=-1,
                           allow_small_or_imprecise_dtypes=True))
            pool.affine_select(out=dist[:, :], in_=dist[:, :], compare_op=ALU.is_ge, fill=MASK, base=SEQ - P,
                               pattern=[[-1, SEQ]], channel_multiplier=1)
            link(pool.memset(cmask[:, :], 0.0))
            pool.affine_select(out=cmask[:, :], in_=cmask[:, :], compare_op=ALU.is_ge, fill=MASK, base=0,
                               pattern=[[-1, P]], channel_multiplier=1).then_inc(consts, 1)
            pool.memset(raw[:, T_SMALL % RAW], 0.0).then_inc(zeroed, 1)
            pool.memset(q_idx[:, :, :], 0.0).then_inc(zeroed, 1)
            pool.wait_ge(h_lo_ready, NCH + 1)
            pool.memset(q_pad[:, :, :, :], 0.0).then_inc(zeroed, 1)

            def power(n):
                pool.wait_ge(ms_tok, n + 1)
                if n >= 1:
                    pool.wait_ge(tok_read, n)
                pool.tensor_tensor(rs8[:, :], ms8[:, :], neghalf[:, :], ALU.pow).then_inc(rstd_tok, 1)

            for p in range(N_PAIRS):
                if p == 0:
                    power(0)
                    for qb in range(1, QB):
                        if qb == 2:
                            power(1)
                        pool.wait_ge(idx_sum, H * qb)
                        o = sel_at[qb] + qb * P
                        pool.affine_select(out=sel[:, o:o + P], in_=sel[:, o:o + P], compare_op=ALU.is_ge, fill=MASK,
                                           base=0, pattern=[[-1, P]], channel_multiplier=1).then_inc(sel_ready, 1)
                else:
                    power(2 * p)
                    power(2 * p + 1)
            pool.wait_ge(o_lo_ready, N_PAIRS)
            pool.wait_ge(pages_landed, 16)
            pages = [pool.value_load(page_row[0:1, i:i + 1], min_val=0, max_val=n_pool - 1) for i in range(NS * NPAGE)]
            for i in range(NS * NPAGE):
                for dup in range(2):
                    pool.dma_start(ki_pg[:, i, dup, :], a["cache_k_idx"][0, bass.ds(pages[i], 1)].rearrange("o p d -> p (o d)"))\
                        .then_inc(kip_landed, 16)
            for b in range(2):
                for m in range(1):
                    pool.dma_start(gq_row[:, b, :], a[["g_qb", "g_qa"][b]][0].partition_broadcast(NS)).then_inc(gq_landed, 16)
            link(pool.memset(qzs[:, :, :, :], 0.0))
            link(pool.memset(onehot[:, :, :], 0.0))
            link(pool.affine_select(out=onehot[:, :, :], in_=onehot[:, :, :], compare_op=ALU.not_equal, fill=1.0, base=0,
                                    pattern=[[1, NS], [-1, NS]], channel_multiplier=0))
            link(pool.memset(spread[:, :], 0.0))
            link(pool.affine_select(out=spread[:, :].rearrange("p (b h) -> p b h", h=H),
                                    in_=spread[:, :].rearrange("p (b h) -> p b h", h=H), compare_op=ALU.not_equal, fill=1.0,
                                    base=0, pattern=[[-1, NS], [0, H]], channel_multiplier=1))
            link(pool.memset(gather[:, :], 1.0))
            link(pool.affine_select(out=gather[:, :], in_=gather[:, :], compare_op=ALU.is_ge, fill=0.0, base=0,
                                    pattern=[[-H, NS]], channel_multiplier=1))
            link(pool.affine_select(out=gather[:, :], in_=gather[:, :], compare_op=ALU.is_ge, fill=0.0, base=H - 1,
                                    pattern=[[H, NS]], channel_multiplier=-1))
            link(pool.memset(pick[:, :], 0.0))
            for b in range(NS):
                link(pool.affine_select(out=pick[:, :], in_=pick[:, :], compare_op=ALU.not_equal, fill=1.0, base=-H * b,
                                        pattern=[[-1, H]], channel_multiplier=1))
            for h in range(H):
                pool.memset(slope_rows[:, h:h + 1], SLOPES[h])
            link(pool.iota(dist_s[:, :], pattern=[[1, L]], base=-PAST, channel_multiplier=0, allow_small_or_imprecise_dtypes=True))
            pool.memset(s8[:, 11, :], 0.0).then_inc(s_consts, 1)
            for i in range(NS * NPAGE):
                pool.dma_start(lfp[:, i % 2, H * (i // 2):H * (i // 2) + H],
                               a["cache_logf_b"][0, bass.ds(pages[i], 1)].rearrange("o p d -> p (o d)")).then_inc(lfp_landed, 16)
            for n, j in enumerate((0, 1, 3, 4)):
                pool.wait_ge(ts_ms, n + 1)
                pool.tensor_tensor(s8[:, 4 + n, :], s8[:, n, :], neghalf[0:NS, :], ALU.pow).then_inc(ts_rs, 1)
            pool.wait_ge(ts_norm, 5)
            pool.dma_start(wi_d, s8[:, 8, :]).then_inc(q_stored, 16)
            pool.dma_start(q_d[0], ts[:, 0, :]).then_inc(q_stored, 16)
            pool.dma_start(q_d[1], ts[:, 3, :]).then_inc(q_stored, 16)
            pool.wait_ge(q_stored, 48)
            pool.dma_start(wbc[:, :, :], wi_d.rearrange("b h -> (b h)").partition_broadcast(P).rearrange("p (b h) -> p b h", h=H))\
                .then_inc(wbc_landed, 16)

            def load_kv(n):
                vals, m, b = n // 16, n // 8 % 2, n % 8
                if n == 0:
                    pool.wait_ge(is_done, 1)
                    pool.wait_ge(prod_used, 1)
                elif n >= 2:
                    pool.wait_ge([prod_dve, prod_pool][n % 2], n // 2)
                cache = a[[["cache_k_b", "cache_k_a"], ["cache_v_b", "cache_v_a"]][vals][m]]
                for pg in range(NPAGE):
                    pool.dma_start(kv[:, n % 2, pg, :],
                                   cache[0, bass.ds(pages[b * NPAGE + pg], 1)].rearrange("o p h d -> p (o h d)"))\
                        .then_inc(kv_landed[n % 2], 16)
                if vals == 0:
                    pool.dma_start(qbc[:, n % 2, :], q_d[m, b].partition_broadcast(P)).then_inc(kv_landed[n % 2], 16)

            def kv_value(n):
                return 16 * sum(3 if j < 16 else 2 for j in range(n % 2, n + 1, 2))

            load_kv(0)
            load_kv(1)
            for n in range(32):
                if n == 16:
                    pool.wait_ge(pts_ready, 2)
                if n % 2:
                    pool.wait_ge(kv_landed[1], kv_value(n))
                    if n >= 2:
                        if n < 18:
                            pool.wait_ge(prod_used, n)
                        else:
                            pool.wait_ge(pv_used, n - 17)
                    if n < 16:
                        pool.tensor_tensor(prod[:, 1], kv[:, 1], qbc[:, 1, :].unsqueeze(1).to_broadcast([P, NPAGE, SEQ]), ALU.mult)\
                            .then_inc(prod_pool, 1)
                    else:
                        m, b = n // 8 % 2, n % 8
                        for pg in range(NPAGE):
                            last = pool.tensor_tensor(prod[:, 1, pg, :].rearrange("p (h d) -> p h d", d=HD),
                                                      kv[:, 1, pg, :].rearrange("p (h d) -> p h d", d=HD),
                                                      pts[:, m, pg, H * b:H * b + H].unsqueeze(2).to_broadcast([P, H, HD]), ALU.mult)
                        last.then_inc(prod_pool, 1)
                if n + 2 < 32:
                    load_kv(n + 2)

        @block.tensor
        def _(pe):
            mm, tr = nc.tensor.matmul, nc.tensor.transpose
            pe.wait_ge(consts, 1)
            pe.wait_ge(small_landed, 16 * N_SMALL)
            tr(bank[7][:, 0:64], vec_rows[:, :], ident[0:64, 0:64])
            for j in range(NCH):
                last = tr(bank[7][:, 64 + 9 * j:73 + 9 * j], cond[:, j * P:(j + 1) * P], ident[0:9, 0:9])
            last.then_inc(vec_done, 1)
            pe.wait_ge(x_landed, 32)
            for j in range(NCH):
                if j >= 4:
                    pe.wait_ge([xt_act, xt_dve][j % 2], (j - 4) // 2 + 1)
                tr(bank[6][:, 8 * j:8 * j + 8], x_stok[:, j * P:(j + 1) * P], ident[0:NS, 0:NS])
                for t in range(QB):
                    last = tr(bank[j % 4][:, t * P:(t + 1) * P], x_tok[:, t, j * P:(j + 1) * P], ident[:, :])
                last.then_inc(xt_done, 1)

            def norm_sums(n):
                pe.wait_ge(consts, 2)
                for j in range(NCH):
                    pe.wait_ge(sq_ready, NCH * n + j + 1)
                    mm(bank[4][:, 0:HALF], ones[:, :], nrm[:, j % 2, 0:HALF], start=j == 0, stop=j == NCH - 1)
                    mm(bank[5][:, 0:HALF], ones[:, :], nrm[:, j % 2, HALF:T], start=j == 0, stop=j == NCH - 1)\
                        .then_inc(sq_used, 1)

            norm_sums(0)

            def ada_products(b, value, rows=None, room=None):
                pe.wait_ge(ada_landed[b], value)
                for k in range(NCH):
                    if k == NCH - 1 and rows is not None:
                        pe.wait_ge(mod_row_ready, rows)
                        pe.wait_ge(mod_ready, room)
                    last = mm(bank[b][0:9, :], cond_t[:, k, :], ada[:, b, k, :], start=k == 0, stop=k == NCH - 1)
                last.then_inc(mod_done, 1)

            def ada_turn(b):
                for q in range(4):
                    last = tr(bank[2 + b][:, 9 * q:9 * q + 9], mod_row[:, b, q * P:(q + 1) * P], ident[0:9, 0:9])
                last.then_inc(mod_turned, 1)

            pe.wait_ge(cond_ready, 1)
            pe.wait_ge(xt_act, 4)
            pe.wait_ge(xt_dve, 5)
            ada_products(0, 16)
            ada_products(1, 16)
            pe.wait_ge(mod_row_ready, 1)
            ada_turn(0)
            with pe.Fori(1, ADA_BLOCKS // 2) as it:
                for b in range(2):
                    pe.wait_ge(mod_row_ready, it * 2 + (b - 1))
                    ada_products(b, it * 16 + 16, it * 2 + b, it * 2 - 1 + b)
                    ada_turn(1 - b)
            pe.wait_ge(mod_row_ready, ADA_BLOCKS)
            pe.wait_ge(mod_ready, ADA_BLOCKS - 2)
            ada_turn(1)

            def half_tile(i, half, out, ks=range(NCH), src=(h_hi, h_lo), k0=0, first=True, last=True):
                n0 = half * HALF
                for k in ks:
                    x_h, x_l = src[0][:, k0 + k, n0:n0 + HALF], src[1][:, k0 + k, n0:n0 + HALF]
                    mm(out, w_hi[:, i % SPL, k, :], x_h, start=first and k == ks[0], stop=False)
                    mm(out, w_hi[:, i % SPL, k, :], x_l, start=False, stop=False)
                    end = mm(out, w_lo[:, i % SPL, k, :], x_h, start=False, stop=last and k == ks[-1])
                return end

            def project(i, half):
                if half == 0:
                    pe.wait_ge(hi_ready, i + 1)
                    pe.wait_ge(lo_ready, i + 1)
                b = half + 4 * par(i)
                if i >= 1:
                    before = i - 1 if par(i - 1) == par(i) else i - 2
                    pe.wait_ge(act_evac, act_evac_value(before, half))
                half_tile(i, half, bank[b][:, 0:HALF]).then_inc(proj_done, 1)

            def scores(U):
                p, hh, qb = U // 8, U // 4 % 2, U % 4
                if U >= 2:
                    pe.wait_ge(lg_ready, U - 1)
                if U % 8 == 0:
                    pe.wait_ge(back_read, 2 * p + 2)
                mm(bank[4 + U % 2][:, 0:width(qb)], q_pad[:, p % 2, hh, qb * P:(qb + 1) * P],
                   k_fm[:, p % 2, 0:width(qb)], start=True, stop=True).then_inc(s_done, 1)

            def turn_probs(U):
                qb = U % 4
                pe.wait_ge(p_ready, U + 1)
                if U >= 1:
                    pe.wait_ge(pt_ready, U)
                for kb in range(qb + 1):
                    last = tr(bank[6][:, kb * P:(kb + 1) * P], lg[:, U % 3, kb * P:(kb + 1) * P], ident[:, :])
                last.then_inc(pt_done, 1)

            def values(p, hh):
                pe.wait_ge(pt_ready, 8 * p + 4 * hh + 4)
                pe.wait_ge(v_ready, p + 1)
                if p >= 1:
                    pe.wait_ge(o_lo_ready, p)
                for kb in range(QB):
                    last = mm(bank[7][64 * hh:64 * hh + 64, kb * P:SEQ], v_tok[:, p % 2, kb, 64 * hh:64 * hh + 64],
                              p_t[:, hh, kb, kb * P:SEQ], start=kb == 0, stop=kb == QB - 1)
                last.then_inc(pv_done, 1)

            def to_tokens(p, kd):
                pe.wait_ge(act_evac, act_evac_value(T_PAIR + 3 * p + kd, 1))
                if kd == 0:
                    if p == 0:
                        pe.wait_ge(smt_ready, 1)
                    else:
                        pe.wait_ge(v_ready, p)
                else:
                    pe.wait_ge(tok_read, 2 * p + kd)
                for t in range(QB):
                    last = tr(bank[2][:, t * P:(t + 1) * P], z[:, kd, t * P:(t + 1) * P], ident[:, :])
                last.then_inc(tok_done, 1)

            def to_features(p, kd):
                pe.wait_ge(tok_read if kd == 0 else tok_ready, 2 * p + 1 if kd == 0 else p + 1)
                if p == 0 and kd == 0:
                    pe.wait_ge(smt_ready, 1)
                if 2 * p + kd >= 1:
                    pe.wait_ge(back_read, 2 * p + kd)
                for t in range(QB):
                    last = tr(bank[3][:, t * P:(t + 1) * P], tok[:, kd, t * P:(t + 1) * P], ident[:, :])
                last.then_inc(back_done, 1)

            def index_scores(n):
                qb, h = 1 + n // H, n % H
                if n >= 2:
                    pe.wait_ge(idx_relu, n - 1)
                mm(bank[4 + n % 2][:, 0:width(qb)], q_idx[:, h, qb * P:(qb + 1) * P], ki2[:, 0:width(qb)],
                   start=True, stop=True).then_inc(idx_done, 1)

            pe.wait_ge(h_hi_ready, NCH + 1)
            pe.wait_ge(h_lo_ready, NCH + 1)
            for i in range(T_PAIR):
                project(i, 0)
                project(i, 1)
                if i == 2:
                    pe.wait_ge(sm_ready, 3)
                    for t in range(QB):
                        tr(bank[2][:, t * P:(t + 1) * P], zsm[:, t * P:(t + 1) * P], ident[:, :])
                    tr(bank[3][0:NS, 0:P], zsm[:, SEQ:T], ident[:, :]).then_inc(smt_done, 1)

            for p in range(N_PAIRS + 1):
                first = T_PAIR + 3 * p
                for s in range(12):
                    if s < 6:
                        project(first + s // 2, s % 2)
                    if p == 0:
                        if s == 0:
                            pe.wait_ge(act_evac, act_evac_value(T_PAIR - 1, 1))
                            pe.wait_ge(sm_ready, 3)
                        index_scores(2 * s)
                        index_scores(2 * s + 1)
                    else:
                        if 2 <= s < 10:
                            turn_probs(8 * (p - 1) + s - 2)
                        if s < 8:
                            if p == 1 and s < 2:
                                pe.wait_ge(idx_relu, 24)
                            scores(8 * (p - 1) + s)
                        if s == 6:
                            values(p - 1, 0)
                        if s == 10:
                            values(p - 1, 1)
                    if p < N_PAIRS:
                        if s == 2:
                            to_tokens(p, 0)
                        if s == 4:
                            to_tokens(p, 1)
                            to_features(p, 0)
                        if s == 6:
                            to_tokens(p, 2)
                            to_features(p, 1)
            def sample_turn(g):
                bk = bank[[2, 3, 6, 7][g % 4]]
                if g >= 4:
                    pe.wait_ge(ts_ready, g - 3)
                for c in range(4):
                    last = tr(bk[0:NS, c * P:(c + 1) * P], z_s[:, 4 * g + c, :], ident[:, :])
                last.then_inc(ts_turned, 1)

            def turn_idx_pages():
                pe.wait_ge(kip_landed, 16 * 2 * NS * NPAGE)
                pe.wait_ge(ts_ready, 7)
                for g in range(4):
                    for q in range(4):
                        last = tr(bank[[2, 3, 6, 7][g]][:, q * P:(q + 1) * P],
                                  ki_pg[:, 4 * g + q].rearrange("p a d -> p (a d)"), ident[:, :])
                    last.then_inc(kip_turned, 1)

            def idx_products():
                pe.wait_ge(kip_ready, 4)
                pe.wait_ge(qzs_ready, 1)
                for i in range(NS * NPAGE):
                    last = mm(bank[2][:, H * i:H * i + H], ki_pt[:, i, :], qzs[:, i // 2].rearrange("p c h -> p (c h)"),
                              start=True, stop=True)
                last.then_inc(is_done, 1)

            def turn_idx_scores():
                pe.wait_ge(is_sum, 1)
                for pg in range(NPAGE):
                    last = tr(bank[3][0:NS, pg * P:(pg + 1) * P], iss[:, :, pg], ident[:, :])
                last.then_inc(is_turned, 1)

            def spread_dist():
                pe.wait_ge(dist_ready, 1)
                mm(bank[6][0:64, 0:L], spread[:, :], srow[:, :], start=True, stop=True).then_inc(dist_spread, 1)

            def turn_rows():
                pe.wait_ge(lgs_ready, 1)
                pe.wait_ge(srow_ready, 1)
                pe.wait_ge(lfp_landed, 16 * NS * NPAGE)
                for m in range(2):
                    for pg in range(NPAGE):
                        tr(bank[2 + m][0:64, pg * P:(pg + 1) * P], lgs[:, m, pg, :], ident[:, :])
                for pg in range(NPAGE):
                    tr(bank[7][0:64, P + pg * P:2 * P + pg * P], lfp[:, pg, :], ident[:, :])
                mm(bank[7][0:64, 0:16], spread[:, :], s8[:, 9:11, :].rearrange("p a h -> p (a h)"), start=True, stop=True)
                mm(bank[7][0:64, 16:24], spread[:, :], sm_tok_s[:, ROW_FL:ROW_FL + H], start=True, stop=True).then_inc(rows_turned, 1)

            def turn_pts():
                for m in range(2):
                    pe.wait_ge(rows_p, m + 1)
                    for pg in range(NPAGE):
                        tr(bank[6][:, (2 * m + pg) * 64:(2 * m + pg + 1) * 64], rows_l[:, m, pg * P:(pg + 1) * P], ident[0:64, 0:64])
                pe.wait_ge(rows_p, 3)
                mm(bank[7][0:NS, 0:16], gather[:, :], pself[:, :, :].rearrange("p a h -> p (a h)"), start=True, stop=True)\
                    .then_inc(pts_turned, 1)

            def sample_values(n):
                m, b = n // 8 % 2, n % 8
                pe.wait_ge(*((prod_pool, n // 2 + 1) if n % 2 else (prod_dve, n // 2 + 1)))
                for pg in range(NPAGE):
                    last = mm(bank[2 + m][0:NS, :], onehot[:, b, :], prod[:, n % 2, pg, :],
                              start=b == 0 and pg == 0, stop=b == NS - 1 and pg == NPAGE - 1)
                last.then_inc(pv_used, 1)

            def turn_os(m):
                pe.wait_ge(os_ready, m + 1)
                for c in range(4):
                    last = tr(bank[6 + m][:, c * NS:(c + 1) * NS], ts[:, 2 + 3 * m, c * P:(c + 1) * P], ident[0:NS, 0:NS])
                last.then_inc(os_turned, 1)

            SAMPLE_STEPS = {
                T_GATE + 3: lambda: [sample_turn(g) for g in range(4)],
                T_GATE + 4: lambda: [sample_turn(g) for g in range(4, 7)],
                T_GATE + 5: turn_idx_pages,
                T_GATE + 6: idx_products,
                T_GATE + 7: turn_idx_scores,
                T_GATE + 10: spread_dist,
                T_GATE + 13: turn_rows,
                T_GATE + 15: turn_pts,
            }
            pe.wait_ge(o_hi_ready, N_PAIRS)
            pe.wait_ge(o_lo_ready, N_PAIRS)
            for i in range(T_GATE + 3, T_WO):
                if i in SAMPLE_STEPS:
                    SAMPLE_STEPS[i]()
                project(i, 0)
                project(i, 1)
            for n in range(16, 32):
                if n == 16:
                    pe.wait_ge(rows_lg, 2)
                sample_values(n)
            turn_os(0)
            turn_os(1)

            pe.wait_ge(os_hi, 2)
            pe.wait_ge(os_lo, 2)
            pe.wait_ge(act_evac, act_evac_value(T_WO - 1, 1))
            for i in range(T_WO, T_OUT):
                pe.wait_ge(hi_ready, i + 1)
                pe.wait_ge(lo_ready, i + 1)
                for half in range(2):
                    if i >= T_WO + 2:
                        pe.wait_ge(dve_evac, 2 * (i - 2 - T_WO) + half + 1)
                    b = half + 4 * par(i)
                    half_tile(i, half, bank[b][:, 0:HALF], range(0, 4), (o_hi, o_lo))
                    half_tile(i, half, bank[b + 2][:, 0:HALF], range(4, 8), (o_hi, o_lo)).then_inc(proj_done, 1)
            pe.wait_ge(mf_hi, 2 * NCH)
            pe.wait_ge(mf_lo, 2 * NCH)
            for i in range(T_OUT, T_MLP):
                pe.wait_ge(hi_ready, i + 1)
                pe.wait_ge(lo_ready, i + 1)
                for half in range(2):
                    pe.wait_ge(dve_evac, 2 * (i - 2 - T_WO) + half + 1)
                    half_tile(i, half, bank[half + 4 * par(i)][:, 0:HALF]).then_inc(proj_done, 1)
            pe.wait_ge(dve_evac, 2 * (T_MLP - T_WO))
            norm_sums(1)
            pe.wait_ge(h_hi_ready, 2 * (NCH + 1))
            pe.wait_ge(h_lo_ready, 2 * (NCH + 1))
            for q in range(2):
                with pe.Fori(0, 4) as it:
                    for b in range(4):
                        i = T_MLP + 32 * q + b
                        pe.wait_ge(hi_ready, it * 4 + (i + 1))
                        pe.wait_ge(lo_ready, it * 4 + (i + 1))
                        for half in range(2):
                            pe.wait_ge(act_evac, it * 8 + (2 * T_WO + 32 * q + 2 * (b - 2) + half + 1))
                            half_tile(i, half, bank[half + 4 * (i % 2)][:, 0:HALF]).then_inc(proj_done, 1)
                pe.wait_ge(u_hi_ready, 32 * (q + 1))
                pe.wait_ge(u_lo_ready, 32 * (q + 1))
                with pe.Fori(0, 4) as it:
                    for b in range(4):
                        i = T_MLP + 32 * q + 16 + b
                        kg, mb = b % 2, b // 2
                        pe.wait_ge(hi_ready, it * 4 + (i + 1))
                        pe.wait_ge(lo_ready, it * 4 + (i + 1))
                        for half in range(2):
                            if kg == 0:
                                pe.wait_ge(dve_evac, it * 4 + (32 + 16 * q + 2 * (mb - 2) + half + 1))
                            half_tile(i, half, bank[2 + half + 4 * mb][:, 0:HALF], src=(u_hi, u_lo), k0=8 * kg,
                                      first=kg == 0, last=kg == 1).then_inc(proj_done, 1)
            pe.wait_ge(dve_evac, 64)
            for j in range(NCH):
                if j >= 4:
                    pe.wait_ge([y_act, y_dve][j % 2], (j - 4) // 2 + 1)
                tr(bank[4 + j // 4][0:NS, (j % 4) * P:(j % 4 + 1) * P], x_t[:, j, SEQ:T], ident[:, :])
                for t in range(QB):
                    last = tr(bank[j % 4][:, t * P:(t + 1) * P], x_t[:, j, t * P:(t + 1) * P], ident[:, :])
                last.then_inc(y_done, 1)

        @block.scalar
        def _(act):
            A = nc.scalar.activation
            steps = [0]

            def link(ins):
                steps[0] += 1
                ins.then_inc(act_self, 1)
                act.wait_ge(act_self, steps[0])

            act.wait_ge(vec_done, 1)
            A(vec_t[:, :], bank[7][:, 0:64], ACT.Copy)
            A(sig[:, :], bank[7][:, 64:136], ACT.Sigmoid).then_inc(vec_ready, 1)
            for j in range(0, NCH, 2):
                act.wait_ge(xt_done, j + 1)
                A(x_t[:, j, 0:SEQ], bank[j % 4][:, :], ACT.Copy).then_inc(xt_act, 1)

            def norm_act(n):
                for j in range(NCH):
                    if j >= 2 or n >= 1:
                        act.wait_ge(sq_used, NCH * n + j - 1)
                    A(nrm[:, j % 2, :], x_t[:, j, :], ACT.Square).then_inc(sq_ready, 1)
                act.wait_ge(ms_ready, n + 1)
                link(A(nbuf[:, 1, :], nbuf[:, 0, :], ACT.Ln))
                A(nbuf[:, 1, :], nbuf[:, 1, :], ACT.Exp, scale=-0.5).then_inc(rs_ready, 1)

            act.wait_ge(xt_act, 4)
            act.wait_ge(xt_dve, 5)
            norm_act(0)

            def mod_rows(b, value):
                act.wait_ge(mod_done, value)
                A(mod_row[:, b, :], bank[b][0:9, :], ACT.Copy).then_inc(mod_row_ready, 1)

            mod_rows(0, 1)
            mod_rows(1, 2)
            with act.Fori(1, ADA_BLOCKS // 2) as it:
                for b in range(2):
                    act.wait_ge(mod_turned, it * 2 + (b - 1))
                    mod_rows(b, it * 2 + (b + 1))

            def round_h(n):
                for j in range(NCH):
                    act.wait_ge(nf_ready, (NCH + 1) * n + j + 1)
                    A(h_hi[:, j, 0:SEQ], nrm[:, j % 2, 0:SEQ], ACT.Copy).then_inc(h_hi_ready, 1)
                act.wait_ge(nf_ready, (NCH + 1) * (n + 1))
                A(h_hi[:, :, SEQ:T], nsm[:, 0], ACT.Copy).then_inc(h_hi_ready, 1)

            round_h(0)

            def round_w(i):
                act.wait_ge(raw_landed[i % RAW], landed_value(i))
                if i >= SPL:
                    act.wait_ge(proj_done, 2 * (i - SPL + 1))
                A(w_hi[:, i % SPL], raw[:, i % RAW], ACT.Copy).then_inc(hi_ready, 1)

            def keep_samples(i, b, chunk):
                A(z_s[:, chunk, :], bank[b][:, HALF - NS:HALF], ACT.Copy)

            def store_z(i, half):
                p, kd = (i - T_PAIR) // 3, (i - T_PAIR) % 3
                m, c = pair_mixer(p)
                act.wait_ge(proj_done, 2 * i + half + 1)
                if half == 0:
                    if p >= 1:
                        act.wait_ge(tok_done, 3 * (p - 1) + kd + 1)
                    A(z[:, kd, 0:HALF], bank[0][:, 0:HALF], ACT.Copy).then_inc(act_evac, 1)
                else:
                    A(z[:, kd, HALF:SEQ], bank[1][:, 0:SEQ - HALF], ACT.Copy)
                    A(z_s[:, 12 * m + 4 * kd + c, :], bank[1][:, SEQ - HALF:HALF], ACT.Copy).then_inc(act_evac, 1)

            def store_gate(i, half):
                j = i - T_GATE
                act.wait_ge(proj_done, 2 * i + half + 1)
                if i < T_GATE + 3:
                    act.wait_ge(k_stored, 16 * N_PAIRS)
                A(gate[:, j, half * HALF:(half + 1) * HALF], bank[half + 4 * par(i)][:, 0:HALF], ACT.Copy).then_inc(act_evac, 1)

            def exps(U):
                w = width(U % 4)
                act.wait_ge(lg_ready, U + 1)
                A(lg[:, U % 3, 0:w], lg[:, U % 3, 0:w], ACT.Exp, bias=stat[:, 8 + U % 8:9 + U % 8],
                  accum_out=stat[:, 16 + U % 8:17 + U % 8]).then_inc(e_ready, 1)

            def store_pt(U):
                p, hh, qb = U // 8, U // 4 % 2, U % 4
                act.wait_ge(pt_done, U + 1)
                if p >= 1:
                    act.wait_ge(pv_done, 2 * (p - 1) + hh + 1)
                A(p_t[:, hh, 0:qb + 1, qb * P:(qb + 1) * P], bank[6][:, 0:width(qb)].rearrange("p (k c) -> p k c", k=qb + 1),
                  ACT.Copy).then_inc(pt_ready, 1)

            def square_tok(p, kd):
                act.wait_ge(tok_done, 3 * p + kd + 1)
                if 2 * p + kd >= 1:
                    act.wait_ge(ms_tok, 2 * p + kd)
                A(sq[:, :], bank[2][:, :], ACT.Square).then_inc(tok_sq, 1)

            def store_back(p, kd):
                m = pair_mixer(p)[0]
                act.wait_ge(back_done, 2 * p + kd + 1)
                if kd == 0:
                    if p == 0:
                        act.wait_ge(zeroed, 3)
                    if p >= 2:
                        act.wait_ge(s_done, 8 * (p - 1))
                    A(q_pad[0:64, p % 2, 0, :], bank[3][0:64, :], ACT.Copy, scale=gq[0:64, m:m + 1])
                    A(q_pad[64:128, p % 2, 1, :], bank[3][64:128, :], ACT.Copy, scale=gq[64:128, m:m + 1]).then_inc(back_read, 1)
                else:
                    A(k_fm[:, p % 2, :], bank[3][:, :], ACT.Copy).then_inc(back_read, 1)

            def store_v(p):
                act.wait_ge(tok_done, 3 * p + 3)
                if p >= 2:
                    act.wait_ge(v_stored, 16 * (p - 1))
                A(v_tok[:, p % 2], bank[2][:, :].rearrange("p (t c) -> p t c", t=QB), ACT.Copy).then_inc(v_ready, 1)

            def round_o(p):
                act.wait_ge(pv_done, 2 * p + 2)
                A(o_hi[:, p, 0:SEQ], bank[7][:, :], ACT.Copy).then_inc(o_hi_ready, 1)

            def relu_scores(n):
                w = width(1 + n // H)
                act.wait_ge(idx_done, n + 1)
                if n >= 2:
                    act.wait_ge(idx_sum, n - 1)
                if n < 2:
                    act.wait_ge(smt_done, 1)
                A(rbuf[:, n % 2, 0:w], bank[4 + n % 2][:, 0:w], ACT.Relu).then_inc(idx_relu, 1)

            round_w(0)
            round_w(1)
            for i in range(T_PAIR):
                for half in range(2):
                    act.wait_ge(proj_done, 2 * i + half + 1)
                    lo, hi = half * HALF, min(half * HALF + HALF, SEQ)
                    if i == T_SMALL:
                        A(zsm[:, half * HALF:(half + 1) * HALF], bank[half][:, 0:HALF], ACT.Copy).then_inc(act_evac, 1)
                        continue
                    c = i - T_QI
                    if i == T_QI:
                        act.wait_ge(zeroed, 2)
                    A(q_idx[0:64, 2 * c, lo:hi], bank[half + 4 * par(i)][0:64, 0:hi - lo], ACT.Copy)
                    last = A(q_idx[64:128, 2 * c + 1, lo:hi], bank[half + 4 * par(i)][64:128, 0:hi - lo], ACT.Copy)
                    if half == 1:
                        last = A(z_s[:, 24 + c, :], bank[1 + 4 * par(i)][:, hi - lo:HALF], ACT.Copy)
                    last.then_inc(act_evac, 1)
                round_w(i + 2)
                if i == 1:
                    act.wait_ge(sm_ready, 1)
                    rows = slice(ROW_FL, ROW_FL + H)
                    link(A(lf[rows, 2, :], lf[rows, 1, :], ACT.Exp, scale=-1.0))
                    A(lf[rows, 3, :], lf[rows, 2, :], ACT.Ln, bias=1.0).then_inc(lf_step, 1)
                if i == 3:
                    act.wait_ge(smt_done, 1)
                    A(abias[:, :], bank[2][:, :], ACT.Copy)
                    A(sm_tok_s[:, :], bank[3][0:NS, 0:P], ACT.Copy).then_inc(smt_ready, 1)

            for p in range(N_PAIRS + 1):
                first = T_PAIR + 3 * p
                for s in range(12):
                    if s in (2, 4, 6):
                        round_w(first + 1 + s // 2)
                    if s < 6:
                        if p < N_PAIRS:
                            store_z(first + s // 2, s % 2)
                        else:
                            store_gate(first + s // 2, s % 2)
                    if p == 0:
                        relu_scores(2 * s)
                        relu_scores(2 * s + 1)
                    else:
                        if s < 8:
                            exps(8 * (p - 1) + s)
                        if 2 <= s < 10:
                            store_pt(8 * (p - 1) + s - 2)
                        if s == 10:
                            round_o(p - 1)
                    if p < N_PAIRS:
                        if s == 2:
                            square_tok(p, 0)
                        if s == 4:
                            square_tok(p, 1)
                            store_back(p, 0)
                        if s == 6:
                            store_back(p, 1)
                            store_v(p)
            def sample_store(g):
                act.wait_ge(ts_turned, g + 1)
                A(ts[:, g, :], bank[[2, 3, 6, 7][g % 4]][0:NS, :], ACT.Copy).then_inc(ts_ready, 1)

            def sample_squares():
                act.wait_ge(kip_turned, 4)
                for n, j in enumerate((0, 1, 3, 4)):
                    if n >= 2:
                        act.wait_ge(ts_ms, n - 1)
                    A(qbc[0:NS, n % 2, :], ts[:, j, :], ACT.Square).then_inc(ts_sq, 1)

            def idx_pages():
                for g in range(4):
                    act.wait_ge(kip_turned, g + 1)
                    A(ki_pt[:, 4 * g:4 * g + 4, :], bank[[2, 3, 6, 7][g]][:, :].rearrange("p (a c) -> p a c", a=4), ACT.Copy)\
                        .then_inc(kip_ready, 1)

            def idx_relu_s():
                act.wait_ge(is_done, 1)
                A(isr[:, :, :, :].rearrange("p b g h -> p (b g h)"), bank[2][:, 0:P], ACT.Relu).then_inc(is_relu, 1)

            def idx_rows():
                act.wait_ge(is_turned, 1)
                A(srow[:, 0:PAST], bank[3][0:NS, 0:PAST], ACT.Copy).then_inc(srow_ready, 1)

            def row_exps():
                for m in range(2):
                    act.wait_ge(rows_lg, m + 1)
                    A(rows_l[:, m, :], rows_l[:, m, :], ACT.Exp, bias=col64[:, 2 + m:3 + m],
                      accum_out=col64[:, 4 + m:5 + m]).then_inc(rows_e, 1)

            def store_pts():
                act.wait_ge(pts_turned, 1)
                A(pts[:, :, :, :].rearrange("p m g r -> p (m g r)"), bank[6][:, 0:256], ACT.Copy).then_inc(pts_ready, 1)
                A(s8[:, 6:8, :].rearrange("p a h -> p (a h)"), bank[7][0:NS, 0:16], ACT.Copy).then_inc(pts_ready, 1)

            SAMPLE_STEPS = {
                T_GATE + 3: lambda: [sample_store(g) for g in range(4)],
                T_GATE + 4: lambda: [sample_store(g) for g in range(4, 7)],
                T_GATE + 5: lambda: [idx_pages(), sample_squares()],
                T_GATE + 6: idx_relu_s,
                T_GATE + 7: idx_rows,
                T_GATE + 13: row_exps,
                T_GATE + 15: store_pts,
            }
            for i in range(T_GATE + 3, T_WO):
                if i in SAMPLE_STEPS:
                    SAMPLE_STEPS[i]()
                for half in range(2):
                    store_gate(i, half)
                round_w(i + 2)
            for j in range(2 * NCH):
                if j == 0:
                    act.wait_ge(act_evac, act_evac_value(T_WO - 1, 1))
                A(gate[:, j, :], gate[:, j, :], ACT.Sigmoid).then_inc(gates_ready, 1)
            for m in range(2):
                act.wait_ge(os_turned, m + 1)
                A(o_hi[:, 4 * m:4 * m + 4, SEQ:T], bank[6 + m][:, 0:4 * NS].rearrange("p (c b) -> p c b", b=NS), ACT.Copy)\
                    .then_inc(os_hi, 1)

            for i in range(T_WO, T_OUT):
                m = i - T_WO
                round_w(i + 2)
                for half in range(2):
                    act.wait_ge(mf_ready, 2 * m + half + 1)
                    if m == 0 and half == 0:
                        act.wait_ge(proj_done, 2 * T_WO)
                    A(h_hi[:, m, half * HALF:(half + 1) * HALF], mix[:, half, 2, :], ACT.Copy).then_inc(mf_hi, 1)
            for i in range(T_OUT, T_MLP):
                round_w(i + 2)
            act.wait_ge(dve_evac, 2 * (T_MLP - T_WO))
            norm_act(1)
            round_h(1)

            def round_loop(i, it):
                act.wait_ge(raw_landed[i % RAW], it * 16 + landed_value(i))
                act.wait_ge(proj_done, it * 8 + 2 * (i - SPL + 1))
                A(w_hi[:, i % SPL], raw[:, i % RAW], ACT.Copy).then_inc(hi_ready, 1)

            def up_tile(q, b, it):
                n = 32 * q + 2 * b
                for half in range(2):
                    act.wait_ge(proj_done, it * 8 + (2 * (T_MLP + 32 * q + b) + half + 1))
                    if q or b >= 2:
                        act.wait_ge(u_lo_ready, it * 8 + (n + half - 3))
                    A(u_f[:, 2 * (b % 2) + half, :], bank[half + 4 * ((T_MLP + b) % 2)][:, 0:HALF], ACT.Relu).then_inc(act_evac, 1)
                round_loop(T_MLP + 32 * q + b + 2, it)
                for half in range(2):
                    act.wait_ge(u_sq, it * 8 + (n + half + 1))
                    A(u_hi[:, bass.ds(it * 4 + b, 1), half * HALF:(half + 1) * HALF], u_f[:, 2 * (b % 2) + half:2 * (b % 2) + half + 1, :],
                      ACT.Copy).then_inc(u_hi_ready, 1)

            for q in range(2):
                if q == 0:
                    for b in range(4):
                        up_tile(q, b, 0)
                    with act.Fori(1, 4) as it:
                        for b in range(4):
                            act.wait_ge(u_lo_ready, it * 8 + (2 * b - 2))
                            up_tile(q, b, it)
                else:
                    with act.Fori(0, 4) as it:
                        for b in range(4):
                            up_tile(q, b, it)
                last = 3 if q else 4
                with act.Fori(0, last) as it:
                    for b in range(4):
                        round_loop(T_MLP + 32 * q + 16 + b + 2, it)
                if q:
                    for b in range(2):
                        round_loop(T_MLP + 32 * q + 16 + b + 2, 3)
            for j in range(0, NCH, 2):
                act.wait_ge(y_done, j + 1)
                A(y_tok[:, :, j * P:(j + 1) * P], bank[j % 4][:, :].rearrange("p (t c) -> p t c", t=QB), ACT.Copy).then_inc(y_act, 1)
            act.wait_ge(y_done, NCH)
            A(y_stok[:, 0:SEQ], bank[4][0:NS, :], ACT.Copy)
            A(y_stok[:, SEQ:DM], bank[5][0:NS, :], ACT.Copy).then_inc(y_act, 1)

        @block.vector
        def _(dve):
            steps = [0]

            def link(ins):
                steps[0] += 1
                ins.then_inc(dve_self, 1)
                dve.wait_ge(dve_self, steps[0])

            dve.wait_ge(small_landed, 16 * N_SMALL)
            dve.tensor_scalar(gq[:, :], g_col[:, :], QK_SCALE, None, ALU.mult)
            dve.wait_ge(vec_ready, 1)
            dve.tensor_tensor(cond_t[:, :, :].rearrange("p k c -> p (k c)"), bank[7][:, 64:136], sig[:, :], ALU.mult).then_inc(cond_ready, 1)
            for j in range(1, NCH, 2):
                dve.wait_ge(xt_done, j + 1)
                dve.tensor_copy(x_t[:, j, 0:SEQ], bank[j % 4][:, :]).then_inc(xt_dve, 1)
            dve.tensor_copy(x_t[:, :, SEQ:T], bank[6][:, 0:64].rearrange("p (j c) -> p j c", c=NS)).then_inc(xt_dve, 1)

            def norm_root(n):
                dve.wait_ge(sq_used, NCH * (n + 1))
                dve.tensor_scalar(nbuf[:, 0, 0:HALF], bank[4][:, 0:HALF], 1.0 / DM, EPS, ALU.mult, ALU.add)
                dve.tensor_scalar(nbuf[:, 0, HALF:T], bank[5][:, 0:HALF], 1.0 / DM, EPS, ALU.mult, ALU.add).then_inc(ms_ready, 1)
                dve.wait_ge(rs_ready, n + 1)
                link(dve.tensor_tensor(nbuf[:, 2, :], nbuf[:, 0, :], nbuf[:, 1, :], ALU.mult))
                link(dve.tensor_tensor(nbuf[:, 2, :], nbuf[:, 2, :], nbuf[:, 1, :], ALU.mult))
                link(dve.tensor_scalar(nbuf[:, 2, :], nbuf[:, 2, :], -0.5, 1.5, ALU.mult, ALU.add))
                link(dve.tensor_tensor(nbuf[:, 1, :], nbuf[:, 1, :], nbuf[:, 2, :], ALU.mult))

            norm_root(0)

            def mod_add(b, block_at, value):
                dve.wait_ge(mod_turned, value)
                dve.tensor_tensor(mod_t[:, block_at, :], bank[2 + b][:, 0:36].rearrange("p (q c) -> p q c", c=9),
                                  vec_t[:, block_at].unsqueeze(2).to_broadcast([P, 4, 9]), ALU.add).then_inc(mod_ready, 1)

            mod_add(0, slice(0, 4), 1)
            mod_add(1, slice(4, 8), 2)
            with dve.Fori(1, ADA_BLOCKS // 2) as it:
                for b in range(2):
                    mod_add(b, bass.ds(it * 8 + 4 * b, 4), it * 2 + (b + 1))

            def norm_apply(n):
                shift, scale = 24 * n, 24 * n + 8
                dve.wait_ge(mod_ready, ADA_BLOCKS)
                link(dve.tensor_scalar(amul[:, :, :], mod_t[:, scale:scale + NCH, :], 1.0, None, ALU.add))
                link(dve.tensor_tensor(amul[:, :, :], amul[:, :, :],
                                       vec_t[:, 48 + 8 * n:56 + 8 * n].unsqueeze(2).to_broadcast([P, NCH, 9]), ALU.mult))

                def rest(j):
                    dve.wait_ge(h_hi_ready, (NCH + 1) * n + j + 1)
                    dve.tensor_tensor(h_lo[:, j, 0:SEQ], nrm[:, j % 2, 0:SEQ], h_hi[:, j, 0:SEQ].bitcast(F32),
                                      ALU.subtract).then_inc(h_lo_ready, 1)

                for j in range(NCH):
                    if j >= 2:
                        dve.wait_ge(h_lo_ready, (NCH + 1) * n + j - 1)
                    link(dve.tensor_tensor(nrm[:, j % 2, :], x_t[:, j, :], nbuf[:, 1, :], ALU.mult))
                    dve.tensor_scalar(nrm[:, j % 2, 0:SEQ], nrm[:, j % 2, 0:SEQ], amul[:, j, 0:1],
                                      mod_t[:, shift + j, 0:1], ALU.mult, ALU.add).then_inc(nf_ready, 1)
                    if j >= 1:
                        rest(j - 1)
                rest(NCH - 1)
                link(dve.tensor_tensor(nsm[:, 0], x_t[:, :, SEQ:T], nbuf[:, 1, SEQ:T].unsqueeze(1).to_broadcast([P, NCH, NS]), ALU.mult))
                link(dve.tensor_tensor(nsm[:, 0], nsm[:, 0], amul[:, :, 1:9], ALU.mult))
                dve.tensor_tensor(nsm[:, 0], nsm[:, 0], mod_t[:, shift:shift + NCH, 1:9], ALU.add).then_inc(nf_ready, 1)
                dve.wait_ge(nf_ready, (NCH + 1) * (n + 1))
                dve.wait_ge(h_hi_ready, (NCH + 1) * (n + 1))
                dve.tensor_tensor(h_lo[:, :, SEQ:T], nsm[:, 0], h_hi[:, :, SEQ:T].bitcast(F32), ALU.subtract).then_inc(h_lo_ready, 1)

            norm_apply(0)

            def rest_w(i):
                dve.wait_ge(hi_ready, i + 1)
                dve.tensor_tensor(w_lo[:, i % SPL], raw[:, i % RAW], w_hi[:, i % SPL].bitcast(F32), ALU.subtract).then_inc(lo_ready, 1)

            def index_sum(n):
                qb, h = 1 + n // H, n % H
                w = width(qb)
                dve.wait_ge(idx_relu, n + 1)
                out = sel[:, sel_at[qb]:sel_at[qb] + w]
                if h == 0:
                    ins = dve.tensor_scalar(out, rbuf[:, n % 2, 0:w], wi_tok[:, qb, h:h + 1], 0.0, ALU.mult, ALU.add)
                else:
                    dve.wait_ge(idx_sum, n)
                    ins = dve.scalar_tensor_tensor(out=out, in0=rbuf[:, n % 2, 0:w], scalar=wi_tok[:, qb, h:h + 1],
                                                   in1=out, op0=ALU.mult, op1=ALU.add)
                ins.then_inc(idx_sum, 1)

            def top_round(r):
                qb = 1 + r // 16
                w = width(qb)
                blk = sel[:, sel_at[qb]:sel_at[qb] + w]
                dve.wait_ge(sel_ready, qb)
                link(dve.max(out=m8[:, :], in_=blk))
                link(dve.match_replace(out=blk, in_to_replace=m8[:, :], in_values=blk, imm_value=TAKEN))
                if r % 16 == 15:
                    link(dve.tensor_scalar(blk, blk, TAKEN, 1.0, ALU.is_equal, ALU.subtract))
                    link(dve.scalar_tensor_tensor(out=blk, in0=blk, scalar=-MASK, in1=dist[:, SEQ - w:SEQ],
                                                  op0=ALU.mult, op1=ALU.add))

            def logits(U):
                p, hh, qb = U // 8, U // 4 % 2, U % 4
                m, c = pair_mixer(p)
                w = width(qb)
                out, s_bank = lg[:, U % 3, :], bank[4 + U % 2]
                mx, nm = stat[:, U % 8:U % 8 + 1], stat[:, 8 + U % 8:9 + U % 8]
                if U >= 3:
                    dve.wait_ge(pt_done, U - 2)
                if m == 1:
                    if U == 32:
                        dve.wait_ge(stored, 64)
                    src = sel[:, sel_at[qb]:sel_at[qb] + w] if qb else dist[:, SEQ - P:SEQ]
                    link(dve.tensor_scalar(abias[:, 0:w], src, SLOPES[2 * c + hh], None, ALU.mult))
                    dve.wait_ge(s_done, U + 1)
                    link(dve.tensor_tensor_reduce(out[:, 0:w], s_bank[:, 0:w], abias[:, 0:w], 1.0, TAKEN, ALU.add, ALU.max, mx))
                else:
                    dve.wait_ge(s_done, U + 1)
                    start = TAKEN
                    if qb:
                        link(dve.tensor_tensor_reduce(out[:, 0:w - P], s_bank[:, 0:w - P], fbc[:, p % 2, hh, 0:w - P], 1.0, TAKEN,
                                                      ALU.add, ALU.max, stat[:, 24:25]))
                        start = stat[:, 24:25]
                    link(dve.tensor_tensor_reduce(out[:, w - P:w], s_bank[:, w - P:w], fdiag[:, hh, w - P:w], 1.0, start,
                                                  ALU.add, ALU.max, mx))
                dve.tensor_scalar(nm, mx, -1.0, None, ALU.mult).then_inc(lg_ready, 1)

            def probs(U):
                w = width(U % 4)
                dve.wait_ge(e_ready, U + 1)
                link(dve.reciprocal(stat[:, 25:26], stat[:, 16 + U % 8:17 + U % 8]))
                dve.tensor_scalar(lg[:, U % 3, 0:w], lg[:, U % 3, 0:w], stat[:, 25:26], None, ALU.mult).then_inc(p_ready, 1)

            def mean_squares(p, kd):
                dve.wait_ge(tok_sq, 2 * p + kd + 1)
                link(dve.tensor_reduce(ms8[:, :], sq[:, :].rearrange("p (g d) -> p g d", d=HD), AX_X, ALU.add))
                dve.tensor_scalar(ms8[:, :], ms8[:, :], 1.0 / HD, EPS, ALU.mult, ALU.add).then_inc(ms_tok, 1)

            def normalize(p, kd):
                m = pair_mixer(p)[0]
                dve.wait_ge(rstd_tok, 2 * p + kd + 1)
                if p >= 1:
                    dve.wait_ge(back_done, 2 * (p - 1) + kd + 1)
                    if kd == 1:
                        dve.wait_ge(k_stored, 16 * p)
                out = tok[:, kd, :].rearrange("p (g d) -> p g d", d=HD)
                dve.tensor_tensor(out, bank[2][:, :].rearrange("p (g d) -> p g d", d=HD),
                                  rs8[:, :].unsqueeze(2).to_broadcast([P, 8, HD]), ALU.mult).then_inc(tok_read, 1)
                if kd == 1:
                    dve.wait_ge(tok_read, 2 * p + 2)
                    dve.tensor_tensor(out, out, gk_row[:, m, :].unsqueeze(1).to_broadcast([P, 8, HD]), ALU.mult).then_inc(tok_ready, 1)

            def rest_o(p):
                dve.wait_ge(o_hi_ready, p + 1)
                dve.tensor_tensor(o_lo[:, p, 0:SEQ], bank[7][:, :], o_hi[:, p, 0:SEQ].bitcast(F32), ALU.subtract).then_inc(o_lo_ready, 1)

            rows = slice(ROW_FL, ROW_FL + H)
            rest_w(0)
            rest_w(1)
            dve.wait_ge(act_evac, 2)
            dve.tensor_copy(ki2[0:64, :], zsm[0:64, 0:SEQ])
            dve.tensor_copy(ki2[64:128, :], zsm[0:64, 0:SEQ])
            link(dve.tensor_scalar(lf[rows, 0, :], zsm[rows, :], bforget[rows, 0:1], None, ALU.add))
            link(dve.tensor_scalar(lf[rows, 1, :], lf[rows, 0, :], -1.0, None, ALU.mult))
            dve.tensor_tensor(lf[rows, 1, :], lf[rows, 1, :], lf[rows, 0, :], ALU.max).then_inc(sm_ready, 1)
            rest_w(2)
            rest_w(3)
            dve.wait_ge(lf_step, 1)
            dve.scalar_tensor_tensor(out=zsm[rows, :], in0=lf[rows, 0, :], scalar=0.0, in1=lf[rows, 3, :],
                                     op0=ALU.min, op1=ALU.subtract).then_inc(sm_ready, 2)
            dve.wait_ge(sm_ready, 3)
            link(dve.tensor_scalar(lf[rows, 0, :], zsm[rows, :], -1.0, None, ALU.mult))
            dve.tensor_tensor_scan(lf[rows, 1, 0:SEQ], ones[rows, 0:1].to_broadcast([H, SEQ]), lf[rows, 0, 0:SEQ], 0.0,
                                   ALU.mult, ALU.add).then_inc(negf_ready, 1)
            rest_w(4)
            dve.wait_ge(smt_ready, 1)
            dve.tensor_scalar(wi_tok[:, :, :], abias[:, :].rearrange("p (t c) -> p t c", t=QB)[:, :, 64:64 + H],
                              H ** -0.5, QK_SCALE, ALU.mult, ALU.mult).then_inc(sm_ready, 1)
            dve.wait_ge(sm_ready, 4)
            rest_w(5)
            rest_w(6)

            for p in range(N_PAIRS + 1):
                first = T_PAIR + 3 * p
                for s in range(12):
                    if p == 0:
                        index_sum(2 * s)
                        index_sum(2 * s + 1)
                    else:
                        if p <= 4 and s == 0:
                            dve.wait_ge(fbc_landed[(p - 1) % 2], 32 * ((p - 1) // 2 + 1))
                            for hh in range(2):
                                link(dve.tensor_tensor(fdiag[:, hh, :].rearrange("p (t c) -> p t c", t=QB),
                                                       fbc[:, (p - 1) % 2, hh, :].rearrange("p (t c) -> p t c", t=QB),
                                                       cmask[:, :].unsqueeze(1).to_broadcast([P, QB, P]), ALU.add))
                        if 1 <= s < 9:
                            probs(8 * (p - 1) + s - 1)
                        if s < 8:
                            logits(8 * (p - 1) + s)
                        if s == 11:
                            rest_o(p - 1)
                    if s in (2, 4, 6):
                        rest_w(first + 1 + s // 2)
                    if p < N_PAIRS:
                        if s in (2, 4):
                            mean_squares(p, s // 2 - 1)
                        if s in (3, 5):
                            normalize(p, s // 2 - 1)
                    if 1 <= p <= 4:
                        top_round(12 * (p - 1) + s)
            def small_q():
                dve.wait_ge(s_consts, 1)
                dve.tensor_copy(qzs[0:64, :, :, 0], z_s[0:64, 24:28, :].rearrange("p c b -> p b c"))
                dve.tensor_copy(qzs[64:128, :, :, 1], z_s[64:128, 24:28, :].rearrange("p c b -> p b c")).then_inc(qzs_ready, 1)
                dve.wait_ge(gq_landed, 32)
                link(dve.tensor_scalar(gq_row[:, :, :], gq_row[:, :, :], QK_SCALE, None, ALU.mult))

            def sample_norm(n):
                j, m = (0, 1, 3, 4)[n], n // 2
                dve.wait_ge(ts_sq, n + 1)
                link(dve.tensor_reduce(s8[:, n, :], qbc[0:NS, n % 2, :].rearrange("p (g d) -> p g d", d=HD), AX_X, ALU.add))
                dve.tensor_scalar(s8[:, n, :], s8[:, n, :], 1.0 / HD, EPS, ALU.mult, ALU.add).then_inc(ts_ms, 1)
                dve.wait_ge(ts_rs, n + 1)
                view = ts[:, j, :].rearrange("p (g d) -> p g d", d=HD)
                gain = (gk_row[0:NS, m, :] if n % 2 else gq_row[:, m, :]).unsqueeze(1).to_broadcast([NS, H, HD])
                link(dve.tensor_tensor(view, view, s8[:, 4 + n, :].unsqueeze(2).to_broadcast([NS, H, HD]), ALU.mult))
                dve.tensor_tensor(view, view, gain, ALU.mult).then_inc(ts_norm, 1)

            def own_keys():
                link(dve.tensor_scalar(s8[:, 8, :], sm_tok_s[:, 64:64 + H], H ** -0.5, QK_SCALE, ALU.mult, ALU.mult))
                dve.tensor_scalar(s8[:, 8, :], s8[:, 8, :], 1.0, None, ALU.mult).then_inc(ts_norm, 1)
                dve.wait_ge(ts_norm, 5)
                buf = qbc[0:NS, 0, :].rearrange("p (g d) -> p g d", d=HD)
                for m in range(2):
                    link(dve.tensor_tensor(qbc[0:NS, 0, :], ts[:, 3 * m, :], ts[:, 3 * m + 1, :], ALU.mult))
                    link(dve.tensor_reduce(s8[:, 9 + m, :], buf, AX_X, ALU.add))
                link(dve.tensor_tensor(buf, ts[:, 6, :].rearrange("p (g d) -> p g d", d=HD),
                                       sm_tok_s[:, 0:HD].unsqueeze(1).to_broadcast([NS, H, HD]), ALU.mult))
                link(dve.tensor_reduce(s8[:, 11, :], buf, AX_X, ALU.add))
                link(dve.scalar_tensor_tensor(out=s8[:, 11, :], in0=s8[:, 11, :], scalar=0.0, in1=s8[:, 8, :],
                                              op0=ALU.max, op1=ALU.mult))
                dve.tensor_reduce(srow[:, PAST:L], s8[:, 11, :], AX_X, ALU.add).then_inc(prod_used, 1)
                dve.wait_ge(prod_used, 1)

            def idx_sum_s():
                dve.wait_ge(is_relu, 1)
                dve.wait_ge(wbc_landed, 16)
                link(dve.tensor_tensor(isr[:, :, :, :], isr[:, :, :, :], wbc[:, :, :].unsqueeze(2).to_broadcast([P, NS, NPAGE, H]), ALU.mult))
                dve.tensor_reduce(iss[:, :, :], isr[:, :, :, :], AX_X, ALU.add).then_inc(is_sum, 1)

            def top_s():
                dve.wait_ge(srow_ready, 1)
                for _ in range(TOPK_S // 8):
                    link(dve.max(out=m8[0:NS, :], in_=srow[:, :]))
                    link(dve.match_replace(out=srow[:, :], in_to_replace=m8[0:NS, :], in_values=srow[:, :], imm_value=TAKEN))
                link(dve.tensor_scalar(srow[:, :], srow[:, :], TAKEN, 1.0, ALU.is_equal, ALU.subtract))
                dve.scalar_tensor_tensor(out=srow[:, :], in0=srow[:, :], scalar=-MASK, in1=dist_s[:, :],
                                         op0=ALU.mult, op1=ALU.add).then_inc(dist_ready, 1)

            def kv_value(n):
                return 16 * sum(3 if j < 16 else 2 for j in range(n % 2, n + 1, 2))

            def sample_keys(n):
                m, b = n // 8 % 2, n % 8
                if n % 2 == 0:
                    dve.wait_ge(kv_landed[0], kv_value(n))
                    if n >= 2:
                        dve.wait_ge(prod_used, n)
                    dve.tensor_tensor(prod[:, 0], kv[:, 0], qbc[:, 0, :].unsqueeze(1).to_broadcast([P, NPAGE, SEQ]), ALU.mult)\
                        .then_inc(prod_dve, 1)
                    dve.wait_ge(prod_dve, n // 2 + 1)
                else:
                    dve.wait_ge(prod_pool, n // 2 + 1)
                last = dve.tensor_reduce(lgs[:, m, :, H * b:H * b + H], prod[:, n % 2].rearrange("p g (h d) -> p g h d", d=HD), AX_X, ALU.add)
                last.then_inc(prod_used, 1)
                if n == 15:
                    dve.wait_ge(prod_used, 17)
                    dve.nop().then_inc(lgs_ready, 1)

            def sample_probs_values(n):
                m, b = n // 8 % 2, n % 8
                dve.wait_ge(kv_landed[0], kv_value(n))
                if n == 16:
                    dve.wait_ge(pts_ready, 2)
                if n >= 18:
                    dve.wait_ge(pv_used, n - 17)
                for pg in range(NPAGE):
                    last = dve.tensor_tensor(prod[:, 0, pg, :].rearrange("p (h d) -> p h d", d=HD),
                                             kv[:, 0, pg, :].rearrange("p (h d) -> p h d", d=HD),
                                             pts[:, m, pg, H * b:H * b + H].unsqueeze(2).to_broadcast([P, H, HD]), ALU.mult)
                last.then_inc(prod_dve, 1)

            def rows_logits():
                dve.wait_ge(rows_turned, 1)
                own = bank[7][0:64, 0:24]
                for j in range(3):
                    link(dve.tensor_tensor_reduce(pself[:, 0, :], own[:, 8 * j:8 * j + 8], pick[:, :], 1.0, 0.0, ALU.mult, ALU.add,
                                                  col64[:, 8 + j:9 + j]))
                link(dve.tensor_tensor_reduce(pself[:, 0, :], slope_rows[:, :], pick[:, :], 1.0, 0.0, ALU.mult, ALU.add, col64[:, 11:12]))
                dve.tensor_copy(rows_f[:, 0:PAST], bank[7][0:64, P:P + PAST])
                link(dve.tensor_copy(rows_f[:, PAST:L], col64[:, 10:11]))
                link(dve.tensor_tensor_scan(rows_l[:, 0, :], ones[0:64, 0:1].to_broadcast([64, L]), rows_f[:, :], 0.0, ALU.mult, ALU.add))
                dve.tensor_tensor(rows_f[:, 0:PAST], bank[2][0:64, 0:PAST], rows_l[:, 0, 0:PAST], ALU.subtract)
                link(dve.tensor_tensor(rows_f[:, PAST:L], col64[:, 8:9], rows_l[:, 0, PAST:L], ALU.subtract))
                dve.tensor_copy(rows_l[:, 0, :], rows_f[:, :])
                link(dve.tensor_reduce(col64[:, 0:1], rows_f[:, :], AX_X, ALU.max))
                dve.tensor_scalar(col64[:, 2:3], col64[:, 0:1], -1.0, None, ALU.mult).then_inc(rows_lg, 1)
                dve.wait_ge(dist_spread, 1)
                dve.tensor_copy(rows_f[:, 0:PAST], bank[3][0:64, 0:PAST])
                link(dve.tensor_copy(rows_f[:, PAST:L], col64[:, 9:10]))
                link(dve.scalar_tensor_tensor(out=rows_l[:, 1, :], in0=bank[6][0:64, 0:L], scalar=col64[:, 11:12], in1=rows_f[:, :],
                                              op0=ALU.mult, op1=ALU.add))
                link(dve.tensor_reduce(col64[:, 1:2], rows_l[:, 1, :], AX_X, ALU.max))
                dve.tensor_scalar(col64[:, 3:4], col64[:, 1:2], -1.0, None, ALU.mult).then_inc(rows_lg, 1)

            def rows_probs():
                for m in range(2):
                    dve.wait_ge(rows_e, m + 1)
                    link(dve.reciprocal(col64[:, 6 + m:7 + m], col64[:, 4 + m:5 + m]))
                    dve.tensor_scalar(rows_l[:, m, :], rows_l[:, m, :], col64[:, 6 + m:7 + m], None, ALU.mult).then_inc(rows_p, 1)
                    dve.wait_ge(rows_p, m + 1)
                    last = dve.tensor_scalar(pself[:, m, :], pick[:, :], rows_l[:, m, PAST:L], None, ALU.mult)
                last.then_inc(rows_p, 1)

            def sample_out(m):
                view = ts[:, 2 + 3 * m, :].rearrange("p (g d) -> p g d", d=HD)
                if m == 0:
                    dve.wait_ge(stored, 16 * 8)
                link(dve.tensor_tensor(view, view, s8[:, 6 + m, :].unsqueeze(2).to_broadcast([NS, H, HD]), ALU.mult))
                dve.wait_ge(pv_used, 8 * (m + 1))
                dve.tensor_tensor(ts[:, 2 + 3 * m, :], ts[:, 2 + 3 * m, :], bank[2 + m][0:NS, :], ALU.add).then_inc(os_ready, 1)

            SAMPLE_STEPS = {
                T_GATE + 4: small_q,
                T_GATE + 5: lambda: [sample_norm(n) for n in range(4)] + [own_keys()],
                T_GATE + 6: idx_sum_s,
                T_GATE + 7: top_s,
                T_GATE + 8: lambda: [sample_keys(n) for n in range(0, 3)],
                T_GATE + 9: lambda: [sample_keys(n) for n in range(3, 6)],
                T_GATE + 10: lambda: [sample_keys(n) for n in range(6, 9)],
                T_GATE + 11: lambda: [sample_keys(n) for n in range(9, 12)],
                T_GATE + 12: lambda: [sample_keys(n) for n in range(12, 16)],
                T_GATE + 13: rows_logits,
                T_GATE + 14: rows_probs,
            }
            for i in range(T_GATE + 3, T_WO):
                if i in SAMPLE_STEPS:
                    SAMPLE_STEPS[i]()
                rest_w(i + 2)
            for n in range(16, 32, 2):
                sample_probs_values(n)
            for m in range(2):
                sample_out(m)
            for m in range(2):
                dve.wait_ge(os_hi, m + 1)
                dve.tensor_tensor(o_lo[:, 4 * m:4 * m + 4, SEQ:T], bank[6 + m][:, 0:4 * NS].rearrange("p (c b) -> p c b", b=NS),
                                  o_hi[:, 4 * m:4 * m + 4, SEQ:T].bitcast(F32), ALU.subtract).then_inc(os_lo, 1)

            for i in range(T_WO, T_OUT):
                m = i - T_WO
                rest_w(i + 2)
                dve.wait_ge(gates_ready, 2 * m + 2)
                for half in range(2):
                    cols = slice(half * HALF, (half + 1) * HALF)
                    b = half + 4 * par(i)
                    dve.wait_ge(proj_done, 2 * i + half + 1)
                    dve.tensor_tensor(mix[:, half, 0, :], bank[b + 2][:, 0:HALF], gate[:, 2 * m, cols], ALU.mult)
                    dve.tensor_tensor(mix[:, half, 1, :], bank[b][:, 0:HALF], gate[:, 2 * m + 1, cols], ALU.mult).then_inc(dve_evac, 1)
                    dve.wait_ge(dve_evac, 2 * m + half + 1)
                    dve.tensor_tensor(mix[:, half, 2, :], mix[:, half, 0, :], mix[:, half, 1, :], ALU.add).then_inc(mf_ready, 1)
                for half in range(2):
                    cols = slice(half * HALF, (half + 1) * HALF)
                    dve.wait_ge(mf_hi, 2 * m + half + 1)
                    dve.tensor_tensor(h_lo[:, m, cols], mix[:, half, 2, :], h_hi[:, m, cols].bitcast(F32), ALU.subtract).then_inc(mf_lo, 1)

            def add_gated(bk, half, m, vec, done):
                n = HALF if half == 0 else SEQ - HALF
                xs = x_t[:, m, half * HALF:half * HALF + n]
                g = mod_t[:, vec, :]
                if half:
                    dve.wait_ge(dve_evac, done * 2 + (2 * NCH + 1))
                    dve.tensor_tensor(xs8[:, 0:1, :], bk[:, n:HALF].unsqueeze(1), g[:, :, 1:9], ALU.mult).then_inc(xs_ready, 1)
                last = dve.scalar_tensor_tensor(out=xs, in0=bk[:, 0:n].unsqueeze(1), scalar=g[:, 0, 0:1], in1=xs,
                                                op0=ALU.mult, op1=ALU.add)
                if half:
                    dve.wait_ge(xs_ready, done + 1)
                    last = dve.tensor_tensor(x_t[:, m, SEQ:T], x_t[:, m, SEQ:T], xs8[:, 0:1, :], ALU.add)
                last.then_inc(dve_evac, 1)

            for i in range(T_OUT, T_MLP):
                m = i - T_OUT
                rest_w(i + 2)
                for half in range(2):
                    dve.wait_ge(proj_done, 2 * i + half + 1)
                    add_gated(bank[half + 4 * par(i)], half, slice(m, m + 1), slice(16 + m, 17 + m), m)
            norm_root(1)
            norm_apply(1)

            def rest_loop(i, it):
                dve.wait_ge(hi_ready, it * 4 + (i + 1))
                dve.tensor_tensor(w_lo[:, i % SPL], raw[:, i % RAW], w_hi[:, i % SPL].bitcast(F32), ALU.subtract).then_inc(lo_ready, 1)

            for q in range(2):
                with dve.Fori(0, 4) as it:
                    for b in range(4):
                        n = 32 * q + 2 * b
                        for half in range(2):
                            uf = u_f[:, 2 * (b % 2) + half, :]
                            dve.wait_ge(act_evac, it * 8 + (2 * T_WO + n + half + 1))
                            dve.tensor_tensor(uf, uf, uf, ALU.mult).then_inc(u_sq, 1)
                        rest_loop(T_MLP + 32 * q + b + 2, it)
                        for half in range(2):
                            slot = 2 * (b % 2) + half
                            cols = slice(half * HALF, (half + 1) * HALF)
                            dve.wait_ge(u_hi_ready, it * 8 + (n + half + 1))
                            dve.tensor_tensor(u_lo[:, bass.ds(it * 4 + b, 1), cols], u_f[:, slot:slot + 1, :],
                                              u_hi[:, bass.ds(it * 4 + b, 1), cols].bitcast(F32), ALU.subtract).then_inc(u_lo_ready, 1)

                def down_pair(it, mb, split):
                    for kg in range(2):
                        if split:
                            rest_loop(T_MLP + 32 * q + 16 + 2 * mb + kg + 2, it)
                    for half in range(2):
                        dve.wait_ge(proj_done, it * 8 + (2 * (T_MLP + 32 * q + 16 + 2 * mb + 1) + half + 1))
                        add_gated(bank[2 + half + 4 * mb], half, bass.ds(it * 2 + mb, 1), bass.ds(it * 2 + (40 + mb), 1),
                                  it * 2 + (8 + 8 * q + mb))

                with dve.Fori(0, 3 if q else 4) as it:
                    for mb in range(2):
                        down_pair(it, mb, True)
                if q:
                    for mb in range(2):
                        down_pair(3, mb, mb == 0)
            for j in range(1, NCH, 2):
                dve.wait_ge(y_done, j + 1)
                dve.tensor_copy(y_tok[:, :, j * P:(j + 1) * P], bank[j % 4][:, :].rearrange("p (t c) -> p t c", t=QB)).then_inc(y_dve, 1)


_OUTS = [("y_p", (1, SEQ, DM)), ("y_s", (NS, 1, DM))] + [
    (name + group, (1, *lead, *shape)) for group, lead in (("_p", (1, SEQ)), ("_s", (NS, 1)))
    for name, shape in (("k_a", (H, HD)), ("v_a", (H, HD)), ("k_idx", (HD,)), ("k_b", (H, HD)), ("v_b", (H, HD)), ("logf", (H,)))]


def kernel(**inputs):
    import numpy as _np
    import concourse.bacc as _bacc
    from concourse import mybir as _mybir
    from concourse.bass_utils import run_bass_kernel_spmd as _run

    nc = _bacc.Bacc("TRN2", target_bir_lowering=False, num_devices=1)
    arrays, aps = {}, {}
    for name, value in inputs.items():
        v = _np.ascontiguousarray(value)
        arrays[f"in_{name}"] = v
        aps[name] = nc.dram_tensor(f"in_{name}", v.shape, _mybir.dt.from_np(v.dtype), kind="ExternalInput").ap()
    for name, shape in _OUTS:
        aps[name] = nc.dram_tensor(f"out_{name}", shape, F32, kind="ExternalOutput").ap()
    layer(nc, aps)
    r = _run(nc, [arrays], core_ids=[0])
    return tuple(r.results[0][f"out_{name}"] for name, _ in _OUTS)
```

```python
from contextlib import ExitStack

import numpy as np

import concourse.bass as bass
from concourse import mybir

ALU = mybir.AluOpType
ACT = mybir.ActivationFunctionType
F32 = mybir.dt.float32
F32R = mybir.dt.float32r
I32 = mybir.dt.int32
AX_X = mybir.AxisListType.X

P = 128
DM = 1024
SEQ = 512
NS = 8
T = SEQ + NS
HALF = T // 2
H = 8
HD = 64
NCH = DM // P
QB = SEQ // P
PAGE = 128
NPAGE = 2
PAST = PAGE * NPAGE
L = PAST + 1
TOPK_P = 128
TOPK_S = L // 4
FF = 4 * DM
EPS = 1e-6
MASK = -1e30
TAKEN = -3e38
QK_SCALE = HD ** -0.5
SLOPES = [2.0 ** (-8.0 * (h + 1) / H) for h in range(H)]

QA, KA, VA, QBC, KBC, VBC, QI, KI, WI, FL, GA, GB = np.cumsum(
    [0, 512, 512, 512, 512, 512, 512, 512, 64, 8, 8, 1024]).tolist()

N_PAIRS = 8
T_SMALL, T_QI = 0, 1
T_PAIR = T_QI + 4
SLOTS = 8
HALVES_AT = [0, 1, 2, 3, 6, 7]
ADA_AT = [[4, 5] if p > 4 else [] for p in range(N_PAIRS + 1)]
STREAM = []
for _p in range(N_PAIRS + 1):
    _items = [(HALVES_AT[2 * kd + 1], "w", kd) for kd in range(3)] + [(s, "ada", 0) for s in ADA_AT[_p]]
    STREAM += [(_p, s, kind, kd) for s, kind, kd in sorted(_items)]
N_ADA = sum(kind == "ada" for _, _, kind, _ in STREAM)
T_GATE = T_PAIR + len(STREAM) - 3
T_WO = T_GATE + 2 * NCH
T_ADA = T_WO + NCH
T_OUT = T_ADA + 32 - N_ADA
T_MLP = T_OUT + NCH
RAW = 4
SPL = 2
ADA_BLOCKS = 4
ROW_FL = 96
SIDE = [(1, 6), (1, 7), (2, 6), (2, 7),
        (3, 6), (4, 7),
        (5, 6), (5, 7), (6, 6), (6, 7),
        (8, 1), (8, 2), (8, 3)]
KEYS_AT = [2, 2, 3, 2, 3, 2, 2]
VALUES_AT = {13: 6, 14: 6, 15: 4}


def pair_mixer(p):
    return p // 4, p % 4


def pair_tile(p, kd):
    return T_PAIR + [(q, kind, k) for q, _, kind, k in STREAM].index((p, "w", kd))


def ada_tile(i):
    if T_ADA <= i < T_OUT:
        return N_ADA + i - T_ADA
    if 0 <= i - T_PAIR < len(STREAM) and STREAM[i - T_PAIR][2] == "ada":
        return sum(item[2] == "ada" for item in STREAM[:i - T_PAIR])
    return None


def slot_before(p, s):
    return (p, s - 1) if s else (p - 1, SLOTS - 1)


def split_at(p, s):
    return [T_PAIR + n + SPL for n, item in enumerate(STREAM) if item[:2] == slot_before(p, s)]


def loads_at(p, s):
    return ([T_PAIR + 1 + RAW] if (p, s) == (0, 0) else []) + [i + RAW for i in split_at(p, s)]


def dma_count(i):
    if i == T_SMALL:
        return 3
    return 2 if T_WO <= i < T_ADA else 1


def unit_tile(n, slots):
    for tile, count in slots:
        if n < count:
            return tile
        n -= count


def landed_value(i):
    return 16 * sum(dma_count(j) for j in range(i % RAW, i + 1, RAW))


def par(i):
    if i < T_GATE + 4:
        return int(i == T_QI)
    return i % 2


def act_evac_value(i, half):
    return 2 * i + half + 1


def layer(nc, a):
    ctx = ExitStack()
    with ctx:
        def sem(name):
            return ctx.enter_context(nc.semaphore(name))

        place = {"at": nc.sbuf_base + 32}
        place["at"] -= place["at"] % 32

        def sb(name, shape, dt=F32, at=None):
            size = int(np.prod(shape[1:])) * 4
            size += -size % 32
            if at is None:
                at = place["at"]
                place["at"] += size
            return nc.alloc_sbuf_tensor_at(name, list(shape), dt, offset=at), at, at + size

        def new(name, shape, dt=F32):
            return sb(name, shape, dt)[0]

        ident = new("ident", [P, P])
        ones = new("ones", [P, P])
        dist = new("dist", [P, SEQ])
        cmask = new("cmask", [P, P])
        vec_t = new("vec_t", [P, 64])
        mod_t = new("mod_t", [P, 48, 9])
        amul = new("amul", [P, NCH, 9])
        cond_h = new("cond_h", [P, NCH, 18], F32R)
        g_col = new("g_col", [P, 2])
        gq = new("gq", [P, 2])
        gk_row = new("gk_row", [P, 2, HD])
        bforget = new("bforget", [P, 1])
        wi_tok = new("wi_tok", [P, QB, H])
        stat = new("stat", [P, 40])
        m8, m8_at, _ = sb("m8", [P, 8])
        xs8 = sb("xs8", [P, 1, NS], F32, m8_at)[0]
        m8b = new("m8b", [P, 8])
        ms8 = new("ms8", [P, 8])
        rs8 = new("rs8", [P, 8])
        neghalf = new("neghalf", [P, 8])
        sm_tok_s = new("sm_tok_s", [NS, P])
        page_row = new("page_row", [1, NS * NPAGE], I32)

        x_t = new("x_t", [P, NCH, T])
        raw = new("raw", [P, RAW, NCH, P])
        w_hi = new("w_hi", [P, SPL, NCH, P], F32R)
        w_lo = new("w_lo", [P, SPL, NCH, P], F32R)
        h_hi = new("h_hi", [P, NCH, T], F32R)
        h_lo = new("h_lo", [P, NCH, T], F32R)
        o_at = place["at"]
        o_hi = new("o_hi", [P, 8, T], F32R)
        o_lo = new("o_lo", [P, 8, T], F32R)
        z_s = new("z_s", [P, 29, NS])

        base = place["at"]
        rbuf = new("rbuf", [P, 2, SEQ])
        sq = new("sq", [P, SEQ])
        tok = new("tok", [P, 2, SEQ])
        z = new("z", [P, 3, SEQ])
        q_pad = new("q_pad", [P, 2, 2, SEQ])
        k_fm = new("k_fm", [P, 2, SEQ])
        v_tok = new("v_tok", [P, 2, QB, P])
        ki2 = new("ki2", [P, SEQ])
        sel = new("sel", [P, 1152])
        fbc_at = place["at"]
        fbc = new("fbc", [P, 2, 2, SEQ])
        fd_at = place["at"]
        fdiag = new("fdiag", [P, 2, SEQ])
        lg_at = place["at"]
        lg = new("lg", [P, 3, SEQ])
        abias = new("abias", [P, SEQ])
        pt_at = place["at"]
        p_t = new("p_t", [P, 2, QB, SEQ])
        ts_b = new("ts_b", [NS, 4, SEQ])
        s8 = new("s8", [NS, 12, H])
        gq_row = new("gq_row", [NS, 2, HD])
        spread = new("spread", [NS, 64])
        gather = new("gather", [64, NS])
        pick = new("pick", [64, H])
        slope_rows = new("slope_rows", [64, H])
        col64 = new("col64", [64, 16])
        wbc = new("wbc", [P, NS, H])
        qzs = new("qzs", [P, NS, 4, 2])
        lfp = new("lfp", [P, NPAGE, NS * H])
        srow = new("srow", [NS, L])
        assert place["at"] <= nc.sbuf_usable_end, (place["at"], nc.sbuf_usable_end)
        q_idx = sb("q_idx", [P, H, SEQ], F32, pt_at)[0]
        ki_pg = sb("ki_pg", [P, NS * NPAGE, 2, HD], F32, o_at + 4 * T * 4)[0]
        ki_pt = sb("ki_pt", [P, NS * NPAGE, P], F32, o_at + 12 * T * 4)[0]
        isr, _, iss_at = sb("isr", [P, NS, NPAGE, H], F32, o_at + 4 * T * 4)
        iss = sb("iss", [P, NS, NPAGE], F32, iss_at)[0]
        ts_a, _, kv0_at = sb("ts_a", [NS, 3, SEQ], F32, fbc_at)
        kv0, _, dist_at = sb("kv0", [P, NPAGE, SEQ], F32, kv0_at)
        mod_row2 = sb("mod_row2", [18, 2, 2 * P], F32, kv0_at + 4 * SEQ)[0]
        sqs = sb("sqs", [NS, SEQ], F32, kv0_at)[0]
        dist_s, _, at = sb("dist_s", [NS, L], F32, dist_at)
        assert at <= lg_at

        gate, _, rows_at = sb("gate", [P, 2 * NCH, T], F32, base)
        kv1, _, at = sb("kv1", [P, NPAGE, SEQ], F32, lg_at)
        prod0, _, at = sb("prod0", [P, NPAGE, SEQ], F32, at)
        prod1, _, at = sb("prod1", [P, NPAGE, SEQ], F32, at)
        ptz, _, at = sb("ptz", [P, 2 * NPAGE, 9 * NS * H], F32, at)
        qbc1, _, at = sb("qbc1", [P, SEQ], F32, at)
        lgs, _, at = sb("lgs", [P, 2, NPAGE, NS * H], F32, at)
        assert at <= pt_at + 4 * 4096, (at, pt_at)
        rows_l, _, at = sb("rows_l", [64, 2, L], F32, rows_at)
        rows_f, _, at = sb("rows_f", [64, L], F32, at)
        pself, _, at = sb("pself", [64, 2, H], F32, at)
        qbc0, _, at = sb("qbc0", [P, SEQ], F32, at)
        assert at <= fbc_at
        kv, prod, qbc = [kv0, kv1], [prod0, prod1], [qbc0, qbc1]
        vbuf = kv + prod
        om, _, at = sb("om", [64, 2, SEQ], F32, kv0_at)
        mix, _, at2 = sb("mix", [P, 2, 3, HALF], F32, at)
        u_hi, _, at2 = sb("u_hi", [P, 16, T], F32R, o_at)
        u_lo, _, at2 = sb("u_lo", [P, 16, T], F32R, at2)
        u_f, _, at2 = sb("u_f", [P, 4, HALF], F32, at2)
        y_tok, _, at2 = sb("y_tok", [P, QB, DM], F32, at2)
        y_stok, _, at2 = sb("y_stok", [NS, DM], F32, at2)
        assert at2 <= nc.sbuf_usable_end, (at2, nc.sbuf_usable_end)
        x_tok, _, e1 = sb("x_tok", [P, QB, DM], F32, base)
        x_stok, _, e1 = sb("x_stok", [NS, DM], F32, e1)
        cond, _, e1 = sb("cond", [9, DM], F32, e1)
        vec_rows, _, e1 = sb("vec_rows", [64, P], F32, e1)
        sig, _, e1 = sb("sig", [P, NCH * 9], F32, e1)
        nbuf, _, e1 = sb("nbuf", [P, 4, T], F32, e1)
        nrm, _, e1 = sb("nrm", [P, 2, T], F32, e1)
        nsm, _, e1 = sb("nsm", [P, 2, NCH, NS], F32, e1)
        mod_row, _, e1 = sb("mod_row", [9, 2, SEQ], F32, e1)
        cond_t, _, e1 = sb("cond_t", [P, NCH, 9], F32, e1)
        ada, _, e1 = sb("ada", [P, 2, NCH, SEQ], F32, o_at)
        assert e1 <= nc.sbuf_usable_end
        del e1
        zsm, _, e2 = sb("zsm", [P, T], F32, base)
        assert e2 <= base + 4096
        lf, _, e2 = sb("lf", [P, 4, T], F32, fd_at)
        assert e2 <= fd_at + 5 * 4 * SEQ

        bank = [ctx.enter_context(nc.psum_tensor(f"bank{i}", [P, SEQ], F32)) for i in range(8)]
        negf_d = nc.dram_tensor("negf_d", (H, SEQ), F32).ap()
        q_d = nc.dram_tensor("q_d", (2, NS, SEQ), F32).ap()
        wi_d = nc.dram_tensor("wi_d", (NS, H), F32).ap()


        small_landed = sem("small_landed")
        x_landed = sem("x_landed")
        ada_landed = [sem("ada_landed0"), sem("ada_landed1")]
        raw_landed = [sem(f"raw_landed{i}") for i in range(RAW)]
        fbc_landed = [sem("fbc_landed0"), sem("fbc_landed1")]
        consts = sem("consts")
        zeroed = sem("zeroed")
        vec_done = sem("vec_done")
        vec_ready = sem("vec_ready")
        cond_ready = sem("cond_ready")
        xt_done = sem("xt_done")
        xt_act = sem("xt_act")
        xt_dve = sem("xt_dve")
        sq_ready = sem("sq_ready")
        sq_used = sem("sq_used")
        ms_ready = sem("ms_ready")
        rs_ready = sem("rs_ready")
        cond_hi = sem("cond_hi")
        cond_lo = sem("cond_lo")
        mod_done = sem("mod_done")
        mod_row_ready = sem("mod_row_ready")
        mod_turned = sem("mod_turned")
        mod_ready = sem("mod_ready")
        nf_ready = sem("nf_ready")
        h_hi_ready = sem("h_hi_ready")
        h_lo_ready = sem("h_lo_ready")
        hi_ready = sem("hi_ready")
        lo_ready = sem("lo_ready")
        proj_done = sem("proj_done")
        act_evac = sem("act_evac")
        xs_ready = sem("xs_ready")
        dve_evac = sem("dve_evac")
        tok_done = sem("tok_done")
        tok_sq = sem("tok_sq")
        ms_tok = sem("ms_tok")
        rstd_tok = sem("rstd_tok")
        tok_ready = sem("tok_ready")
        tok_read = sem("tok_read")
        v_ready = sem("v_ready")
        back_done = sem("back_done")
        back_read = sem("back_read")
        s_done = sem("s_done")
        lg_ready = sem("lg_ready")
        e_ready = sem("e_ready")
        p_ready = sem("p_ready")
        pt_done = sem("pt_done")
        pt_ready = sem("pt_ready")
        pv_done = sem("pv_done")
        o_hi_ready = sem("o_hi_ready")
        o_lo_ready = sem("o_lo_ready")
        idx_done = sem("idx_done")
        idx_relu = sem("idx_relu")
        idx_sum = sem("idx_sum")
        sel_ready = sem("sel_ready")
        sm_ready = sem("sm_ready")
        lf_step = sem("lf_step")
        smt_done = sem("smt_done")
        smt_ready = sem("smt_ready")
        negf_ready = sem("negf_ready")
        negf_stored = sem("negf_stored")
        pages_landed = sem("pages_landed")
        side_done = sem("side_done")
        side_read = sem("side_read")
        qzs_ready = sem("qzs_ready")
        wi_ready = sem("wi_ready")
        is_sum = sem("is_sum")
        ts_ms = sem("ts_ms")
        ts_rs = sem("ts_rs")
        ts_norm = sem("ts_norm")
        wi_stored = sem("wi_stored")
        q_stored = sem("q_stored")
        wbc_landed = sem("wbc_landed")
        s_consts = sem("s_consts")
        kip_landed = sem("kip_landed")
        lfp_landed = sem("lfp_landed")
        dist_ready = sem("dist_ready")
        dist_spread = sem("dist_spread")
        kv_landed = [sem("kv_landed0"), sem("kv_landed1")]
        val_landed = [sem(f"val_landed{i}") for i in range(4)]
        prod_pool = sem("prod_pool")
        prod_dve = sem("prod_dve")
        prod_used = sem("prod_used")
        pv_used = sem("pv_used")
        rows_turned = sem("rows_turned")
        rows_lg = sem("rows_lg")
        rows_e = sem("rows_e")
        rows_p = sem("rows_p")
        pts_turned = sem("pts_turned")
        pts_ready = sem("pts_ready")
        om_ready = sem("om_ready")
        os_done = sem("os_done")
        os_hi = sem("os_hi")
        os_lo = sem("os_lo")
        gates_ready = sem("gates_ready")
        mf_ready = sem("mf_ready")
        mf_hi = sem("mf_hi")
        mf_lo = sem("mf_lo")
        u_sq = sem("u_sq")
        u_hi_ready = sem("u_hi_ready")
        u_lo_ready = sem("u_lo_ready")
        y_done = sem("y_done")
        y_act = sem("y_act")
        y_dve = sem("y_dve")
        act_self = sem("act_self")
        dve_self = sem("dve_self")
        pool_self = sem("pool_self")
        k_stored = sem("k_stored")
        v_stored = sem("v_stored")
        stored = sem("stored")

        w_in_v = a["w_in"][0].rearrange("(k p) n -> p k n", p=P)
        ada_v = a["w_ada"][0].rearrange("(k p) n -> p k n", p=P)

        def tile_dmas(i):
            dst = raw[:, i % RAW]
            if i == T_SMALL:
                return [(dst[:, :, 0:HD], w_in_v[:, :, KI:KI + HD]), (dst[:, :, 64:64 + H], w_in_v[:, :, WI:WI + H]),
                        (dst[:, :, ROW_FL:ROW_FL + H], w_in_v[:, :, FL:FL + H])]
            if i < T_PAIR:
                col = QI + (i - T_QI) * P
            elif ada_tile(i) is not None:
                n = ada_tile(i)
                col = ADA_BLOCKS * SEQ + n // 2 * 2 * P
                return [(dst.rearrange("p k c -> p (k c)").rearrange("p (k c) -> p k c", k=4),
                         ada_v[:, 4 * (n % 2):4 * (n % 2) + 4, col:col + 2 * P])]
            elif i < T_GATE + 3:
                p, _, _, kd = STREAM[i - T_PAIR]
                if p < N_PAIRS:
                    m, c = pair_mixer(p)
                    col = [[QBC, KBC, VBC], [QA, KA, VA]][m][kd] + c * P
                else:
                    col = [GA, GB][kd % 2] + kd // 2 * P
            elif i < T_WO:
                j = i - T_GATE
                col = [GA, GB][j % 2] + j // 2 * P
            elif i < T_ADA:
                m = i - T_WO
                return [(dst[:, 0:4], wob_v[:, :, m * P:(m + 1) * P]), (dst[:, 4:8], woa_v[:, :, m * P:(m + 1) * P])]
            else:
                m = i - T_OUT
                return [(dst, wout_v[:, :, m * P:(m + 1) * P])]
            return [(dst, w_in_v[:, :, col:col + P])]

        wob_v = a["w_o_b"][0].rearrange("(k p) n -> p k n", p=P)
        woa_v = a["w_o_a"][0].rearrange("(k p) n -> p k n", p=P)
        wout_v = a["w_out"][0].rearrange("(k p) n -> p k n", p=P)

        N_SMALL = 14
        n_pool = a["cache_k_a"].shape[1]
        wup_v = a["w_up"][0].rearrange("(k p) n -> p k n", p=P)
        wdn_v = a["w_down"][0].rearrange("(k p) n -> p k n", p=P)
        sel_at = [0, 0, 256, 640]

        def width(qb):
            return (qb + 1) * P

        ITERATIONS = [(p, s) for p in range(N_PAIRS + 1) for s in range(SLOTS)] + [(N_PAIRS + 1, s) for s in range(4)]
        N_UNITS = N_PAIRS * 2 * QB
        SAMPLE_POWERS = [(5, 7), (6, 1), (8, 3), (8, 5)]
        K_BACK = 6
        ADA_TILE_AT = {(p, s): T_PAIR + n for n, (p, s, kind, _) in enumerate(STREAM) if kind == "ada"}
        ADA_SECOND = {at: i for at, i in ADA_TILE_AT.items() if ada_tile(i) % 2}

        def kv_value(n):
            return 16 * (NPAGE + 1) * (n // 2 + 1)

        block = ctx.enter_context(nc.Block())

        @block.sync
        def _(sp):
            def small(dst, src):
                sp.dma_start(dst, src).then_inc(small_landed, 16)

            small(cond[0:1, :], a["c_prompt"])
            small(cond[1:9, :], a["c_sample"])
            small(vec_rows[0:48, :], a["b_ada"][0].rearrange("(r c) -> r c", c=P))
            small(vec_rows[48:56, :], a["g_norm1"][0].rearrange("(r c) -> r c", c=P))
            small(vec_rows[56:64, :], a["g_norm2"][0].rearrange("(r c) -> r c", c=P))
            for half in range(2):
                small(g_col[64 * half:64 * half + 64, 0:1], a["g_qb"][0].rearrange("(d o) -> d o", o=1))
                small(g_col[64 * half:64 * half + 64, 1:2], a["g_qa"][0].rearrange("(d o) -> d o", o=1))
            small(gk_row[:, 0, :], a["g_kb"][0].partition_broadcast(P))
            small(gk_row[:, 1, :], a["g_ka"][0].partition_broadcast(P))
            small(bforget[ROW_FL:ROW_FL + H, :], a["b_forget"][0].rearrange("(d o) -> d o", o=1))
            small(gq_row[:, 0, :], a["g_qb"][0].partition_broadcast(NS))
            small(gq_row[:, 1, :], a["g_qa"][0].partition_broadcast(NS))
            sp.dma_start(page_row[:, :], a["page_table"].rearrange("(o b) n -> o (b n)", o=1)).then_inc(pages_landed, 16)
            sp.dma_start(x_tok[:, :, :], a["x_prompt"][0].rearrange("(t p) n -> p t n", p=P)).then_inc(x_landed, 16)
            sp.dma_start(x_stok[:, :], a["x_sample"][:, 0, :]).then_inc(x_landed, 16)
            for b in range(2):
                sp.dma_start(ada[:, b], ada_v[:, :, b * SEQ:(b + 1) * SEQ]).then_inc(ada_landed[b], 16)
            for b in range(2, ADA_BLOCKS):
                sp.wait_ge(mod_done, b - 1)
                sp.dma_start(ada[:, b % 2], ada_v[:, :, b * SEQ:(b + 1) * SEQ]).then_inc(ada_landed[b % 2], 16)

            def load(i):
                if i == T_SMALL:
                    sp.wait_ge(zeroed, 1)
                if i >= RAW:
                    sp.wait_ge(lo_ready, i - RAW + 1)
                for dst, src in tile_dmas(i):
                    sp.dma_start(dst, src).then_inc(raw_landed[i % RAW], 16)

            for i in range(RAW):
                load(i)
            for i in range(RAW, T_PAIR + 2 + RAW - 1):
                load(i)
            sp.wait_ge(negf_ready, 1)
            sp.dma_start(negf_d, lf[ROW_FL:ROW_FL + H, 1, 0:SEQ]).then_inc(negf_stored, 16)
            sp.wait_ge(smt_ready, 1)
            smt = abias[:, :].rearrange("p (t c) -> p t c", t=QB)
            sp.dma_start(a["k_idx_p"][0, 0].rearrange("(t p) d -> p t d", p=P), smt[:, :, 0:HD]).then_inc(stored, 16)
            sp.dma_start(a["logf_p"][0, 0].rearrange("(t p) d -> p t d", p=P), smt[:, :, ROW_FL:ROW_FL + H]).then_inc(stored, 16)
            sp.dma_start(a["k_idx_s"][0, :, 0, :], sm_tok_s[:, 0:HD]).then_inc(stored, 16)
            sp.dma_start(a["logf_s"][0, :, 0, :], sm_tok_s[:, ROW_FL:ROW_FL + H]).then_inc(stored, 16)
            sp.wait_ge(negf_stored, 16)
            sp.wait_ge(pages_landed, 16)
            pages = [sp.value_load(page_row[0:1, i:i + 1], min_val=0, max_val=n_pool - 1) for i in range(NS * NPAGE)]
            for i in range(NS * NPAGE):
                for dup in range(2):
                    sp.dma_start(ki_pg[:, i, dup, :], a["cache_k_idx"][0, bass.ds(pages[i], 1)].rearrange("o p d -> p (o d)"))\
                        .then_inc(kip_landed, 16)
                sp.dma_start(lfp[:, i % 2, H * (i // 2):H * (i // 2) + H],
                             a["cache_logf_b"][0, bass.ds(pages[i], 1)].rearrange("o p d -> p (o d)")).then_inc(lfp_landed, 16)

            def sample_stores(m):
                ts = [ts_b, ts_a][m]
                sp.wait_ge(ts_norm, 2 * m + 2)
                sp.wait_ge(side_read, [10, 13][m])
                sp.dma_start(q_d[m], ts[:, 0, :]).then_inc(q_stored, 16)
                for j, name in ((1, ["k_b_s", "k_a_s"][m]), (2, ["v_b_s", "v_a_s"][m])):
                    sp.dma_start(a[name][0, :, 0].rearrange("b h d -> b (h d)"), ts[:, j, :]).then_inc(stored, 16)

            for p, s in ITERATIONS:
                if s == 0 and p < 4:
                    if p >= 2:
                        sp.wait_ge(lg_ready, 8 * (p - 1))
                    for hh in range(2):
                        sp.dma_start(fbc[:, p % 2, hh, :], negf_d[2 * p + hh].partition_broadcast(P)).then_inc(fbc_landed[p % 2], 16)
                for i in loads_at(p, s):
                    load(i)
                if s == K_BACK and p < N_PAIRS:
                    m, c = pair_mixer(p)
                    sp.wait_ge(tok_ready, p + 1)
                    dst = a[["k_b_p", "k_a_p"][m]][0, 0].rearrange("(t p) h d -> p t (h d)", p=P)
                    sp.dma_start(dst[:, :, c * P:(c + 1) * P], tok[:, 1, :].rearrange("p (t c) -> p t c", t=QB)).then_inc(k_stored, 16)
                if s == 1 and 1 <= p <= N_PAIRS:
                    m, c = pair_mixer(p - 1)
                    sp.wait_ge(v_ready, p)
                    dst = a[["v_b_p", "v_a_p"][m]][0, 0].rearrange("(t p) h d -> p t (h d)", p=P)
                    sp.dma_start(dst[:, :, c * P:(c + 1) * P], v_tok[:, (p - 1) % 2]).then_inc(v_stored, 16)
                if (p, s) == (1, 7):
                    sp.wait_ge(wi_ready, 1)
                    sp.dma_start(wi_d, s8[:, 8, :]).then_inc(wi_stored, 16)
                if (p, s) == (2, 7):
                    sp.wait_ge(wi_stored, 16)
                    sp.dma_start(wbc[:, :, :], wi_d.rearrange("b h -> (b h)").partition_broadcast(P).rearrange("p (b h) -> p b h", h=H))\
                        .then_inc(wbc_landed, 16)
                if (p, s) == (7, 7):
                    sample_stores(0)
            def load_pages(dst, which, unit, landed):
                m, b = unit // NS, unit % NS
                for pg in range(NPAGE):
                    sp.dma_start(dst[:, pg, :], a[which + "ba"[m]][0, bass.ds(pages[b * NPAGE + pg], 1)].rearrange("o p h d -> p (o h d)"))\
                        .then_inc(landed, 16)

            def load_keys(n):
                if n >= 2:
                    sp.wait_ge([prod_dve, prod_pool][n % 2], n // 2)
                load_pages(kv[n % 2], "cache_k_", n, kv_landed[n % 2])
                sp.dma_start(qbc[n % 2][:, :], q_d[n // NS, n % NS].partition_broadcast(P)).then_inc(kv_landed[n % 2], 16)

            def load_values(v):
                if v < 2:
                    sp.wait_ge([prod_dve, prod_pool][v], NS)
                elif v < 4:
                    sp.wait_ge(prod_used, 2 * NS - 3 + v)
                else:
                    sp.wait_ge(pv_used, v - 3)
                load_pages(vbuf[v % 4], "cache_v_", v, val_landed[v % 4])

            keys_at = [(T_GATE + 8 + j, count) for j, count in enumerate(KEYS_AT)]
            values_at = [(T_GATE + 5 + j, count) for j, count in VALUES_AT.items()]
            for i in range(T_GATE + 8, T_MLP):
                if i >= T_GATE + 9:
                    load(i)
                if i == T_GATE + 8:
                    sample_stores(1)
                    sp.wait_ge(q_stored, 32)
                    sp.wait_ge(o_lo_ready, N_PAIRS)
                    sp.wait_ge(mod_turned, ADA_BLOCKS + N_ADA // 2)
                    load_keys(0)
                    load_keys(1)
                for n in range(2, 2 * NS):
                    if i == unit_tile(n - 2, keys_at):
                        load_keys(n)
                if i == keys_at[-1][0]:
                    for v in range(4):
                        load_values(v)
                for v in range(4, 2 * NS):
                    if i == unit_tile(v - 4, values_at):
                        load_values(v)
            for q in range(2):
                with sp.Fori(0, 4) as it:
                    for b in range(4):
                        i = T_MLP + 32 * q + b
                        sp.wait_ge(lo_ready, it * 4 + (i - RAW + 1))
                        sp.dma_start(raw[:, i % RAW], wup_v[:, :, bass.ds((it * 4 + (16 * q + b)) * P, P)])\
                            .then_inc(raw_landed[i % RAW], 16)
                with sp.Fori(0, 4) as it:
                    for b in range(4):
                        i = T_MLP + 32 * q + 16 + b
                        k0 = 16 * q + 8 * (b % 2)
                        sp.wait_ge(lo_ready, it * 4 + (i - RAW + 1))
                        sp.dma_start(raw[:, i % RAW], wdn_v[:, k0:k0 + NCH, bass.ds((it * 2 + b // 2) * P, P)])\
                            .then_inc(raw_landed[i % RAW], 16)
            y_v = a["y_p"][0].rearrange("(t p) n -> p t n", p=P)
            for g in range(4):
                sp.wait_ge(y_act, g + 1)
                sp.wait_ge(y_dve, g + 1)
                sp.dma_start(y_v[:, :, 256 * g:256 * g + 256], y_tok[:, :, 256 * g:256 * g + 256]).then_inc(stored, 16)
            sp.wait_ge(y_act, 5)
            sp.dma_start(a["y_s"][:, 0, :], y_stok[:, :]).then_inc(stored, 16)
            sp.wait_ge(stored, 16 * (4 + 4 + 5))
            sp.wait_ge(k_stored, 16 * N_PAIRS)
            sp.wait_ge(v_stored, 16 * N_PAIRS)

        @block.gpsimd
        def _(pool):
            steps = [0]

            def link(ins):
                steps[0] += 1
                ins.then_inc(pool_self, 1)
                pool.wait_ge(pool_self, steps[0])

            link(pool.memset(ident[:, :], 0.0))
            pool.affine_select(out=ident[:, :], in_=ident[:, :], compare_op=ALU.not_equal, fill=1.0, base=0,
                               pattern=[[-1, P]], channel_multiplier=1).then_inc(consts, 1)
            pool.memset(ones[:, :], 1.0)
            pool.memset(neghalf[:, :], -0.5)
            link(pool.iota(dist[:, :], pattern=[[1, SEQ]], base=-(SEQ - P), channel_multiplier=-1,
                           allow_small_or_imprecise_dtypes=True))
            pool.affine_select(out=dist[:, :], in_=dist[:, :], compare_op=ALU.is_ge, fill=MASK, base=SEQ - P,
                               pattern=[[-1, SEQ]], channel_multiplier=1)
            link(pool.memset(cmask[:, :], 0.0))
            pool.affine_select(out=cmask[:, :], in_=cmask[:, :], compare_op=ALU.is_ge, fill=MASK, base=0,
                               pattern=[[-1, P]], channel_multiplier=1).then_inc(consts, 1)
            pool.memset(raw[:, T_SMALL % RAW], 0.0).then_inc(zeroed, 1)
            pool.memset(q_idx[:, :, :], 0.0).then_inc(zeroed, 1)
            pool.memset(qzs[:, :, :, :], 0.0)
            link(pool.memset(spread[:, :], 0.0))
            link(pool.affine_select(out=spread[:, :].rearrange("p (b h) -> p b h", h=H),
                                    in_=spread[:, :].rearrange("p (b h) -> p b h", h=H), compare_op=ALU.not_equal, fill=1.0,
                                    base=0, pattern=[[-1, NS], [0, H]], channel_multiplier=1))
            link(pool.memset(gather[:, :], 1.0))
            link(pool.affine_select(out=gather[:, :], in_=gather[:, :], compare_op=ALU.is_ge, fill=0.0, base=0,
                                    pattern=[[-H, NS]], channel_multiplier=1))
            link(pool.affine_select(out=gather[:, :], in_=gather[:, :], compare_op=ALU.is_ge, fill=0.0, base=H - 1,
                                    pattern=[[H, NS]], channel_multiplier=-1))
            link(pool.memset(pick[:, :], 0.0))
            for b in range(NS):
                link(pool.affine_select(out=pick[:, :], in_=pick[:, :], compare_op=ALU.not_equal, fill=1.0, base=-H * b,
                                        pattern=[[-1, H]], channel_multiplier=1))
            for h in range(H):
                pool.memset(slope_rows[:, h:h + 1], SLOPES[h])
            pool.memset(s8[:, 11, :], 0.0).then_inc(s_consts, 1)
            pool.wait_ge(h_lo_ready, NCH + 1)
            pool.memset(q_pad[:, :, :, :], 0.0).then_inc(zeroed, 1)

            def power(n):
                pool.wait_ge(ms_tok, n + 1)
                if n >= 1:
                    pool.wait_ge(tok_read, n)
                pool.tensor_tensor(rs8[:, :], ms8[:, :], neghalf[:, :], ALU.pow).then_inc(rstd_tok, 1)

            def sample_power(n):
                pool.wait_ge(ts_ms, n + 1)
                pool.tensor_tensor(s8[:, 4 + n, :], s8[:, n, :], neghalf[0:NS, :], ALU.pow).then_inc(ts_rs, 1)

            for p, s in ITERATIONS:
                for i in split_at(p, s):
                    if (p, s) == (0, 0):
                        pool.wait_ge(lo_ready, i)
                    pool.wait_ge(hi_ready, i + 1)
                    pool.tensor_tensor(w_lo[:, i % SPL], raw[:, i % RAW], w_hi[:, i % SPL].bitcast(F32), ALU.subtract).then_inc(lo_ready, 1)
                if p < N_PAIRS and s in (2, 4):
                    power(2 * p + s // 2 - 1)
                if p == 0 and s in (3, 5, 7):
                    qb = s // 2
                    pool.wait_ge(idx_sum, H * qb)
                    o = sel_at[qb] + qb * P
                    pool.affine_select(out=sel[:, o:o + P], in_=sel[:, o:o + P], compare_op=ALU.is_ge, fill=MASK,
                                       base=0, pattern=[[-1, P]], channel_multiplier=1).then_inc(sel_ready, 1)
                if (p, s) == (5, 5):
                    pool.wait_ge(lg_ready, 8 * 4)
                    pool.iota(dist_s[:, :], pattern=[[1, L]], base=-PAST, channel_multiplier=0, allow_small_or_imprecise_dtypes=True)\
                        .then_inc(s_consts, 1)
                if (p, s) in SAMPLE_POWERS:
                    sample_power(SAMPLE_POWERS.index((p, s)))
            pool.wait_ge(o_lo_ready, N_PAIRS)
            pool.memset(ptz[:, :, :], 0.0).then_inc(s_consts, 1)
            for n in range(1, 2 * NS, 2):
                pool.wait_ge(kv_landed[1], kv_value(n))
                if n >= 3:
                    pool.wait_ge(prod_used, n - 1)
                pool.tensor_tensor(prod1[:, :, :], kv1[:, :, :], qbc1[:, :].unsqueeze(1).to_broadcast([P, NPAGE, SEQ]), ALU.mult)\
                    .then_inc(prod_pool, 1)

        @block.tensor
        def _(pe):
            mm, tr = nc.tensor.matmul, nc.tensor.transpose
            pe.wait_ge(consts, 1)
            pe.wait_ge(small_landed, 16 * N_SMALL)
            tr(bank[7][:, 0:64], vec_rows[:, :], ident[0:64, 0:64])
            for j in range(NCH):
                last = tr(bank[7][:, 64 + 9 * j:73 + 9 * j], cond[:, j * P:(j + 1) * P], ident[0:9, 0:9])
            last.then_inc(vec_done, 1)
            pe.wait_ge(x_landed, 32)
            for j in range(NCH):
                if j >= 4:
                    pe.wait_ge([xt_act, xt_dve][j % 2], (j - 4) // 2 + 1)
                tr(bank[6][:, 8 * j:8 * j + 8], x_stok[:, j * P:(j + 1) * P], ident[0:NS, 0:NS])
                for t in range(QB):
                    last = tr(bank[j % 4][:, t * P:(t + 1) * P], x_tok[:, t, j * P:(j + 1) * P], ident[:, :])
                last.then_inc(xt_done, 1)

            def norm_sum(n, j):
                pe.wait_ge(sq_ready, NCH * n + j + 1)
                for half in range(2):
                    last = mm(bank[[4, 2][n] + half][:, 0:HALF], ones[:, :], nrm[:, j % 2, half * HALF:(half + 1) * HALF],
                              start=j == 0, stop=j == NCH - 1)
                last.then_inc(sq_used, 1)

            pe.wait_ge(consts, 2)
            for j in range(NCH):
                norm_sum(0, j)

            pe.wait_ge(cond_ready, 1)
            pe.wait_ge(xt_act, 4)
            pe.wait_ge(xt_dve, 5)
            for b in range(ADA_BLOCKS + 1):
                if b < ADA_BLOCKS:
                    if b >= 2:
                        pe.wait_ge(mod_row_ready, b - 1)
                    pe.wait_ge(ada_landed[b % 2], 16 * (b // 2 + 1))
                    for k in range(NCH):
                        last = mm(bank[b % 2][0:9, :], cond_t[:, k, :], ada[:, b % 2, k, :], start=k == 0, stop=k == NCH - 1)
                    last.then_inc(mod_done, 1)
                if b >= 1:
                    t = b - 1
                    pe.wait_ge(mod_row_ready, t + 1)
                    if t >= 2:
                        pe.wait_ge(mod_ready, t - 1)
                    for q in range(4):
                        last = tr(bank[2 + t % 2][:, 9 * q:9 * q + 9], mod_row[:, t % 2, q * P:(q + 1) * P], ident[0:9, 0:9])
                    last.then_inc(mod_turned, 1)

            def half_tile(i, half, out, ks=range(NCH), src=(h_hi, h_lo), k0=0, first=True, last=True):
                n0 = half * HALF
                for k in ks:
                    x_h, x_l = src[0][:, k0 + k, n0:n0 + HALF], src[1][:, k0 + k, n0:n0 + HALF]
                    mm(out, w_hi[:, i % SPL, k, :], x_h, start=first and k == ks[0], stop=False)
                    mm(out, w_hi[:, i % SPL, k, :], x_l, start=False, stop=False)
                    end = mm(out, w_lo[:, i % SPL, k, :], x_h, start=False, stop=last and k == ks[-1])
                return end

            def first_tiles(i, n):
                pe.wait_ge(hi_ready, i + 2)
                pe.wait_ge(lo_ready, i + 2)
                pe.wait_ge(h_lo_ready, (NCH + 1) * n + 1)
                for k in range(NCH):
                    pe.wait_ge(h_lo_ready, (NCH + 1) * n + k + 2)
                    for tile_ in (i, i + 1):
                        for half in range(2):
                            last = half_tile(tile_, half, bank[half + 4 * par(tile_)][:, 0:HALF], ks=[k], first=k == 0, last=k == NCH - 1)
                            if k == NCH - 1:
                                last.then_inc(proj_done, 1)

            def project(i, half):
                if half == 0:
                    pe.wait_ge(hi_ready, i + 1)
                    pe.wait_ge(lo_ready, i + 1)
                b = half + 4 * par(i)
                if ada_tile(i - 1) is not None:
                    pe.wait_ge(act_evac, 2 * i)
                    if half == 1:
                        pe.wait_ge(mod_ready, ADA_BLOCKS + (ada_tile(i - 1) + 1) // 2)
                elif i >= 1:
                    before = i - 1 if par(i - 1) == par(i) else i - 2
                    pe.wait_ge(act_evac, act_evac_value(before, half))
                half_tile(i, half, bank[b][:, 0:HALF]).then_inc(proj_done, 1)

            def evacuated(i):
                return 2 * i if i <= T_WO else 2 * (T_WO + i - T_ADA)

            def ada_product(i, bk):
                n = ada_tile(i)
                pe.wait_ge(hi_ready, i + 1)
                pe.wait_ge(lo_ready, i + 1)
                if n % 2 == 0 and i != T_ADA:
                    pe.wait_ge(act_evac, evacuated(i))
                hi, lo = (w[:, i % SPL].rearrange("p k c -> p (k c)").rearrange("p (k c) -> p k c", k=4) for w in (w_hi, w_lo))
                for k in range(4):
                    c = 4 * (n % 2) + k
                    if n % 2 == 0:
                        last = mm(bk[0:18, 0:2 * P], cond_h[:, c, :], hi[:, k, :], start=k == 0, stop=False)
                        last = mm(bk[0:9, 0:2 * P], cond_h[:, c, 0:9], lo[:, k, :], start=False, stop=False)
                    else:
                        mm(bk[0:9, 0:2 * P], cond_h[:, c, 0:9], lo[:, k, :], start=False, stop=False)
                        last = mm(bk[0:18, 0:2 * P], cond_h[:, c, :], hi[:, k, :], start=False, stop=k == 3)
                last.then_inc(proj_done, 2)

            def ada_turn(i, bk):
                n = ada_tile(i) // 2
                pe.wait_ge(act_evac, evacuated(i + 1))
                pe.wait_ge(mod_ready, ADA_BLOCKS + n)
                for u in range(2):
                    last = tr(bk[:, 18 * u:18 * u + 18], mod_row2[:, n % 2, u * P:(u + 1) * P], ident[0:18, 0:18])
                last.then_inc(mod_turned, 1)

            def scores(U):
                p, hh, qb = U // 8, U // 4 % 2, U % 4
                if U >= 2:
                    pe.wait_ge(lg_ready, U - 1)
                if U % 8 == 0:
                    pe.wait_ge(back_read, 2 * p + 2)
                mm(bank[4 + U % 2][:, 0:width(qb)], q_pad[:, p % 2, hh, qb * P:(qb + 1) * P],
                   k_fm[:, p % 2, 0:width(qb)], start=True, stop=True).then_inc(s_done, 1)

            def turn_probs(U):
                qb = U % 4
                pe.wait_ge(p_ready, U + 1)
                if U >= 1:
                    pe.wait_ge(pt_ready, U)
                for kb in range(qb + 1):
                    last = tr(bank[6][:, kb * P:(kb + 1) * P], lg[:, U % 3, kb * P:(kb + 1) * P], ident[:, :])
                last.then_inc(pt_done, 1)

            def values(p, hh):
                pe.wait_ge(pt_ready, 8 * p + 4 * hh + 4)
                pe.wait_ge(v_ready, p + 1)
                if p >= 1:
                    pe.wait_ge(o_lo_ready, p)
                for kb in range(QB):
                    last = mm(bank[7][64 * hh:64 * hh + 64, kb * P:SEQ], v_tok[:, p % 2, kb, 64 * hh:64 * hh + 64],
                              p_t[:, hh, kb, kb * P:SEQ], start=kb == 0, stop=kb == QB - 1)
                last.then_inc(pv_done, 1)

            def to_tokens(p, kd):
                pe.wait_ge(act_evac, act_evac_value(pair_tile(p, kd), 1))
                if kd == 0:
                    if p == 0:
                        pe.wait_ge(smt_ready, 1)
                    else:
                        pe.wait_ge(v_ready, p)
                else:
                    pe.wait_ge(tok_read, 2 * p + kd)
                before = sum(at[0] < p or (kd == 2 and at[0] == p) for at in SIDE)
                if before:
                    pe.wait_ge(side_read, before)
                for t in range(QB):
                    last = tr(bank[2][:, t * P:(t + 1) * P], z[:, kd, t * P:(t + 1) * P], ident[:, :])
                last.then_inc(tok_done, 1)

            def to_features(p, kd):
                pe.wait_ge(tok_read if kd == 0 else tok_ready, 2 * p + 1 if kd == 0 else p + 1)
                if p == 0 and kd == 0:
                    pe.wait_ge(smt_ready, 1)
                if 2 * p + kd >= 1:
                    pe.wait_ge(back_read, 2 * p + kd)
                for t in range(QB):
                    last = tr(bank[3][:, t * P:(t + 1) * P], tok[:, kd, t * P:(t + 1) * P], ident[:, :])
                last.then_inc(back_done, 1)

            def index_scores(n):
                qb, h = 1 + n // H, n % H
                if n >= 2:
                    pe.wait_ge(idx_relu, n - 1)
                mm(bank[4 + n % 2][:, 0:width(qb)], q_idx[:, h, qb * P:(qb + 1) * P], ki2[:, 0:width(qb)],
                   start=True, stop=True).then_inc(idx_done, 1)

            def side_step(e):
                p, bk = SIDE[e][0], bank[2 + e % 2]
                if e >= 2:
                    pe.wait_ge(side_read, e - 1)
                if p == N_PAIRS:
                    pe.wait_ge(v_ready, p)
                elif e % 2:
                    pe.wait_ge(back_read, 2 * p + 2)
                else:
                    pe.wait_ge(tok_read, 2 * p + 2)
                if e < 4:
                    pe.wait_ge(kip_landed, 16 * 2 * NS * NPAGE)
                    for q in range(4):
                        last = tr(bk[:, q * P:(q + 1) * P], ki_pg[:, 4 * e + q].rearrange("p a d -> p (a d)"), ident[:, :])
                elif e == 4:
                    pe.wait_ge(side_read, 4)
                    pe.wait_ge(qzs_ready, 1)
                    for i in range(NS * NPAGE):
                        last = mm(bk[:, H * i:H * i + H], ki_pt[:, i, :], qzs[:, i // 2].rearrange("p c h -> p (c h)"),
                                  start=True, stop=True)
                elif e == 5:
                    pe.wait_ge(is_sum, 1)
                    for pg in range(NPAGE):
                        last = tr(bk[0:NS, pg * P:(pg + 1) * P], iss[:, :, pg], ident[:, :])
                else:
                    z0 = [0, 4, 24, 8, 12, 16, 20][e - 6]
                    for c in range(4):
                        last = tr(bk[0:NS, c * P:(c + 1) * P], z_s[:, z0 + c, :], ident[:, :])
                last.then_inc(side_done, 1)

            first_tiles(0, 0)
            for i in range(2, T_PAIR):
                project(i, 0)
                project(i, 1)
                if i == 2:
                    pe.wait_ge(sm_ready, 3)
                    for t in range(QB):
                        tr(bank[2][:, t * P:(t + 1) * P], zsm[:, t * P:(t + 1) * P], ident[:, :])
                    tr(bank[3][0:NS, 0:P], zsm[:, SEQ:T], ident[:, :]).then_inc(smt_done, 1)

            for p, s in ITERATIONS:
                U = SLOTS * (p - 1) + s
                if s in HALVES_AT and p <= N_PAIRS:
                    project(pair_tile(p, HALVES_AT.index(s) // 2), HALVES_AT.index(s) % 2)
                if p < N_PAIRS:
                    if s == 2:
                        to_tokens(p, 0)
                    if s == 4:
                        to_tokens(p, 1)
                        to_features(p, 0)
                    if s == K_BACK:
                        to_features(p, 1)
                if s == 0 and 1 <= p <= N_PAIRS:
                    to_tokens(p - 1, 2)
                if p == 0:
                    if s == 0:
                        pe.wait_ge(act_evac, act_evac_value(T_PAIR - 1, 1))
                        pe.wait_ge(sm_ready, 3)
                    for n in range(3 * s, 3 * s + 3):
                        index_scores(n)
                if 0 <= U - 2 < N_UNITS:
                    turn_probs(U - 2)
                if 0 <= U < N_UNITS:
                    if U < 2:
                        pe.wait_ge(idx_relu, 24)
                    scores(U)
                if s == 6 and 1 <= p <= N_PAIRS:
                    values(p - 1, 0)
                if s == 2 and p >= 2:
                    values(p - 2, 1)
                if slot_before(p, s) in ADA_SECOND:
                    ada_turn(ADA_SECOND[slot_before(p, s)], bank[1])
                if (p, s) in ADA_TILE_AT:
                    ada_product(ADA_TILE_AT[p, s], bank[0])
                if (p, s) in SIDE:
                    side_step(SIDE.index((p, s)))
            def spread_dist():
                pe.wait_ge(dist_ready, 1)
                mm(bank[6][0:64, 0:L], spread[:, :], srow[:, :], start=True, stop=True).then_inc(dist_spread, 1)

            def turn_rows():
                pe.wait_ge(prod_used, 2 * NS)
                pe.wait_ge(side_read, len(SIDE))
                pe.wait_ge(lfp_landed, 16 * NS * NPAGE)
                for m in range(2):
                    for pg in range(NPAGE):
                        tr(bank[2 + m][0:64, pg * P:(pg + 1) * P], lgs[:, m, pg, :], ident[:, :])
                for pg in range(NPAGE):
                    tr(bank[7][0:64, P + pg * P:2 * P + pg * P], lfp[:, pg, :], ident[:, :])
                mm(bank[7][0:64, 0:16], spread[:, :], s8[:, 9:11, :].rearrange("p a h -> p (a h)"), start=True, stop=True)
                mm(bank[7][0:64, 16:24], spread[:, :], sm_tok_s[:, ROW_FL:ROW_FL + H], start=True, stop=True).then_inc(rows_turned, 1)

            def turn_pts():
                for m in range(2):
                    pe.wait_ge(rows_p, m + 1)
                    for pg in range(NPAGE):
                        tr(bank[6][:, (2 * m + pg) * 64:(2 * m + pg + 1) * 64], rows_l[:, m, pg * P:(pg + 1) * P], ident[0:64, 0:64])
                pe.wait_ge(rows_p, 3)
                mm(bank[7][0:NS, 0:16], gather[:, :], pself[:, :, :].rearrange("p a h -> p (a h)"), start=True, stop=True)\
                    .then_inc(pts_turned, 1)

            def sample_values(v):
                m, b = v // NS, v % NS
                pe.wait_ge(val_landed[v % 4], 16 * NPAGE * (v // 4 + 1))
                for pg in range(NPAGE):
                    last = mm(bank[2 + m][0:64, :], ptz[:, NPAGE * m + pg, 64 * b:64 * b + 64], vbuf[v % 4][:, pg, :],
                              start=b == 0 and pg == 0, stop=b == NS - 1 and pg == NPAGE - 1)
                last.then_inc(pv_used, 1)

            def sample_outputs(m):
                pe.wait_ge(om_ready, m + 1)
                for c in range(4):
                    out = bank[6][:, 256 + (4 * m + c) * NS:256 + (4 * m + c + 1) * NS]
                    mm(out, om[:, m, c * P:(c + 1) * P], gather[:, :], start=True, stop=False)
                    last = mm(out, [ts_b, ts_a][m][:, 2, c * P:(c + 1) * P], ident[0:NS, 0:NS], start=False, stop=True)
                last.then_inc(os_done, 1)

            pe.wait_ge(o_hi_ready, N_PAIRS)
            pe.wait_ge(o_lo_ready, N_PAIRS)
            v = 0
            for i in range(T_GATE + 3, T_WO):
                if i == T_GATE + 3:
                    spread_dist()
                if i == T_GATE + 10:
                    turn_rows()
                if i == T_GATE + 12:
                    turn_pts()
                for _ in range(VALUES_AT.get(i - T_GATE, 0)):
                    if v == 0:
                        pe.wait_ge(pts_ready, 2)
                    sample_values(v)
                    v += 1
                project(i, 0)
                project(i, 1)
            sample_outputs(0)
            sample_outputs(1)

            pe.wait_ge(os_hi, 1)
            pe.wait_ge(os_lo, 1)
            pe.wait_ge(act_evac, act_evac_value(T_WO - 1, 1))
            for i in range(T_WO, T_ADA):
                pe.wait_ge(hi_ready, i + 1)
                pe.wait_ge(lo_ready, i + 1)
                for half in range(2):
                    if i >= T_WO + 2:
                        pe.wait_ge(dve_evac, 2 * (i - 2 - T_WO) + half + 1)
                    b = half + 4 * par(i)
                    half_tile(i, half, bank[b][:, 0:HALF], range(0, 4), (o_hi, o_lo))
                    half_tile(i, half, bank[b + 2][:, 0:HALF], range(4, 8), (o_hi, o_lo)).then_inc(proj_done, 1)
            pe.wait_ge(dve_evac, 2 * (NCH - 1))
            for i in range(T_ADA, T_OUT):
                ada_product(i, bank[4])
                if ada_tile(i) % 2:
                    ada_turn(i, bank[5])
            pe.wait_ge(mf_hi, 2 * NCH)
            pe.wait_ge(mf_lo, 2 * NCH)
            for i in range(T_OUT, T_MLP):
                pe.wait_ge(hi_ready, i + 1)
                pe.wait_ge(lo_ready, i + 1)
                for half in range(2):
                    if i == T_OUT:
                        pe.wait_ge(mod_ready, ADA_BLOCKS + 16)
                    pe.wait_ge(dve_evac, 2 * (NCH + i - T_OUT - 2) + half + 1)
                    half_tile(i, half, bank[half + 4 * par(i)][:, 0:HALF]).then_inc(proj_done, 1)
                if i > T_OUT:
                    norm_sum(1, i - T_OUT - 1)
            norm_sum(1, NCH - 1)
            def up_tile(q, b, it):
                i = T_MLP + 32 * q + b
                pe.wait_ge(hi_ready, it * 4 + (i + 1))
                pe.wait_ge(lo_ready, it * 4 + (i + 1))
                for half in range(2):
                    pe.wait_ge(act_evac, it * 8 + (2 * (T_WO + T_OUT - T_ADA) + 32 * q + 2 * (b - 2) + half + 1))
                    half_tile(i, half, bank[half + 4 * (i % 2)][:, 0:HALF]).then_inc(proj_done, 1)

            first_tiles(T_MLP, 1)
            up_tile(0, 2, 0)
            up_tile(0, 3, 0)
            for q in range(2):
                with pe.Fori(0 if q else 1, 4) as it:
                    for b in range(4):
                        up_tile(q, b, it)
                pe.wait_ge(u_hi_ready, 32 * (q + 1))
                pe.wait_ge(u_lo_ready, 32 * (q + 1))
                with pe.Fori(0, 4) as it:
                    for b in range(4):
                        i = T_MLP + 32 * q + 16 + b
                        kg, mb = b % 2, b // 2
                        pe.wait_ge(hi_ready, it * 4 + (i + 1))
                        pe.wait_ge(lo_ready, it * 4 + (i + 1))
                        for half in range(2):
                            if kg == 0:
                                pe.wait_ge(dve_evac, it * 4 + (32 + 16 * q + 2 * (mb - 2) + half + 1))
                            half_tile(i, half, bank[2 + half + 4 * mb][:, 0:HALF], src=(u_hi, u_lo), k0=8 * kg,
                                      first=kg == 0, last=kg == 1).then_inc(proj_done, 1)
            pe.wait_ge(dve_evac, 64)
            for j in range(NCH):
                if j >= 4:
                    pe.wait_ge([y_act, y_dve][j % 2], (j - 4) // 2 + 1)
                tr(bank[4 + j // 4][0:NS, (j % 4) * P:(j % 4 + 1) * P], x_t[:, j, SEQ:T], ident[:, :])
                for t in range(QB):
                    last = tr(bank[j % 4][:, t * P:(t + 1) * P], x_t[:, j, t * P:(t + 1) * P], ident[:, :])
                last.then_inc(y_done, 1)

        @block.scalar
        def _(act):
            A = nc.scalar.activation
            steps = [0]

            def link(ins):
                steps[0] += 1
                ins.then_inc(act_self, 1)
                act.wait_ge(act_self, steps[0])

            act.wait_ge(vec_done, 1)
            A(vec_t[:, :], bank[7][:, 0:64], ACT.Copy)
            A(sig[:, :], bank[7][:, 64:136], ACT.Sigmoid).then_inc(vec_ready, 1)
            for j in range(0, NCH, 2):
                act.wait_ge(xt_done, j + 1)
                A(x_t[:, j, 0:SEQ], bank[j % 4][:, :], ACT.Copy).then_inc(xt_act, 1)

            def square(n, j):
                if j >= 2 or n >= 1:
                    act.wait_ge(sq_used, NCH * n + j - 1)
                A(nrm[:, j % 2, :], x_t[:, j, :], ACT.Square).then_inc(sq_ready, 1)

            def inverse_root(n):
                A(stat[0:1, 39:40], ones[0:1, 0:1], ACT.Ln)
                act.wait_ge(ms_ready, n + 1)
                link(A(nbuf[:, 1, :], nbuf[:, 0, :], ACT.Ln))
                A(nbuf[:, 1, :], nbuf[:, 1, :], ACT.Exp, scale=-0.5).then_inc(rs_ready, 1)

            act.wait_ge(cond_ready, 1)
            A(cond_h[:, :, 0:9], cond_t[:, :, :], ACT.Copy).then_inc(cond_hi, 1)
            act.wait_ge(xt_act, 4)
            act.wait_ge(xt_dve, 5)
            for j in range(NCH):
                square(0, j)
            act.wait_ge(consts, 2)
            inverse_root(0)

            def mod_rows(b, value):
                act.wait_ge(mod_done, value)
                A(mod_row[:, b, :], bank[b][0:9, :], ACT.Copy).then_inc(mod_row_ready, 1)

            for t in range(ADA_BLOCKS):
                if t >= 2:
                    act.wait_ge(mod_turned, t - 1)
                mod_rows(t % 2, t + 1)

            def round_h(n):
                act.wait_ge(nf_ready, (NCH + 1) * n + 1)
                A(h_hi[:, :, SEQ:T], nsm[:, 0], ACT.Copy).then_inc(h_hi_ready, 1)
                for j in range(NCH):
                    act.wait_ge(nf_ready, (NCH + 1) * n + j + 2)
                    A(h_hi[:, j, 0:SEQ], nrm[:, j % 2, 0:SEQ], ACT.Copy).then_inc(h_hi_ready, 1)

            def round_w(i):
                act.wait_ge(raw_landed[i % RAW], landed_value(i))
                if i >= SPL:
                    act.wait_ge(proj_done, 2 * (i - SPL + 1))
                A(w_hi[:, i % SPL], raw[:, i % RAW], ACT.Copy).then_inc(hi_ready, 1)

            round_w(0)
            round_w(1)
            round_h(0)

            def keep_samples(i, b, chunk):
                A(z_s[:, chunk, :], bank[b][:, HALF - NS:HALF], ACT.Copy)

            def store_z(p, kd, half):
                m, c = pair_mixer(p)
                i = pair_tile(p, kd)
                act.wait_ge(proj_done, 2 * i + half + 1)
                if half == 0:
                    if p >= 1:
                        act.wait_ge(tok_done, 3 * (p - 1) + kd + 1)
                    A(z[:, kd, 0:HALF], bank[0][:, 0:HALF], ACT.Copy).then_inc(act_evac, 1)
                else:
                    A(z[:, kd, HALF:SEQ], bank[1][:, 0:SEQ - HALF], ACT.Copy)
                    A(z_s[:, 12 * m + 4 * kd + c, :], bank[1][:, SEQ - HALF:HALF], ACT.Copy).then_inc(act_evac, 1)

            def store_gate(i, j, half):
                act.wait_ge(proj_done, 2 * i + half + 1)
                if j < 3:
                    act.wait_ge(k_stored, 16 * N_PAIRS)
                A(gate[:, j, half * HALF:(half + 1) * HALF], bank[half + 4 * par(i)][:, 0:HALF], ACT.Copy).then_inc(act_evac, 1)

            def exps(U):
                w = width(U % 4)
                act.wait_ge(lg_ready, U + 1)
                A(lg[:, U % 3, 0:w], lg[:, U % 3, 0:w], ACT.Exp, bias=stat[:, 8 + U % 8:9 + U % 8],
                  accum_out=stat[:, 16 + U % 8:17 + U % 8]).then_inc(e_ready, 1)

            def store_pt(U):
                p, hh, qb = U // 8, U // 4 % 2, U % 4
                act.wait_ge(pt_done, U + 1)
                if p >= 1:
                    act.wait_ge(pv_done, 2 * (p - 1) + hh + 1)
                A(p_t[:, hh, 0:qb + 1, qb * P:(qb + 1) * P], bank[6][:, 0:width(qb)].rearrange("p (k c) -> p k c", k=qb + 1),
                  ACT.Copy).then_inc(pt_ready, 1)

            def square_tok(p, kd):
                act.wait_ge(tok_done, 3 * p + kd + 1)
                if 2 * p + kd >= 1:
                    act.wait_ge(ms_tok, 2 * p + kd)
                A(sq[:, :], bank[2][:, :], ACT.Square).then_inc(tok_sq, 1)

            def store_back(p, kd):
                m = pair_mixer(p)[0]
                act.wait_ge(back_done, 2 * p + kd + 1)
                if kd == 0:
                    if p == 0:
                        act.wait_ge(zeroed, 3)
                    if p >= 2:
                        act.wait_ge(s_done, 8 * (p - 1))
                    A(q_pad[0:64, p % 2, 0, :], bank[3][0:64, :], ACT.Copy, scale=gq[0:64, m:m + 1])
                    A(q_pad[64:128, p % 2, 1, :], bank[3][64:128, :], ACT.Copy, scale=gq[64:128, m:m + 1]).then_inc(back_read, 1)
                else:
                    A(k_fm[:, p % 2, :], bank[3][:, :], ACT.Copy).then_inc(back_read, 1)

            def store_v(p):
                act.wait_ge(tok_done, 3 * p + 3)
                if p >= 2:
                    act.wait_ge(v_stored, 16 * (p - 1))
                    act.wait_ge(pv_done, 2 * (p - 1))
                A(v_tok[:, p % 2], bank[2][:, :].rearrange("p (t c) -> p t c", t=QB), ACT.Copy).then_inc(v_ready, 1)

            def round_o(p):
                act.wait_ge(pv_done, 2 * p + 2)
                A(o_hi[:, p, 0:SEQ], bank[7][:, :], ACT.Copy).then_inc(o_hi_ready, 1)

            def relu_scores(n):
                w = width(1 + n // H)
                act.wait_ge(idx_done, n + 1)
                if n >= 2:
                    act.wait_ge(idx_sum, n - 1)
                if n < 2:
                    act.wait_ge(smt_done, 1)
                A(rbuf[:, n % 2, 0:w], bank[4 + n % 2][:, 0:w], ACT.Relu).then_inc(idx_relu, 1)

            def ada_rows(i, bk):
                n = ada_tile(i) // 2
                act.wait_ge(proj_done, 2 * (i + 1))
                act.wait_ge(mod_turned, ADA_BLOCKS + n - 1)
                A(mod_row2[:, n % 2, :], bk[0:18, 0:2 * P], ACT.Copy).then_inc(act_evac, 4)

            def side_store(e):
                bk = bank[2 + e % 2]
                act.wait_ge(side_done, e + 1)
                if e < 4:
                    ins = A(ki_pt[:, 4 * e:4 * e + 4, :], bk[:, :].rearrange("p (a c) -> p a c", a=4), ACT.Copy)
                elif e == 4:
                    ins = A(isr[:, :, :, :].rearrange("p b g h -> p (b g h)"), bk[:, 0:P], ACT.Relu)
                elif e == 5:
                    ins = A(srow[:, 0:PAST], bk[0:NS, 0:PAST], ACT.Copy)
                else:
                    ins = A(ts_b[:, [0, 1, 3, 2][e - 6], :] if e < 10 else ts_a[:, e - 10, :], bk[0:NS, :], ACT.Copy)
                ins.then_inc(side_read, 1)

            for i in range(T_PAIR):
                for half in range(2):
                    act.wait_ge(proj_done, 2 * i + half + 1)
                    lo, hi = half * HALF, min(half * HALF + HALF, SEQ)
                    if i == T_SMALL:
                        A(zsm[:, half * HALF:(half + 1) * HALF], bank[half][:, 0:HALF], ACT.Copy).then_inc(act_evac, 1)
                        continue
                    c = i - T_QI
                    if i == T_QI:
                        act.wait_ge(zeroed, 2)
                    A(q_idx[0:64, 2 * c, lo:hi], bank[half + 4 * par(i)][0:64, 0:hi - lo], ACT.Copy)
                    last = A(q_idx[64:128, 2 * c + 1, lo:hi], bank[half + 4 * par(i)][64:128, 0:hi - lo], ACT.Copy)
                    if half == 1:
                        last = A(z_s[:, 24 + c, :], bank[1 + 4 * par(i)][:, hi - lo:HALF], ACT.Copy)
                    last.then_inc(act_evac, 1)
                round_w(i + 2)
                if i == 1:
                    act.wait_ge(sm_ready, 1)
                    rows = slice(ROW_FL, ROW_FL + H)
                    link(A(lf[rows, 2, :], lf[rows, 1, :], ACT.Exp, scale=-1.0))
                    A(lf[rows, 3, :], lf[rows, 2, :], ACT.Ln, bias=1.0).then_inc(lf_step, 1)
                if i == 3:
                    act.wait_ge(smt_done, 1)
                    A(abias[:, :], bank[2][:, :], ACT.Copy)
                    A(sm_tok_s[:, :], bank[3][0:NS, 0:P], ACT.Copy).then_inc(smt_ready, 1)

            for p, s in ITERATIONS:
                U = SLOTS * (p - 1) + s
                before = slot_before(p, s)
                if before in ADA_SECOND:
                    ada_rows(ADA_SECOND[before], bank[0])
                if before in SIDE:
                    side_store(SIDE.index(before))
                for i in split_at(p, s):
                    round_w(i)
                if s in HALVES_AT and p <= N_PAIRS:
                    kd, half = divmod(HALVES_AT.index(s), 2)
                    if p < N_PAIRS:
                        store_z(p, kd, half)
                    else:
                        store_gate(pair_tile(p, kd), kd, half)
                if p < N_PAIRS and s in (2, 4):
                    square_tok(p, s // 2 - 1)
                if p == 0:
                    for n in range(3 * s, 3 * s + 3):
                        relu_scores(n)
                if 0 <= U < N_UNITS:
                    exps(U)
                if 0 <= U - 2 < N_UNITS:
                    store_pt(U - 2)
                if s == 2 and p >= 2:
                    round_o(p - 2)
                if p < N_PAIRS:
                    if s == 4:
                        store_back(p, 0)
                    if s == K_BACK:
                        store_back(p, 1)
                if s == 0 and 1 <= p <= N_PAIRS:
                    store_v(p - 1)
            def row_exps():
                for m in range(2):
                    act.wait_ge(rows_lg, m + 1)
                    A(rows_l[:, m, :], rows_l[:, m, :], ACT.Exp, bias=col64[:, 2 + m:3 + m],
                      accum_out=col64[:, 4 + m:5 + m]).then_inc(rows_e, 1)

            def store_pts():
                act.wait_ge(pts_turned, 1)
                act.wait_ge(s_consts, 3)
                A(ptz[:, :, :].rearrange("p g (b x) -> p g b x", b=NS)[:, :, :, 0:H],
                  bank[6][:, 0:256].rearrange("p (g b h) -> p g b h", g=2 * NPAGE, b=NS), ACT.Copy).then_inc(pts_ready, 1)
                A(s8[:, 6:8, :].rearrange("p a h -> p (a h)"), bank[7][0:NS, 0:16], ACT.Copy).then_inc(pts_ready, 1)

            for i in range(T_GATE + 3, T_WO):
                if i == T_GATE + 11:
                    row_exps()
                if i == T_GATE + 12:
                    store_pts()
                for half in range(2):
                    store_gate(i, i - T_GATE, half)
                round_w(i + 2)
            for j in range(2 * NCH):
                if j == 0:
                    act.wait_ge(act_evac, act_evac_value(T_WO - 1, 1))
                A(gate[:, j, :], gate[:, j, :], ACT.Sigmoid).then_inc(gates_ready, 1)
            act.wait_ge(os_done, 2)
            A(o_hi[:, :, SEQ:T], bank[6][:, 256:256 + 8 * NS].rearrange("p (c b) -> p c b", b=NS), ACT.Copy).then_inc(os_hi, 1)

            for i in range(T_WO, T_ADA):
                m = i - T_WO
                round_w(i + 2)
                for half in range(2):
                    act.wait_ge(mf_ready, 2 * m + half + 1)
                    if m == 0 and half == 0:
                        act.wait_ge(proj_done, 2 * T_WO)
                    A(h_hi[:, m, half * HALF:(half + 1) * HALF], mix[:, half, 2, :], ACT.Copy).then_inc(mf_hi, 1)
            for i in range(T_ADA, T_OUT):
                if ada_tile(i) % 2:
                    ada_rows(i, bank[4])
                round_w(i + 2)
            for i in range(T_OUT, T_MLP):
                if i > T_OUT:
                    act.wait_ge(dve_evac, 2 * (NCH + i - T_OUT))
                    square(1, i - T_OUT - 1)
                round_w(i + 2)
            act.wait_ge(dve_evac, 4 * NCH)
            square(1, NCH - 1)
            inverse_root(1)
            round_h(1)

            def round_loop(i, it):
                act.wait_ge(raw_landed[i % RAW], it * 16 + landed_value(i))
                act.wait_ge(proj_done, it * 8 + 2 * (i - SPL + 1))
                A(w_hi[:, i % SPL], raw[:, i % RAW], ACT.Copy).then_inc(hi_ready, 1)

            def up_tile(q, b, it):
                n = 32 * q + 2 * b
                for half in range(2):
                    act.wait_ge(proj_done, it * 8 + (2 * (T_MLP + 32 * q + b) + half + 1))
                    if q or b >= 2:
                        act.wait_ge(u_lo_ready, it * 8 + (n + half - 3))
                    A(u_f[:, 2 * (b % 2) + half, :], bank[half + 4 * ((T_MLP + b) % 2)][:, 0:HALF], ACT.Relu).then_inc(act_evac, 1)
                round_loop(T_MLP + 32 * q + b + 2, it)
                for half in range(2):
                    act.wait_ge(u_sq, it * 8 + (n + half + 1))
                    A(u_hi[:, bass.ds(it * 4 + b, 1), half * HALF:(half + 1) * HALF], u_f[:, 2 * (b % 2) + half:2 * (b % 2) + half + 1, :],
                      ACT.Copy).then_inc(u_hi_ready, 1)

            for q in range(2):
                if q == 0:
                    for b in range(4):
                        up_tile(q, b, 0)
                    with act.Fori(1, 4) as it:
                        for b in range(4):
                            act.wait_ge(u_lo_ready, it * 8 + (2 * b - 2))
                            up_tile(q, b, it)
                else:
                    with act.Fori(0, 4) as it:
                        for b in range(4):
                            up_tile(q, b, it)
                last = 3 if q else 4
                with act.Fori(0, last) as it:
                    for b in range(4):
                        round_loop(T_MLP + 32 * q + 16 + b + 2, it)
                if q:
                    for b in range(2):
                        round_loop(T_MLP + 32 * q + 16 + b + 2, 3)
            for j in range(0, NCH, 2):
                act.wait_ge(y_done, j + 1)
                A(y_tok[:, :, j * P:(j + 1) * P], bank[j % 4][:, :].rearrange("p (t c) -> p t c", t=QB), ACT.Copy).then_inc(y_act, 1)
            act.wait_ge(y_done, NCH)
            A(y_stok[:, 0:SEQ], bank[4][0:NS, :], ACT.Copy)
            A(y_stok[:, SEQ:DM], bank[5][0:NS, :], ACT.Copy).then_inc(y_act, 1)

        @block.vector
        def _(dve):
            steps = [0]

            def link(ins):
                steps[0] += 1
                ins.then_inc(dve_self, 1)
                dve.wait_ge(dve_self, steps[0])

            dve.wait_ge(small_landed, 16 * N_SMALL)
            dve.tensor_scalar(gq[:, :], g_col[:, :], QK_SCALE, None, ALU.mult)
            dve.wait_ge(vec_ready, 1)
            dve.tensor_tensor(cond_t[:, :, :].rearrange("p k c -> p (k c)"), bank[7][:, 64:136], sig[:, :], ALU.mult).then_inc(cond_ready, 1)
            for j in range(1, NCH, 2):
                dve.wait_ge(xt_done, j + 1)
                dve.tensor_copy(x_t[:, j, 0:SEQ], bank[j % 4][:, :]).then_inc(xt_dve, 1)
            dve.tensor_copy(x_t[:, :, SEQ:T], bank[6][:, 0:64].rearrange("p (j c) -> p j c", c=NS)).then_inc(xt_dve, 1)

            def norm_root(n):
                dve.wait_ge(sq_used, NCH * (n + 1))
                dve.tensor_scalar(nbuf[:, 0, 0:HALF], bank[[4, 2][n]][:, 0:HALF], 1.0 / DM, EPS, ALU.mult, ALU.add)
                dve.tensor_scalar(nbuf[:, 0, HALF:T], bank[[5, 3][n]][:, 0:HALF], 1.0 / DM, EPS, ALU.mult, ALU.add).then_inc(ms_ready, 1)
                dve.wait_ge(rs_ready, n + 1)
                link(dve.tensor_tensor(nbuf[:, 2, :], nbuf[:, 0, :], nbuf[:, 1, :], ALU.mult))
                link(dve.tensor_tensor(nbuf[:, 2, :], nbuf[:, 2, :], nbuf[:, 1, :], ALU.mult))
                link(dve.tensor_scalar(nbuf[:, 2, :], nbuf[:, 2, :], -0.5, 1.5, ALU.mult, ALU.add))
                link(dve.tensor_tensor(nbuf[:, 1, :], nbuf[:, 1, :], nbuf[:, 2, :], ALU.mult))

            norm_root(0)

            dve.wait_ge(cond_hi, 1)
            dve.tensor_tensor(cond_h[:, :, 9:18], cond_t[:, :, :], cond_h[:, :, 0:9].bitcast(F32), ALU.subtract).then_inc(cond_lo, 1)

            def mod_add(b, block_at, value):
                dve.wait_ge(mod_turned, value)
                dve.tensor_tensor(mod_t[:, block_at, :], bank[2 + b][:, 0:36].rearrange("p (q c) -> p q c", c=9),
                                  vec_t[:, block_at].unsqueeze(2).to_broadcast([P, 4, 9]), ALU.add).then_inc(mod_ready, 1)

            for t in range(ADA_BLOCKS):
                mod_add(t % 2, slice(4 * t, 4 * t + 4), t + 1)

            def mod_pair(i, bk):
                n = ada_tile(i) // 2
                at = slice(4 * ADA_BLOCKS + 2 * n, 4 * ADA_BLOCKS + 2 * n + 2)
                turned = bk[:, 0:36].rearrange("p (u c) -> p u c", u=2)
                dve.wait_ge(mod_turned, ADA_BLOCKS + n + 1)
                link(dve.tensor_tensor(mod_t[:, at, :], turned[:, :, 0:9], vec_t[:, at].unsqueeze(2).to_broadcast([P, 2, 9]), ALU.add))
                dve.tensor_tensor(mod_t[:, at, :], mod_t[:, at, :], turned[:, :, 9:18], ALU.add).then_inc(mod_ready, 1)

            def norm_apply(n):
                shift, scale = 24 * n, 24 * n + 8
                dve.wait_ge(mod_ready, ADA_BLOCKS + 12 * n)
                link(dve.tensor_scalar(amul[:, :, :], mod_t[:, scale:scale + NCH, :], 1.0, None, ALU.add))
                link(dve.tensor_tensor(amul[:, :, :], amul[:, :, :],
                                       vec_t[:, 48 + 8 * n:56 + 8 * n].unsqueeze(2).to_broadcast([P, NCH, 9]), ALU.mult))

                def rest(j):
                    dve.wait_ge(h_hi_ready, (NCH + 1) * n + j + 2)
                    dve.tensor_tensor(h_lo[:, j, 0:SEQ], nrm[:, j % 2, 0:SEQ], h_hi[:, j, 0:SEQ].bitcast(F32),
                                      ALU.subtract).then_inc(h_lo_ready, 1)

                link(dve.tensor_tensor(nsm[:, 0], x_t[:, :, SEQ:T], nbuf[:, 1, SEQ:T].unsqueeze(1).to_broadcast([P, NCH, NS]), ALU.mult))
                link(dve.tensor_tensor(nsm[:, 0], nsm[:, 0], amul[:, :, 1:9], ALU.mult))
                dve.tensor_tensor(nsm[:, 0], nsm[:, 0], mod_t[:, shift:shift + NCH, 1:9], ALU.add).then_inc(nf_ready, 1)
                dve.wait_ge(nf_ready, (NCH + 1) * n + 1)
                for j in range(NCH):
                    if j >= 2:
                        dve.wait_ge(h_lo_ready, (NCH + 1) * n + j)
                    link(dve.tensor_tensor(nrm[:, j % 2, 0:SEQ], x_t[:, j, 0:SEQ], nbuf[:, 1, 0:SEQ], ALU.mult))
                    dve.tensor_scalar(nrm[:, j % 2, 0:SEQ], nrm[:, j % 2, 0:SEQ], amul[:, j, 0:1],
                                      mod_t[:, shift + j, 0:1], ALU.mult, ALU.add).then_inc(nf_ready, 1)
                    if j == 0:
                        dve.wait_ge(h_hi_ready, (NCH + 1) * n + 1)
                        dve.tensor_tensor(h_lo[:, :, SEQ:T], nsm[:, 0], h_hi[:, :, SEQ:T].bitcast(F32), ALU.subtract).then_inc(h_lo_ready, 1)
                    else:
                        rest(j - 1)
                rest(NCH - 1)

            def rest_w(i):
                dve.wait_ge(hi_ready, i + 1)
                dve.tensor_tensor(w_lo[:, i % SPL], raw[:, i % RAW], w_hi[:, i % SPL].bitcast(F32), ALU.subtract).then_inc(lo_ready, 1)

            rest_w(0)
            rest_w(1)
            norm_apply(0)

            def index_sum(n):
                qb, h = 1 + n // H, n % H
                w = width(qb)
                dve.wait_ge(idx_relu, n + 1)
                out = sel[:, sel_at[qb]:sel_at[qb] + w]
                if h == 0:
                    ins = dve.tensor_scalar(out, rbuf[:, n % 2, 0:w], wi_tok[:, qb, h:h + 1], 0.0, ALU.mult, ALU.add)
                else:
                    dve.wait_ge(idx_sum, n)
                    ins = dve.scalar_tensor_tensor(out=out, in0=rbuf[:, n % 2, 0:w], scalar=wi_tok[:, qb, h:h + 1],
                                                   in1=out, op0=ALU.mult, op1=ALU.add)
                ins.then_inc(idx_sum, 1)

            def top_round(r):
                blocks = (1, 3) if r < 16 else (2,)
                views = [(sel[:, sel_at[qb]:sel_at[qb] + width(qb)], top8) for qb, top8 in zip(blocks, (m8, m8b))]
                dve.wait_ge(sel_ready, 3)
                done = steps[0]
                for blk, top8 in views:
                    dve.max(out=top8[:, :], in_=blk).then_inc(dve_self, 1)
                for n, (blk, top8) in enumerate(views):
                    dve.wait_ge(dve_self, done + n + 1)
                    dve.match_replace(out=blk, in_to_replace=top8[:, :], in_values=blk, imm_value=TAKEN).then_inc(dve_self, 1)
                steps[0] += 2 * len(views)
                dve.wait_ge(dve_self, steps[0])
                if r in (15, 31):
                    for (blk, _), qb in zip(views, blocks):
                        w = width(qb)
                        link(dve.tensor_scalar(blk, blk, TAKEN, 1.0, ALU.is_equal, ALU.subtract))
                        link(dve.scalar_tensor_tensor(out=blk, in0=blk, scalar=-MASK, in1=dist[:, SEQ - w:SEQ],
                                                      op0=ALU.mult, op1=ALU.add))

            def logits(U):
                p, hh, qb = U // 8, U // 4 % 2, U % 4
                m, c = pair_mixer(p)
                w = width(qb)
                out, s_bank = lg[:, U % 3, :], bank[4 + U % 2]
                mx, nm = stat[:, U % 8:U % 8 + 1], stat[:, 8 + U % 8:9 + U % 8]
                if U >= 3:
                    dve.wait_ge(pt_done, U - 2)
                if m == 1:
                    if U == 32:
                        dve.wait_ge(stored, 64)
                    src = sel[:, sel_at[qb]:sel_at[qb] + w] if qb else dist[:, SEQ - P:SEQ]
                    link(dve.tensor_scalar(abias[:, 0:w], src, SLOPES[2 * c + hh], None, ALU.mult))
                    dve.wait_ge(s_done, U + 1)
                    link(dve.tensor_tensor_reduce(out[:, 0:w], s_bank[:, 0:w], abias[:, 0:w], 1.0, TAKEN, ALU.add, ALU.max, mx))
                else:
                    dve.wait_ge(s_done, U + 1)
                    start = TAKEN
                    if qb:
                        link(dve.tensor_tensor_reduce(out[:, 0:w - P], s_bank[:, 0:w - P], fbc[:, p % 2, hh, 0:w - P], 1.0, TAKEN,
                                                      ALU.add, ALU.max, stat[:, 24:25]))
                        start = stat[:, 24:25]
                    link(dve.tensor_tensor_reduce(out[:, w - P:w], s_bank[:, w - P:w], fdiag[:, hh, w - P:w], 1.0, start,
                                                  ALU.add, ALU.max, mx))
                dve.tensor_scalar(nm, mx, -1.0, None, ALU.mult).then_inc(lg_ready, 1)

            def probs(U):
                w = width(U % 4)
                dve.wait_ge(e_ready, U + 1)
                link(dve.reciprocal(stat[:, 25:26], stat[:, 16 + U % 8:17 + U % 8]))
                dve.tensor_scalar(lg[:, U % 3, 0:w], lg[:, U % 3, 0:w], stat[:, 25:26], None, ALU.mult).then_inc(p_ready, 1)

            def mean_squares(p, kd):
                dve.wait_ge(tok_sq, 2 * p + kd + 1)
                link(dve.tensor_reduce(ms8[:, :], sq[:, :].rearrange("p (g d) -> p g d", d=HD), AX_X, ALU.add))
                dve.tensor_scalar(ms8[:, :], ms8[:, :], 1.0 / HD, EPS, ALU.mult, ALU.add).then_inc(ms_tok, 1)

            def normalize(p, kd):
                m = pair_mixer(p)[0]
                dve.wait_ge(rstd_tok, 2 * p + kd + 1)
                if p >= 1:
                    dve.wait_ge(back_done, 2 * (p - 1) + kd + 1)
                    if kd == 1:
                        dve.wait_ge(k_stored, 16 * p)
                out = tok[:, kd, :].rearrange("p (g d) -> p g d", d=HD)
                dve.tensor_tensor(out, bank[2][:, :].rearrange("p (g d) -> p g d", d=HD),
                                  rs8[:, :].unsqueeze(2).to_broadcast([P, 8, HD]), ALU.mult).then_inc(tok_read, 1)
                if kd == 1:
                    dve.wait_ge(tok_read, 2 * p + 2)
                    dve.tensor_tensor(out, out, gk_row[:, m, :].unsqueeze(1).to_broadcast([P, 8, HD]), ALU.mult).then_inc(tok_ready, 1)

            def rest_o(p):
                dve.wait_ge(o_hi_ready, p + 1)
                dve.tensor_tensor(o_lo[:, p, 0:SEQ], bank[7][:, :], o_hi[:, p, 0:SEQ].bitcast(F32), ALU.subtract).then_inc(o_lo_ready, 1)

            def padded_queries():
                dve.wait_ge(s_consts, 1)
                dve.tensor_copy(qzs[0:64, :, :, 0], z_s[0:64, 24:28, :].rearrange("p c b -> p b c"))
                dve.tensor_copy(qzs[64:128, :, :, 1], z_s[64:128, 24:28, :].rearrange("p c b -> p b c")).then_inc(qzs_ready, 1)
                dve.tensor_scalar(gq_row[:, :, :], gq_row[:, :, :], QK_SCALE, None, ALU.mult)
                dve.tensor_scalar(s8[:, 8, :], sm_tok_s[:, 64:64 + H], H ** -0.5, QK_SCALE, ALU.mult, ALU.mult).then_inc(wi_ready, 1)
                dve.wait_ge(wi_ready, 1)

            def index_sum_s():
                dve.wait_ge(side_read, 5)
                dve.wait_ge(wbc_landed, 16)
                link(dve.tensor_tensor(isr[:, :, :, :], isr[:, :, :, :], wbc[:, :, :].unsqueeze(2).to_broadcast([P, NS, NPAGE, H]), ALU.mult))
                dve.tensor_reduce(iss[:, :, :], isr[:, :, :, :], AX_X, ALU.add).then_inc(is_sum, 1)

            def heads(row):
                return row.rearrange("p (g d) -> p g d", d=HD)

            def sample_square(n):
                row = [ts_b, ts_a][n // 2][:, n % 2, :]
                dve.wait_ge(side_read, [7, 8, 11, 12][n])
                if n == 0:
                    dve.wait_ge(lg_ready, 8 * 4)
                link(dve.tensor_tensor(sqs[:, :], row, row, ALU.mult))
                link(dve.tensor_reduce(s8[:, n, :], heads(sqs[:, :]), AX_X, ALU.add))
                dve.tensor_scalar(s8[:, n, :], s8[:, n, :], 1.0 / HD, EPS, ALU.mult, ALU.add).then_inc(ts_ms, 1)

            def sample_norm(n):
                m = n // 2
                dve.wait_ge(ts_rs, n + 1)
                view = heads([ts_b, ts_a][m][:, n % 2, :])
                gain = (gk_row[0:NS, m, :] if n % 2 else gq_row[:, m, :]).unsqueeze(1).to_broadcast([NS, H, HD])
                link(dve.tensor_tensor(view, view, s8[:, 4 + n, :].unsqueeze(2).to_broadcast([NS, H, HD]), ALU.mult))
                dve.tensor_tensor(view, view, gain, ALU.mult).then_inc(ts_norm, 1)

            def own_key(m):
                ts = [ts_b, ts_a][m]
                dve.wait_ge(ts_norm, 2 * m + 2)
                link(dve.tensor_tensor(sqs[:, :], ts[:, 0, :], ts[:, 1, :], ALU.mult))
                link(dve.tensor_reduce(s8[:, 9 + m, :], heads(sqs[:, :]), AX_X, ALU.add))

            def own_index():
                dve.wait_ge(side_read, 9)
                link(dve.tensor_tensor(heads(sqs[:, :]), heads(ts_b[:, 3, :]), sm_tok_s[:, 0:HD].unsqueeze(1).to_broadcast([NS, H, HD]), ALU.mult))
                link(dve.tensor_reduce(s8[:, 11, :], heads(sqs[:, :]), AX_X, ALU.add))
                link(dve.scalar_tensor_tensor(out=s8[:, 11, :], in0=s8[:, 11, :], scalar=0.0, in1=s8[:, 8, :],
                                              op0=ALU.max, op1=ALU.mult))
                link(dve.tensor_reduce(srow[:, PAST:L], s8[:, 11, :], AX_X, ALU.add))

            def top_s(rounds, last):
                for _ in range(rounds):
                    link(dve.max(out=m8[0:NS, :], in_=srow[:, :]))
                    link(dve.match_replace(out=srow[:, :], in_to_replace=m8[0:NS, :], in_values=srow[:, :], imm_value=TAKEN))
                if last:
                    dve.wait_ge(s_consts, 2)
                    link(dve.tensor_scalar(srow[:, :], srow[:, :], TAKEN, 1.0, ALU.is_equal, ALU.subtract))
                    dve.scalar_tensor_tensor(out=srow[:, :], in0=srow[:, :], scalar=-MASK, in1=dist_s[:, :],
                                             op0=ALU.mult, op1=ALU.add).then_inc(dist_ready, 1)

            SAMPLE_STEPS = {
                (1, 6): padded_queries,
                (4, 0): index_sum_s,
                (5, 7): lambda: sample_square(0), (6, 0): lambda: sample_norm(0),
                (6, 1): lambda: sample_square(1), (6, 2): lambda: sample_norm(1),
                (6, 3): lambda: own_key(0), (7, 0): own_index,
                **{(7, s): lambda: top_s(1, False) for s in range(1, 8)}, (8, 0): lambda: top_s(1, True),
                (8, 3): lambda: sample_square(2), (8, 4): lambda: sample_norm(2),
                (8, 5): lambda: sample_square(3), (8, 6): lambda: sample_norm(3), (8, 7): lambda: own_key(1),
            }

            rows = slice(ROW_FL, ROW_FL + H)
            dve.wait_ge(act_evac, 2)
            dve.tensor_copy(ki2[0:64, :], zsm[0:64, 0:SEQ])
            dve.tensor_copy(ki2[64:128, :], zsm[0:64, 0:SEQ])
            link(dve.tensor_scalar(lf[rows, 0, :], zsm[rows, :], bforget[rows, 0:1], None, ALU.add))
            link(dve.tensor_scalar(lf[rows, 1, :], lf[rows, 0, :], -1.0, None, ALU.mult))
            dve.tensor_tensor(lf[rows, 1, :], lf[rows, 1, :], lf[rows, 0, :], ALU.max).then_inc(sm_ready, 1)
            rest_w(2)
            rest_w(3)
            dve.wait_ge(lf_step, 1)
            dve.scalar_tensor_tensor(out=zsm[rows, :], in0=lf[rows, 0, :], scalar=0.0, in1=lf[rows, 3, :],
                                     op0=ALU.min, op1=ALU.subtract).then_inc(sm_ready, 2)
            dve.wait_ge(sm_ready, 3)
            link(dve.tensor_scalar(lf[rows, 0, :], zsm[rows, :], -1.0, None, ALU.mult))
            dve.tensor_tensor_scan(lf[rows, 1, 0:SEQ], ones[rows, 0:1].to_broadcast([H, SEQ]), lf[rows, 0, 0:SEQ], 0.0,
                                   ALU.mult, ALU.add).then_inc(negf_ready, 1)
            rest_w(4)
            dve.wait_ge(smt_ready, 1)
            dve.tensor_scalar(wi_tok[:, :, :], abias[:, :].rearrange("p (t c) -> p t c", t=QB)[:, :, 64:64 + H],
                              H ** -0.5, QK_SCALE, ALU.mult, ALU.mult).then_inc(sm_ready, 1)
            dve.wait_ge(sm_ready, 4)
            rest_w(5)
            rest_w(6)

            for p, s in ITERATIONS:
                U = SLOTS * (p - 1) + s
                if p == 0:
                    for n in range(3 * s, 3 * s + 3):
                        index_sum(n)
                if 1 <= p <= 4 and s == 0:
                    dve.wait_ge(fbc_landed[(p - 1) % 2], 32 * ((p - 1) // 2 + 1))
                    for hh in range(2):
                        link(dve.tensor_tensor(fdiag[:, hh, :].rearrange("p (t c) -> p t c", t=QB),
                                               fbc[:, (p - 1) % 2, hh, :].rearrange("p (t c) -> p t c", t=QB),
                                               cmask[:, :].unsqueeze(1).to_broadcast([P, QB, P]), ALU.add))
                if 0 <= U - 1 < N_UNITS:
                    probs(U - 1)
                if 0 <= U < N_UNITS:
                    logits(U)
                if s == 3 and p >= 2:
                    rest_o(p - 2)
                if p < N_PAIRS:
                    if s in (2, 4):
                        mean_squares(p, s // 2 - 1)
                    if s in (3, 5):
                        normalize(p, s // 2 - 1)
                if slot_before(p, s) in ADA_SECOND:
                    mod_pair(ADA_SECOND[slot_before(p, s)], bank[1])
                if 0 <= U < 32:
                    top_round(U)
                if (p, s) in SAMPLE_STEPS:
                    SAMPLE_STEPS[p, s]()
            def sample_keys(n):
                m, b = n // NS, n % NS
                if n % 2 == 0:
                    dve.wait_ge(kv_landed[0], kv_value(n))
                    if n >= 2:
                        dve.wait_ge(prod_used, n - 1)
                    dve.tensor_tensor(prod0[:, :, :], kv0[:, :, :], qbc0[:, :].unsqueeze(1).to_broadcast([P, NPAGE, SEQ]), ALU.mult)\
                        .then_inc(prod_dve, 1)
                dve.wait_ge([prod_dve, prod_pool][n % 2], n // 2 + 1)
                dve.tensor_reduce(lgs[:, m, :, H * b:H * b + H], prod[n % 2][:, :, :].rearrange("p g (h d) -> p g h d", d=HD), AX_X, ALU.add)\
                    .then_inc(prod_used, 1)

            def rows_logits():
                dve.wait_ge(rows_turned, 1)
                own = bank[7][0:64, 0:24]
                for j in range(3):
                    link(dve.tensor_tensor_reduce(pself[:, 0, :], own[:, 8 * j:8 * j + 8], pick[:, :], 1.0, 0.0, ALU.mult, ALU.add,
                                                  col64[:, 8 + j:9 + j]))
                link(dve.tensor_tensor_reduce(pself[:, 0, :], slope_rows[:, :], pick[:, :], 1.0, 0.0, ALU.mult, ALU.add, col64[:, 11:12]))
                dve.tensor_copy(rows_f[:, 0:PAST], bank[7][0:64, P:P + PAST])
                link(dve.tensor_copy(rows_f[:, PAST:L], col64[:, 10:11]))
                link(dve.tensor_tensor_scan(rows_l[:, 0, :], ones[0:64, 0:1].to_broadcast([64, L]), rows_f[:, :], 0.0, ALU.mult, ALU.add))
                dve.tensor_tensor(rows_f[:, 0:PAST], bank[2][0:64, 0:PAST], rows_l[:, 0, 0:PAST], ALU.subtract)
                link(dve.tensor_tensor(rows_f[:, PAST:L], col64[:, 8:9], rows_l[:, 0, PAST:L], ALU.subtract))
                dve.tensor_copy(rows_l[:, 0, :], rows_f[:, :])
                link(dve.tensor_reduce(col64[:, 0:1], rows_f[:, :], AX_X, ALU.max))
                dve.tensor_scalar(col64[:, 2:3], col64[:, 0:1], -1.0, None, ALU.mult).then_inc(rows_lg, 1)
                dve.wait_ge(dist_spread, 1)
                dve.tensor_copy(rows_f[:, 0:PAST], bank[3][0:64, 0:PAST])
                link(dve.tensor_copy(rows_f[:, PAST:L], col64[:, 9:10]))
                link(dve.scalar_tensor_tensor(out=rows_l[:, 1, :], in0=bank[6][0:64, 0:L], scalar=col64[:, 11:12], in1=rows_f[:, :],
                                              op0=ALU.mult, op1=ALU.add))
                link(dve.tensor_reduce(col64[:, 1:2], rows_l[:, 1, :], AX_X, ALU.max))
                dve.tensor_scalar(col64[:, 3:4], col64[:, 1:2], -1.0, None, ALU.mult).then_inc(rows_lg, 1)

            def rows_probs():
                for m in range(2):
                    dve.wait_ge(rows_e, m + 1)
                    link(dve.reciprocal(col64[:, 6 + m:7 + m], col64[:, 4 + m:5 + m]))
                    dve.tensor_scalar(rows_l[:, m, :], rows_l[:, m, :], col64[:, 6 + m:7 + m], None, ALU.mult).then_inc(rows_p, 1)
                    dve.wait_ge(rows_p, m + 1)
                    last = dve.tensor_scalar(pself[:, m, :], pick[:, :], rows_l[:, m, PAST:L], None, ALU.mult)
                last.then_inc(rows_p, 1)

            def own_value(m):
                row = heads([ts_b, ts_a][m][:, 2, :])
                if m == 0:
                    dve.wait_ge(pts_ready, 2)
                    dve.wait_ge(stored, 16 * 8)
                dve.tensor_tensor(row, row, s8[:, 6 + m, :].unsqueeze(2).to_broadcast([NS, H, HD]), ALU.mult)

            def own_features(m):
                dve.wait_ge(pv_used, NS * (m + 1))
                dve.tensor_tensor(heads(om[:, m, :]), heads(bank[2 + m][0:64, :]), pick[:, :].unsqueeze(2).to_broadcast([64, H, HD]), ALU.mult)\
                    .then_inc(om_ready, 1)

            dve.wait_ge(lo_ready, T_GATE + 5)
            n = 0
            for i in range(T_GATE + 3, T_WO):
                for _ in range(KEYS_AT[i - T_GATE - 3] if i - T_GATE - 3 < len(KEYS_AT) else 0):
                    sample_keys(n)
                    n += 1
                if i == T_GATE + 10:
                    rows_logits()
                if i == T_GATE + 11:
                    rows_probs()
                if i == T_GATE + 13:
                    own_value(0)
                    own_value(1)
                rest_w(i + 2)
            for m in range(2):
                own_features(m)
            dve.wait_ge(os_hi, 1)
            dve.tensor_tensor(o_lo[:, :, SEQ:T], bank[6][:, 256:256 + 8 * NS].rearrange("p (c b) -> p c b", b=NS),
                              o_hi[:, :, SEQ:T].bitcast(F32), ALU.subtract).then_inc(os_lo, 1)

            for i in range(T_WO, T_ADA):
                m = i - T_WO
                rest_w(i + 2)
                dve.wait_ge(gates_ready, 2 * m + 2)
                for half in range(2):
                    cols = slice(half * HALF, (half + 1) * HALF)
                    b = half + 4 * par(i)
                    dve.wait_ge(proj_done, 2 * i + half + 1)
                    dve.tensor_tensor(mix[:, half, 0, :], bank[b + 2][:, 0:HALF], gate[:, 2 * m, cols], ALU.mult)
                    dve.tensor_tensor(mix[:, half, 1, :], bank[b][:, 0:HALF], gate[:, 2 * m + 1, cols], ALU.mult).then_inc(dve_evac, 1)
                    dve.wait_ge(dve_evac, 2 * m + half + 1)
                    dve.tensor_tensor(mix[:, half, 2, :], mix[:, half, 0, :], mix[:, half, 1, :], ALU.add).then_inc(mf_ready, 1)
                for half in range(2):
                    cols = slice(half * HALF, (half + 1) * HALF)
                    dve.wait_ge(mf_hi, 2 * m + half + 1)
                    dve.tensor_tensor(h_lo[:, m, cols], mix[:, half, 2, :], h_hi[:, m, cols].bitcast(F32), ALU.subtract).then_inc(mf_lo, 1)

            def add_gated(bk, half, m, vec, done):
                n = HALF if half == 0 else SEQ - HALF
                xs = x_t[:, m, half * HALF:half * HALF + n]
                g = mod_t[:, vec, :]
                if half:
                    dve.wait_ge(dve_evac, done * 2 + (2 * NCH + 1))
                    dve.tensor_tensor(xs8[:, 0:1, :], bk[:, n:HALF].unsqueeze(1), g[:, :, 1:9], ALU.mult).then_inc(xs_ready, 1)
                last = dve.scalar_tensor_tensor(out=xs, in0=bk[:, 0:n].unsqueeze(1), scalar=g[:, 0, 0:1], in1=xs,
                                                op0=ALU.mult, op1=ALU.add)
                if half:
                    dve.wait_ge(xs_ready, done + 1)
                    last = dve.tensor_tensor(x_t[:, m, SEQ:T], x_t[:, m, SEQ:T], xs8[:, 0:1, :], ALU.add)
                last.then_inc(dve_evac, 1)

            for i in range(T_ADA, T_OUT):
                rest_w(i + 2)
                if ada_tile(i) % 2:
                    mod_pair(i, bank[5])
            dve.wait_ge(mod_ready, ADA_BLOCKS + 16)
            for i in range(T_OUT, T_MLP):
                m = i - T_OUT
                rest_w(i + 2)
                for half in range(2):
                    dve.wait_ge(proj_done, 2 * i + half + 1)
                    add_gated(bank[half + 4 * par(i)], half, slice(m, m + 1), slice(16 + m, 17 + m), m)
            norm_root(1)
            norm_apply(1)

            def rest_loop(i, it):
                dve.wait_ge(hi_ready, it * 4 + (i + 1))
                dve.tensor_tensor(w_lo[:, i % SPL], raw[:, i % RAW], w_hi[:, i % SPL].bitcast(F32), ALU.subtract).then_inc(lo_ready, 1)

            for q in range(2):
                with dve.Fori(0, 4) as it:
                    for b in range(4):
                        n = 32 * q + 2 * b
                        for half in range(2):
                            uf = u_f[:, 2 * (b % 2) + half, :]
                            dve.wait_ge(act_evac, it * 8 + (2 * (T_WO + T_OUT - T_ADA) + n + half + 1))
                            dve.tensor_tensor(uf, uf, uf, ALU.mult).then_inc(u_sq, 1)
                        rest_loop(T_MLP + 32 * q + b + 2, it)
                        for half in range(2):
                            slot = 2 * (b % 2) + half
                            cols = slice(half * HALF, (half + 1) * HALF)
                            dve.wait_ge(u_hi_ready, it * 8 + (n + half + 1))
                            dve.tensor_tensor(u_lo[:, bass.ds(it * 4 + b, 1), cols], u_f[:, slot:slot + 1, :],
                                              u_hi[:, bass.ds(it * 4 + b, 1), cols].bitcast(F32), ALU.subtract).then_inc(u_lo_ready, 1)

                def down_pair(it, mb, split):
                    for kg in range(2):
                        if split:
                            rest_loop(T_MLP + 32 * q + 16 + 2 * mb + kg + 2, it)
                    for half in range(2):
                        dve.wait_ge(proj_done, it * 8 + (2 * (T_MLP + 32 * q + 16 + 2 * mb + 1) + half + 1))
                        add_gated(bank[2 + half + 4 * mb], half, bass.ds(it * 2 + mb, 1), bass.ds(it * 2 + (40 + mb), 1),
                                  it * 2 + (8 + 8 * q + mb))

                with dve.Fori(0, 3 if q else 4) as it:
                    for mb in range(2):
                        down_pair(it, mb, True)
                if q:
                    for mb in range(2):
                        down_pair(3, mb, mb == 0)
            for j in range(1, NCH, 2):
                dve.wait_ge(y_done, j + 1)
                dve.tensor_copy(y_tok[:, :, j * P:(j + 1) * P], bank[j % 4][:, :].rearrange("p (t c) -> p t c", t=QB)).then_inc(y_dve, 1)


_OUTS = [("y_p", (1, SEQ, DM)), ("y_s", (NS, 1, DM))] + [
    (name + group, (1, *lead, *shape)) for group, lead in (("_p", (1, SEQ)), ("_s", (NS, 1)))
    for name, shape in (("k_a", (H, HD)), ("v_a", (H, HD)), ("k_idx", (HD,)), ("k_b", (H, HD)), ("v_b", (H, HD)), ("logf", (H,)))]


def kernel(**inputs):
    import numpy as _np
    import concourse.bacc as _bacc
    from concourse import mybir as _mybir
    from concourse.bass_utils import run_bass_kernel_spmd as _run

    nc = _bacc.Bacc("TRN2", target_bir_lowering=False, num_devices=1)
    arrays, aps = {}, {}
    for name, value in inputs.items():
        v = _np.ascontiguousarray(value)
        arrays[f"in_{name}"] = v
        aps[name] = nc.dram_tensor(f"in_{name}", v.shape, _mybir.dt.from_np(v.dtype), kind="ExternalInput").ap()
    for name, shape in _OUTS:
        aps[name] = nc.dram_tensor(f"out_{name}", shape, F32, kind="ExternalOutput").ap()
    layer(nc, aps)
    r = _run(nc, [arrays], core_ids=[0])
    return tuple(r.results[0][f"out_{name}"] for name, _ in _OUTS)
```

```python
from contextlib import ExitStack

import numpy as np

import concourse.bass as bass
from concourse import mybir

ALU = mybir.AluOpType
ACT = mybir.ActivationFunctionType
F32 = mybir.dt.float32
F32R = mybir.dt.float32r
I32 = mybir.dt.int32
AX_X = mybir.AxisListType.X

P = 128
DM = 1024
SEQ = 512
NS = 8
T = SEQ + NS
HALF = T // 2
H = 8
HD = 64
NCH = DM // P
QB = SEQ // P
PAGE = 128
NPAGE = 2
PAST = PAGE * NPAGE
L = PAST + 1
TOPK_P = 128
TOPK_S = L // 4
EPS = 1e-6
MASK = -1e30
TAKEN = -3e38
QK_SCALE = HD ** -0.5
SLOPES = [2.0 ** (-8.0 * (h + 1) / H) for h in range(H)]

QA, KA, VA, QBC, KBC, VBC, QI, KI, WI, FL, GA, GB = np.cumsum(
    [0, 512, 512, 512, 512, 512, 512, 512, 64, 8, 8, 1024]).tolist()

N_PAIRS = 8
T_SMALL, T_QI = 0, 1
T_PAIR = T_QI + 4
SLOTS = 8
HALVES_AT = [0, 1, 2, 3, 4, 6]
T_GATE = T_PAIR + 3 * N_PAIRS
T_WO = T_GATE + 2 * NCH
GROUP = 3
T_MLP = T_WO + 2 * NCH * GROUP
RAW = 4
SPL = 2
ADA_BLOCKS = 4
ROW_FL = 96
SIDE = [(1, 6), (1, 7), (2, 6), (2, 7),
        (3, 6), (4, 7),
        (5, 6), (5, 7), (6, 6), (6, 7),
        (8, 1), (8, 2), (8, 3)]
KEYS_AT = [0, 2, 3, 3, 2, 3, 3]
VALUES_AT = {15: 2 * NS}


def pair_mixer(p):
    return p // 4, p % 4


def ada_pair(i):
    return (i - T_WO) // GROUP, (i - T_WO) % GROUP - 1


def is_ada(i):
    return T_WO <= i < T_MLP and (i - T_WO) % GROUP > 0


def split_slot(i):
    if T_WO <= i < T_MLP and (i - T_WO) % 4 >= SPL:
        return (i - T_WO) % 4
    return i % SPL


def slot_before(p, s):
    return (p, s - 1) if s else (p - 1, SLOTS - 1)


def split_at(p, s):
    q, t = slot_before(p, s)
    return [T_PAIR + 3 * q + HALVES_AT.index(t) // 2 + SPL] if 0 <= q <= N_PAIRS + 1 and t in HALVES_AT[1::2] else []


def loads_at(p, s):
    return ([T_PAIR + 1 + RAW] if (p, s) == (0, 0) else []) + [i + RAW for i in split_at(p, s)]


def dma_count(i):
    if i == T_SMALL:
        return 3
    return 2 if T_WO <= i < T_WO + NCH * GROUP and not is_ada(i) else 1


def unit_tile(n, slots):
    for tile, count in slots:
        if n < count:
            return tile
        n -= count


def landed_value(i):
    return 16 * sum(dma_count(j) for j in range(i % RAW, i + 1, RAW))


def par(i):
    if i < T_GATE + 4:
        return int(i == T_QI)
    return i % 2


def act_evac_value(i, half):
    return 2 * i + half + 1


def layer(nc, a):
    ctx = ExitStack()
    with ctx:
        def sem(name):
            return ctx.enter_context(nc.semaphore(name))

        place = {"at": nc.sbuf_base + 32}
        place["at"] -= place["at"] % 32

        def sb(name, shape, dt=F32, at=None):
            size = int(np.prod(shape[1:])) * 4
            size += -size % 32
            if at is None:
                at = place["at"]
                place["at"] += size
            return nc.alloc_sbuf_tensor_at(name, list(shape), dt, offset=at), at, at + size

        def new(name, shape, dt=F32):
            return sb(name, shape, dt)[0]

        ident = new("ident", [P, P])
        ones = new("ones", [P, P])
        dist = new("dist", [P, SEQ])
        cmask = new("cmask", [P, P])
        vec_t = new("vec_t", [P, 64])
        mod_t = new("mod_t", [P, 48, 9])
        amul = new("amul", [P, NCH, 9])
        cond_h = new("cond_h", [P, NCH, 18], F32R)
        g_col = new("g_col", [P, 2])
        gq = new("gq", [P, 2])
        gk_row = new("gk_row", [P, 2, HD])
        bforget = new("bforget", [P, 1])
        wi_tok = new("wi_tok", [P, QB, H])
        stat = new("stat", [P, 40])
        m8, m8_at, _ = sb("m8", [P, 8])
        xs8 = sb("xs8", [P, 1, NS], F32, m8_at)[0]
        m8b = new("m8b", [P, 8])
        ms8 = new("ms8", [P, 8])
        rs8 = new("rs8", [P, 8])
        neghalf = new("neghalf", [P, 8])
        sm_tok_s = new("sm_tok_s", [NS, P])
        page_row = new("page_row", [1, NS * NPAGE], I32)

        x_t = new("x_t", [P, NCH, T])
        raw = new("raw", [P, RAW, NCH, P])
        w_hi = new("w_hi", [P, SPL, NCH, P], F32R)
        w_lo = new("w_lo", [P, SPL, NCH, P], F32R)
        h_hi = new("h_hi", [P, NCH, T], F32R)
        h_lo = new("h_lo", [P, NCH, T], F32R)
        o_at = place["at"]
        o_hi = new("o_hi", [P, 8, T], F32R)
        o_lo = new("o_lo", [P, 8, T], F32R)
        z_s = new("z_s", [P, 29, NS])

        base = place["at"]
        rbuf = new("rbuf", [P, 2, SEQ])
        sq = new("sq", [P, SEQ])
        tok = new("tok", [P, 2, SEQ])
        z = new("z", [P, 3, SEQ])
        q_pad = new("q_pad", [P, 2, 2, SEQ])
        k_fm = new("k_fm", [P, 2, SEQ])
        v_tok = new("v_tok", [P, 2, QB, P])
        ki2 = new("ki2", [P, SEQ])
        sel = new("sel", [P, 1152])
        fbc_at = place["at"]
        fbc = new("fbc", [P, 2, 2, SEQ])
        fd_at = place["at"]
        fdiag = new("fdiag", [P, 2, SEQ])
        lg_at = place["at"]
        lg = new("lg", [P, 3, SEQ])
        abias = new("abias", [P, SEQ])
        pt_at = place["at"]
        p_t = new("p_t", [P, 2, QB, SEQ])
        ts_b = new("ts_b", [NS, 4, SEQ])
        s8 = new("s8", [NS, 12, H])
        gq_row = new("gq_row", [NS, 2, HD])
        spread = new("spread", [NS, 64])
        gather = new("gather", [64, NS])
        pick = new("pick", [64, H])
        slope_rows = new("slope_rows", [64, H])
        col64 = new("col64", [64, 16])
        wbc = new("wbc", [P, NS, H])
        qzs = new("qzs", [P, NS, 4, 2])
        lfp = new("lfp", [P, NPAGE, NS * H])
        srow = new("srow", [NS, L])
        assert place["at"] <= nc.sbuf_usable_end, (place["at"], nc.sbuf_usable_end)
        q_idx = sb("q_idx", [P, H, SEQ], F32, pt_at)[0]
        ki_pg = sb("ki_pg", [P, NS * NPAGE, 2, HD], F32, o_at + 4 * T * 4)[0]
        ki_pt = sb("ki_pt", [P, NS * NPAGE, P], F32, o_at + 12 * T * 4)[0]
        isr, _, iss_at = sb("isr", [P, NS, NPAGE, H], F32, o_at + 4 * T * 4)
        iss = sb("iss", [P, NS, NPAGE], F32, iss_at)[0]
        ts_a, _, kv0_at = sb("ts_a", [NS, 3, SEQ], F32, fbc_at)
        kv0, _, dist_at = sb("kv0", [P, NPAGE, SEQ], F32, kv0_at)
        mod_row2 = sb("mod_row2", [18, 2, 2 * P], F32, kv0_at + 4 * SEQ)[0]
        sqs = sb("sqs", [NS, SEQ], F32, kv0_at)[0]
        dist_s, _, at = sb("dist_s", [NS, L], F32, dist_at)
        assert at <= lg_at

        gate, _, rows_at = sb("gate", [P, 2 * NCH, T], F32, base)
        kv1, _, at = sb("kv1", [P, NPAGE, SEQ], F32, lg_at)
        prod0, _, at = sb("prod0", [P, NPAGE, SEQ], F32, at)
        prod1, _, at = sb("prod1", [P, NPAGE, SEQ], F32, at)
        ptz, _, at = sb("ptz", [P, 2 * NPAGE, 9 * NS * H], F32, at)
        qbc1, _, at = sb("qbc1", [P, SEQ], F32, at)
        lgs, _, at = sb("lgs", [P, 2, NPAGE, NS * H], F32, at)
        assert at <= pt_at + 4 * 4096, (at, pt_at)
        rows_l, _, at = sb("rows_l", [64, 2, L], F32, rows_at)
        rows_f, _, at = sb("rows_f", [64, L], F32, at)
        pself, _, at = sb("pself", [64, 2, H], F32, at)
        qbc0, _, at = sb("qbc0", [P, SEQ], F32, at)
        assert at <= fbc_at
        kv, prod, qbc = [kv0, kv1], [prod0, prod1], [qbc0, qbc1]
        vbuf = kv + prod
        om, _, at = sb("om", [64, 2, SEQ], F32, kv0_at)
        mix, _, at = sb("mix", [P, 2, 3, HALF], F32, at)
        w_hi2, _, at = sb("w_hi2", [P, SPL, NCH, P], F32R, at)
        w_lo2, _, at = sb("w_lo2", [P, SPL, NCH, P], F32R, at)
        assert at <= pt_at + 4 * 4096
        u_hi, _, at2 = sb("u_hi", [P, 16, T], F32R, o_at)
        u_lo, _, at2 = sb("u_lo", [P, 16, T], F32R, at2)
        u_f, _, at2 = sb("u_f", [P, 4, HALF], F32, at2)
        y_tok, _, at2 = sb("y_tok", [P, QB, DM], F32, at2)
        y_stok, _, at2 = sb("y_stok", [NS, DM], F32, at2)
        assert at2 <= nc.sbuf_usable_end, (at2, nc.sbuf_usable_end)
        x_tok, _, e1 = sb("x_tok", [P, QB, DM], F32, base)
        x_stok, _, e1 = sb("x_stok", [NS, DM], F32, e1)
        cond, _, e1 = sb("cond", [9, DM], F32, e1)
        vec_rows, _, e1 = sb("vec_rows", [64, P], F32, e1)
        sig, _, e1 = sb("sig", [P, NCH * 9], F32, e1)
        nbuf, _, e1 = sb("nbuf", [P, 4, T], F32, e1)
        nrm, _, e1 = sb("nrm", [P, 2, T], F32, e1)
        nsm, _, e1 = sb("nsm", [P, 2, NCH, NS], F32, e1)
        mod_row, _, e1 = sb("mod_row", [9, 2, SEQ], F32, e1)
        cond_t, _, e1 = sb("cond_t", [P, NCH, 9], F32, e1)
        ada, _, e1 = sb("ada", [P, 2, NCH, SEQ], F32, o_at)
        assert e1 <= nc.sbuf_usable_end
        del e1
        zsm, _, e2 = sb("zsm", [P, T], F32, base)
        assert e2 <= base + 4096
        lf, _, e2 = sb("lf", [P, 4, T], F32, fd_at)
        assert e2 <= fd_at + 5 * 4 * SEQ

        bank = [ctx.enter_context(nc.psum_tensor(f"bank{i}", [P, SEQ], F32)) for i in range(8)]

        negf_d = nc.dram_tensor("negf_d", (H, SEQ), F32).ap()
        q_d = nc.dram_tensor("q_d", (2, NS, SEQ), F32).ap()
        wi_d = nc.dram_tensor("wi_d", (NS, H), F32).ap()

        small_landed = sem("small_landed")
        x_landed = sem("x_landed")
        ada_landed = [sem("ada_landed0"), sem("ada_landed1")]
        raw_landed = [sem(f"raw_landed{i}") for i in range(RAW)]
        fbc_landed = [sem("fbc_landed0"), sem("fbc_landed1")]
        consts = sem("consts")
        zeroed = sem("zeroed")
        vec_done = sem("vec_done")
        vec_ready = sem("vec_ready")
        cond_ready = sem("cond_ready")
        xt_done = sem("xt_done")
        xt_act = sem("xt_act")
        xt_dve = sem("xt_dve")
        sq_ready = sem("sq_ready")
        sq_used = sem("sq_used")
        ms_ready = sem("ms_ready")
        rs_ready = sem("rs_ready")
        cond_hi = sem("cond_hi")
        cond_lo = sem("cond_lo")
        mod_done = sem("mod_done")
        mod_row_ready = sem("mod_row_ready")
        mod_turned = sem("mod_turned")
        mod_ready = sem("mod_ready")
        nf_ready = sem("nf_ready")
        h_hi_ready = sem("h_hi_ready")
        h_lo_ready = sem("h_lo_ready")
        hi_ready = sem("hi_ready")
        lo_ready = sem("lo_ready")
        proj_done = sem("proj_done")
        act_evac = sem("act_evac")
        xs_ready = sem("xs_ready")
        dve_evac = sem("dve_evac")
        tok_done = sem("tok_done")
        tok_sq = sem("tok_sq")
        ms_tok = sem("ms_tok")
        rstd_tok = sem("rstd_tok")
        tok_ready = sem("tok_ready")
        tok_read = sem("tok_read")
        v_ready = sem("v_ready")
        back_done = sem("back_done")
        back_read = sem("back_read")
        s_done = sem("s_done")
        lg_ready = sem("lg_ready")
        e_ready = sem("e_ready")
        p_ready = sem("p_ready")
        pt_done = sem("pt_done")
        pt_ready = sem("pt_ready")
        pv_done = sem("pv_done")
        o_hi_ready = sem("o_hi_ready")
        o_lo_ready = sem("o_lo_ready")
        idx_done = sem("idx_done")
        idx_relu = sem("idx_relu")
        idx_sum = sem("idx_sum")
        sel_ready = sem("sel_ready")
        sm_ready = sem("sm_ready")
        lf_step = sem("lf_step")
        smt_done = sem("smt_done")
        smt_ready = sem("smt_ready")
        negf_ready = sem("negf_ready")
        negf_stored = sem("negf_stored")
        pages_landed = sem("pages_landed")
        side_done = sem("side_done")
        side_read = sem("side_read")
        qzs_ready = sem("qzs_ready")
        wi_ready = sem("wi_ready")
        is_sum = sem("is_sum")
        ts_ms = sem("ts_ms")
        ts_rs = sem("ts_rs")
        ts_norm = sem("ts_norm")
        own_done = sem("own_done")
        wi_stored = sem("wi_stored")
        q_stored = sem("q_stored")
        wbc_landed = sem("wbc_landed")
        s_consts = sem("s_consts")
        kip_landed = sem("kip_landed")
        lfp_landed = sem("lfp_landed")
        dist_ready = sem("dist_ready")
        dist_spread = sem("dist_spread")
        kv_landed = [sem("kv_landed0"), sem("kv_landed1")]
        val_landed = [sem(f"val_landed{i}") for i in range(4)]
        prod_pool = sem("prod_pool")
        prod_dve = sem("prod_dve")
        prod_used = sem("prod_used")
        pv_used = sem("pv_used")
        rows_turned = sem("rows_turned")
        rows_lg = sem("rows_lg")
        rows_e = sem("rows_e")
        rows_p = sem("rows_p")
        pts_turned = sem("pts_turned")
        pts_ready = sem("pts_ready")
        om_ready = sem("om_ready")
        os_done = sem("os_done")
        os_hi = sem("os_hi")
        os_lo = sem("os_lo")
        gates_ready = sem("gates_ready")
        mf_ready = sem("mf_ready")
        mf_hi = sem("mf_hi")
        mf_lo = sem("mf_lo")
        u_sq = sem("u_sq")
        u_hi_ready = sem("u_hi_ready")
        u_lo_ready = sem("u_lo_ready")
        y_done = sem("y_done")
        y_act = sem("y_act")
        y_dve = sem("y_dve")
        act_self = sem("act_self")
        dve_self = sem("dve_self")
        pool_self = sem("pool_self")
        k_stored = sem("k_stored")
        v_stored = sem("v_stored")
        stored = sem("stored")

        w_in_v = a["w_in"][0].rearrange("(k p) n -> p k n", p=P)
        ada_v = a["w_ada"][0].rearrange("(k p) n -> p k n", p=P)

        def tile_dmas(i):
            dst = raw[:, i % RAW]
            if i == T_SMALL:
                return [(dst[:, :, 0:HD], w_in_v[:, :, KI:KI + HD]), (dst[:, :, 64:64 + H], w_in_v[:, :, WI:WI + H]),
                        (dst[:, :, ROW_FL:ROW_FL + H], w_in_v[:, :, FL:FL + H])]
            if i < T_PAIR:
                col = QI + (i - T_QI) * P
            elif i < T_GATE:
                m, c = pair_mixer((i - T_PAIR) // 3)
                col = [[QBC, KBC, VBC], [QA, KA, VA]][m][(i - T_PAIR) % 3] + c * P
            elif i < T_WO:
                j = i - T_GATE
                col = [GA, GB][j % 2] + j // 2 * P
            elif is_ada(i):
                g, half = ada_pair(i)
                col = ADA_BLOCKS * SEQ + g * 2 * P
                return [(dst.rearrange("p k c -> p (k c)").rearrange("p (k c) -> p k c", k=4),
                         ada_v[:, 4 * half:4 * half + 4, col:col + 2 * P])]
            else:
                m = (i - T_WO) // GROUP
                if m < NCH:
                    return [(dst[:, 0:4], wob_v[:, :, m * P:(m + 1) * P]), (dst[:, 4:8], woa_v[:, :, m * P:(m + 1) * P])]
                return [(dst, wout_v[:, :, (m - NCH) * P:(m - NCH + 1) * P])]
            return [(dst, w_in_v[:, :, col:col + P])]

        wob_v = a["w_o_b"][0].rearrange("(k p) n -> p k n", p=P)
        woa_v = a["w_o_a"][0].rearrange("(k p) n -> p k n", p=P)
        wout_v = a["w_out"][0].rearrange("(k p) n -> p k n", p=P)

        N_SMALL = 14
        n_pool = a["cache_k_a"].shape[1]
        wup_v = a["w_up"][0].rearrange("(k p) n -> p k n", p=P)
        wdn_v = a["w_down"][0].rearrange("(k p) n -> p k n", p=P)
        sel_at = [0, 0, 256, 640]

        def width(qb):
            return (qb + 1) * P

        ITERATIONS = [(p, s) for p in range(N_PAIRS + 1) for s in range(SLOTS)] + [(N_PAIRS + 1, s) for s in range(5)]
        N_UNITS = N_PAIRS * 2 * QB
        SAMPLE_POWERS = [(5, 7), (6, 1), (8, 3), (8, 5)]
        K_BACK = 6

        def parts(i):
            s = split_slot(i)
            return (w_hi[:, s], w_lo[:, s]) if s < SPL else (w_hi2[:, s - SPL], w_lo2[:, s - SPL])

        def ada_bank(g):
            return bank[3 if g < NCH and g % 2 else 7]

        def kv_value(n):
            return 16 * (NPAGE + 1) * (n // 2 + 1)

        block = ctx.enter_context(nc.Block())

        @block.sync
        def _(sp):
            def small(dst, src):
                sp.dma_start(dst, src).then_inc(small_landed, 16)

            small(cond[0:1, :], a["c_prompt"])
            small(cond[1:9, :], a["c_sample"])
            small(vec_rows[0:48, :], a["b_ada"][0].rearrange("(r c) -> r c", c=P))
            small(vec_rows[48:56, :], a["g_norm1"][0].rearrange("(r c) -> r c", c=P))
            small(vec_rows[56:64, :], a["g_norm2"][0].rearrange("(r c) -> r c", c=P))
            for half in range(2):
                small(g_col[64 * half:64 * half + 64, 0:1], a["g_qb"][0].rearrange("(d o) -> d o", o=1))
                small(g_col[64 * half:64 * half + 64, 1:2], a["g_qa"][0].rearrange("(d o) -> d o", o=1))
            small(gk_row[:, 0, :], a["g_kb"][0].partition_broadcast(P))
            small(gk_row[:, 1, :], a["g_ka"][0].partition_broadcast(P))
            small(bforget[ROW_FL:ROW_FL + H, :], a["b_forget"][0].rearrange("(d o) -> d o", o=1))
            small(gq_row[:, 0, :], a["g_qb"][0].partition_broadcast(NS))
            small(gq_row[:, 1, :], a["g_qa"][0].partition_broadcast(NS))
            sp.dma_start(page_row[:, :], a["page_table"].rearrange("(o b) n -> o (b n)", o=1)).then_inc(pages_landed, 16)
            sp.dma_start(x_tok[:, :, :], a["x_prompt"][0].rearrange("(t p) n -> p t n", p=P)).then_inc(x_landed, 16)
            sp.dma_start(x_stok[:, :], a["x_sample"][:, 0, :]).then_inc(x_landed, 16)
            for b in range(2):
                sp.dma_start(ada[:, b], ada_v[:, :, b * SEQ:(b + 1) * SEQ]).then_inc(ada_landed[b], 16)
            for b in range(2, ADA_BLOCKS):
                sp.wait_ge(mod_done, b - 1)
                sp.dma_start(ada[:, b % 2], ada_v[:, :, b * SEQ:(b + 1) * SEQ]).then_inc(ada_landed[b % 2], 16)

            def load(i):
                if i == T_SMALL:
                    sp.wait_ge(zeroed, 1)
                if i >= RAW:
                    sp.wait_ge(lo_ready, i - RAW + 1)
                for dst, src in tile_dmas(i):
                    sp.dma_start(dst, src).then_inc(raw_landed[i % RAW], 16)

            for i in range(RAW):
                load(i)
            for i in range(RAW, T_PAIR + 2 + RAW - 1):
                load(i)
            sp.wait_ge(negf_ready, 1)
            sp.dma_start(negf_d, lf[ROW_FL:ROW_FL + H, 1, 0:SEQ]).then_inc(negf_stored, 16)
            sp.wait_ge(smt_ready, 1)
            smt = abias[:, :].rearrange("p (t c) -> p t c", t=QB)
            sp.dma_start(a["k_idx_p"][0, 0].rearrange("(t p) d -> p t d", p=P), smt[:, :, 0:HD]).then_inc(stored, 16)
            sp.dma_start(a["logf_p"][0, 0].rearrange("(t p) d -> p t d", p=P), smt[:, :, ROW_FL:ROW_FL + H]).then_inc(stored, 16)
            sp.dma_start(a["k_idx_s"][0, :, 0, :], sm_tok_s[:, 0:HD]).then_inc(stored, 16)
            sp.dma_start(a["logf_s"][0, :, 0, :], sm_tok_s[:, ROW_FL:ROW_FL + H]).then_inc(stored, 16)
            sp.wait_ge(negf_stored, 16)
            sp.wait_ge(pages_landed, 16)
            pages = [sp.value_load(page_row[0:1, i:i + 1], min_val=0, max_val=n_pool - 1) for i in range(NS * NPAGE)]
            for i in range(NS * NPAGE):
                for dup in range(2):
                    sp.dma_start(ki_pg[:, i, dup, :], a["cache_k_idx"][0, bass.ds(pages[i], 1)].rearrange("o p d -> p (o d)"))\
                        .then_inc(kip_landed, 16)
                sp.dma_start(lfp[:, i % 2, H * (i // 2):H * (i // 2) + H],
                             a["cache_logf_b"][0, bass.ds(pages[i], 1)].rearrange("o p d -> p (o d)")).then_inc(lfp_landed, 16)

            def sample_stores(m):
                ts = [ts_b, ts_a][m]
                sp.wait_ge(ts_norm, 2 * m + 2)
                sp.wait_ge(side_read, [10, 13][m])
                sp.dma_start(q_d[m], ts[:, 0, :]).then_inc(q_stored, 16)
                for j, name in ((1, ["k_b_s", "k_a_s"][m]), (2, ["v_b_s", "v_a_s"][m])):
                    sp.dma_start(a[name][0, :, 0].rearrange("b h d -> b (h d)"), ts[:, j, :]).then_inc(stored, 16)

            for p, s in ITERATIONS:
                if s == 0 and p < 4:
                    if p >= 2:
                        sp.wait_ge(lg_ready, 8 * (p - 1))
                    for hh in range(2):
                        sp.dma_start(fbc[:, p % 2, hh, :], negf_d[2 * p + hh].partition_broadcast(P)).then_inc(fbc_landed[p % 2], 16)
                for i in loads_at(p, s):
                    load(i)
                if s == K_BACK and p < N_PAIRS:
                    m, c = pair_mixer(p)
                    sp.wait_ge(tok_ready, p + 1)
                    dst = a[["k_b_p", "k_a_p"][m]][0, 0].rearrange("(t p) h d -> p t (h d)", p=P)
                    sp.dma_start(dst[:, :, c * P:(c + 1) * P], tok[:, 1, :].rearrange("p (t c) -> p t c", t=QB)).then_inc(k_stored, 16)
                if s == 1 and 1 <= p <= N_PAIRS:
                    m, c = pair_mixer(p - 1)
                    sp.wait_ge(v_ready, p)
                    dst = a[["v_b_p", "v_a_p"][m]][0, 0].rearrange("(t p) h d -> p t (h d)", p=P)
                    sp.dma_start(dst[:, :, c * P:(c + 1) * P], v_tok[:, (p - 1) % 2]).then_inc(v_stored, 16)
                if (p, s) == (1, 7):
                    sp.wait_ge(wi_ready, 1)
                    sp.dma_start(wi_d, s8[:, 8, :]).then_inc(wi_stored, 16)
                if (p, s) == (2, 7):
                    sp.wait_ge(wi_stored, 16)
                    sp.dma_start(wbc[:, :, :], wi_d.rearrange("b h -> (b h)").partition_broadcast(P).rearrange("p (b h) -> p b h", h=H))\
                        .then_inc(wbc_landed, 16)
                if (p, s) == (7, 7):
                    sample_stores(0)
            def load_pages(dst, which, unit, landed):
                m, b = unit // NS, unit % NS
                for pg in range(NPAGE):
                    sp.dma_start(dst[:, pg, :], a[which + "ba"[m]][0, bass.ds(pages[b * NPAGE + pg], 1)].rearrange("o p h d -> p (o h d)"))\
                        .then_inc(landed, 16)

            def load_keys(n):
                if n >= 2:
                    sp.wait_ge([prod_dve, prod_pool][n % 2], n // 2)
                load_pages(kv[n % 2], "cache_k_", n, kv_landed[n % 2])
                sp.dma_start(qbc[n % 2][:, :], q_d[n // NS, n % NS].partition_broadcast(P)).then_inc(kv_landed[n % 2], 16)

            def load_values(v):
                if v < 2:
                    sp.wait_ge([prod_dve, prod_pool][v], NS)
                elif v < 4:
                    sp.wait_ge(prod_used, 2 * NS - 3 + v)
                else:
                    sp.wait_ge(pv_used, v - 3)
                load_pages(vbuf[v % 4], "cache_v_", v, val_landed[v % 4])

            keys_at = [(T_GATE + 10 + j, count) for j, count in enumerate(KEYS_AT)]
            values_at = [(T_GATE + 5 + j, count) for j, count in VALUES_AT.items()]
            for i in range(T_GATE + 10, T_MLP):
                if i >= T_GATE + 11:
                    load(i)
                if i == T_GATE + 10:
                    sample_stores(1)
                    sp.wait_ge(q_stored, 32)
                    sp.wait_ge(own_done, 2)
                    sp.wait_ge(o_lo_ready, N_PAIRS)
                    load_keys(0)
                    load_keys(1)
                for n in range(2, 2 * NS):
                    if i == unit_tile(n - 2, keys_at):
                        load_keys(n)
                if i == keys_at[-1][0]:
                    for v in range(4):
                        load_values(v)
                for v in range(4, 2 * NS):
                    if i == unit_tile(v - 4, values_at):
                        load_values(v)
            for q in range(2):
                with sp.Fori(0, 4) as it:
                    for b in range(4):
                        i = T_MLP + 32 * q + b
                        sp.wait_ge(lo_ready, it * 4 + (i - RAW + 1))
                        sp.dma_start(raw[:, i % RAW], wup_v[:, :, bass.ds((it * 4 + (16 * q + b)) * P, P)])\
                            .then_inc(raw_landed[i % RAW], 16)
                with sp.Fori(0, 4) as it:
                    for b in range(4):
                        i = T_MLP + 32 * q + 16 + b
                        k0 = 16 * q + 8 * (b % 2)
                        sp.wait_ge(lo_ready, it * 4 + (i - RAW + 1))
                        sp.dma_start(raw[:, i % RAW], wdn_v[:, k0:k0 + NCH, bass.ds((it * 2 + b // 2) * P, P)])\
                            .then_inc(raw_landed[i % RAW], 16)
            y_v = a["y_p"][0].rearrange("(t p) n -> p t n", p=P)
            for g in range(4):
                sp.wait_ge(y_act, g + 1)
                sp.wait_ge(y_dve, g + 1)
                sp.dma_start(y_v[:, :, 256 * g:256 * g + 256], y_tok[:, :, 256 * g:256 * g + 256]).then_inc(stored, 16)
            sp.wait_ge(y_act, 5)
            sp.dma_start(a["y_s"][:, 0, :], y_stok[:, :]).then_inc(stored, 16)
            sp.wait_ge(stored, 16 * (4 + 4 + 5))
            sp.wait_ge(k_stored, 16 * N_PAIRS)
            sp.wait_ge(v_stored, 16 * N_PAIRS)

        @block.gpsimd
        def _(pool):
            steps = [0]

            def link(ins):
                steps[0] += 1
                ins.then_inc(pool_self, 1)
                pool.wait_ge(pool_self, steps[0])

            link(pool.memset(ident[:, :], 0.0))
            pool.affine_select(out=ident[:, :], in_=ident[:, :], compare_op=ALU.not_equal, fill=1.0, base=0,
                               pattern=[[-1, P]], channel_multiplier=1).then_inc(consts, 1)
            pool.memset(ones[:, :], 1.0)
            pool.memset(neghalf[:, :], -0.5)
            link(pool.iota(dist[:, :], pattern=[[1, SEQ]], base=-(SEQ - P), channel_multiplier=-1,
                           allow_small_or_imprecise_dtypes=True))
            pool.affine_select(out=dist[:, :], in_=dist[:, :], compare_op=ALU.is_ge, fill=MASK, base=SEQ - P,
                               pattern=[[-1, SEQ]], channel_multiplier=1)
            link(pool.memset(cmask[:, :], 0.0))
            pool.affine_select(out=cmask[:, :], in_=cmask[:, :], compare_op=ALU.is_ge, fill=MASK, base=0,
                               pattern=[[-1, P]], channel_multiplier=1).then_inc(consts, 1)
            pool.memset(raw[:, T_SMALL % RAW], 0.0).then_inc(zeroed, 1)
            pool.memset(q_idx[:, :, :], 0.0).then_inc(zeroed, 1)
            pool.memset(qzs[:, :, :, :], 0.0)
            link(pool.memset(spread[:, :], 0.0))
            link(pool.affine_select(out=spread[:, :].rearrange("p (b h) -> p b h", h=H),
                                    in_=spread[:, :].rearrange("p (b h) -> p b h", h=H), compare_op=ALU.not_equal, fill=1.0,
                                    base=0, pattern=[[-1, NS], [0, H]], channel_multiplier=1))
            link(pool.memset(gather[:, :], 1.0))
            link(pool.affine_select(out=gather[:, :], in_=gather[:, :], compare_op=ALU.is_ge, fill=0.0, base=0,
                                    pattern=[[-H, NS]], channel_multiplier=1))
            link(pool.affine_select(out=gather[:, :], in_=gather[:, :], compare_op=ALU.is_ge, fill=0.0, base=H - 1,
                                    pattern=[[H, NS]], channel_multiplier=-1))
            link(pool.memset(pick[:, :], 0.0))
            for b in range(NS):
                link(pool.affine_select(out=pick[:, :], in_=pick[:, :], compare_op=ALU.not_equal, fill=1.0, base=-H * b,
                                        pattern=[[-1, H]], channel_multiplier=1))
            for h in range(H):
                pool.memset(slope_rows[:, h:h + 1], SLOPES[h])
            pool.memset(s8[:, 11, :], 0.0).then_inc(s_consts, 1)
            pool.wait_ge(h_lo_ready, NCH + 1)
            pool.memset(q_pad[:, :, :, :], 0.0).then_inc(zeroed, 1)

            def power(n):
                pool.wait_ge(ms_tok, n + 1)
                if n >= 1:
                    pool.wait_ge(tok_read, n)
                pool.tensor_tensor(rs8[:, :], ms8[:, :], neghalf[:, :], ALU.pow).then_inc(rstd_tok, 1)

            def rest_w(i):
                pool.wait_ge(lo_ready, i)
                pool.wait_ge(hi_ready, i + 1)
                pool.tensor_tensor(parts(i)[1], raw[:, i % RAW], parts(i)[0].bitcast(F32), ALU.subtract).then_inc(lo_ready, 1)

            def sample_power(n):
                pool.wait_ge(ts_ms, n + 1)
                pool.tensor_tensor(s8[:, 4 + n, :], s8[:, n, :], neghalf[0:NS, :], ALU.pow).then_inc(ts_rs, 1)

            for p, s in ITERATIONS:
                for i in split_at(p, s):
                    rest_w(i)
                if p < N_PAIRS and s in (2, 4):
                    power(2 * p + s // 2 - 1)
                if p == 0 and s in (3, 5, 7):
                    qb = s // 2
                    pool.wait_ge(idx_sum, H * qb)
                    o = sel_at[qb] + qb * P
                    pool.affine_select(out=sel[:, o:o + P], in_=sel[:, o:o + P], compare_op=ALU.is_ge, fill=MASK,
                                       base=0, pattern=[[-1, P]], channel_multiplier=1).then_inc(sel_ready, 1)
                if (p, s) == (5, 5):
                    pool.wait_ge(lg_ready, 8 * 4)
                    pool.iota(dist_s[:, :], pattern=[[1, L]], base=-PAST, channel_multiplier=0, allow_small_or_imprecise_dtypes=True)\
                        .then_inc(s_consts, 1)
                if (p, s) in SAMPLE_POWERS:
                    sample_power(SAMPLE_POWERS.index((p, s)))
            pool.wait_ge(o_lo_ready, N_PAIRS)
            pool.memset(ptz[:, :, :], 0.0).then_inc(s_consts, 1)
            for n in range(1, 2 * NS, 2):
                pool.wait_ge(kv_landed[1], kv_value(n))
                if n >= 3:
                    pool.wait_ge(prod_used, n - 1)
                pool.tensor_tensor(prod1[:, :, :], kv1[:, :, :], qbc1[:, :].unsqueeze(1).to_broadcast([P, NPAGE, SEQ]), ALU.mult)\
                    .then_inc(prod_pool, 1)
            for g in range(2 * NCH - 1):
                rest_w(T_WO + GROUP * g + 6)

        @block.tensor
        def _(pe):
            mm, tr = nc.tensor.matmul, nc.tensor.transpose
            pe.wait_ge(consts, 1)
            pe.wait_ge(small_landed, 16 * N_SMALL)
            tr(bank[7][:, 0:64], vec_rows[:, :], ident[0:64, 0:64])
            for j in range(NCH):
                last = tr(bank[7][:, 64 + 9 * j:73 + 9 * j], cond[:, j * P:(j + 1) * P], ident[0:9, 0:9])
            last.then_inc(vec_done, 1)
            pe.wait_ge(x_landed, 32)
            for j in range(NCH):
                if j >= 4:
                    pe.wait_ge([xt_act, xt_dve][j % 2], (j - 4) // 2 + 1)
                tr(bank[6][:, 8 * j:8 * j + 8], x_stok[:, j * P:(j + 1) * P], ident[0:NS, 0:NS])
                for t in range(QB):
                    last = tr(bank[j % 4][:, t * P:(t + 1) * P], x_tok[:, t, j * P:(j + 1) * P], ident[:, :])
                last.then_inc(xt_done, 1)

            def norm_sum(n, j):
                pe.wait_ge(sq_ready, NCH * n + j + 1)
                for half in range(2):
                    last = mm(bank[[4, 2][n] + half][:, 0:HALF], ones[:, :], nrm[:, j % 2, half * HALF:(half + 1) * HALF],
                              start=j == 0, stop=j == NCH - 1)
                last.then_inc(sq_used, 1)

            pe.wait_ge(consts, 2)
            for j in range(NCH):
                norm_sum(0, j)

            pe.wait_ge(cond_ready, 1)
            pe.wait_ge(xt_act, 4)
            pe.wait_ge(xt_dve, 5)
            for b in range(ADA_BLOCKS + 1):
                if b < ADA_BLOCKS:
                    if b >= 2:
                        pe.wait_ge(mod_row_ready, b - 1)
                    pe.wait_ge(ada_landed[b % 2], 16 * (b // 2 + 1))
                    for k in range(NCH):
                        last = mm(bank[b % 2][0:9, :], cond_t[:, k, :], ada[:, b % 2, k, :], start=k == 0, stop=k == NCH - 1)
                    last.then_inc(mod_done, 1)
                if b >= 1:
                    t = b - 1
                    pe.wait_ge(mod_row_ready, t + 1)
                    if t >= 2:
                        pe.wait_ge(mod_ready, t - 1)
                    for q in range(4):
                        last = tr(bank[2 + t % 2][:, 9 * q:9 * q + 9], mod_row[:, t % 2, q * P:(q + 1) * P], ident[0:9, 0:9])
                    last.then_inc(mod_turned, 1)

            def half_tile(i, half, out, ks=range(NCH), src=(h_hi, h_lo), k0=0, first=True, last=True):
                n0 = half * HALF
                hi, lo = parts(i)
                for k in ks:
                    x_h, x_l = src[0][:, k0 + k, n0:n0 + HALF], src[1][:, k0 + k, n0:n0 + HALF]
                    mm(out, hi[:, k, :], x_h, start=first and k == ks[0], stop=False)
                    mm(out, hi[:, k, :], x_l, start=False, stop=False)
                    end = mm(out, lo[:, k, :], x_h, start=False, stop=last and k == ks[-1])
                return end

            def first_tiles(i, n):
                pe.wait_ge(hi_ready, i + 2)
                pe.wait_ge(lo_ready, i + 2)
                pe.wait_ge(h_lo_ready, (NCH + 1) * n + 1)
                for k in range(NCH):
                    pe.wait_ge(h_lo_ready, (NCH + 1) * n + k + 2)
                    for tile_ in (i, i + 1):
                        for half in range(2):
                            last = half_tile(tile_, half, bank[half + 4 * par(tile_)][:, 0:HALF], ks=[k], first=k == 0, last=k == NCH - 1)
                            if k == NCH - 1:
                                last.then_inc(proj_done, 1)

            def project(i, half):
                if half == 0:
                    pe.wait_ge(hi_ready, i + 1)
                    pe.wait_ge(lo_ready, i + 1)
                b = half + 4 * par(i)
                if i >= 1:
                    before = i - 1 if par(i - 1) == par(i) else i - 2
                    pe.wait_ge(act_evac, act_evac_value(before, half))
                half_tile(i, half, bank[b][:, 0:HALF]).then_inc(proj_done, 1)

            def ada_product(g, half):
                i, bk = T_WO + GROUP * g + 1 + half, ada_bank(g)
                pe.wait_ge(hi_ready, i + 1)
                pe.wait_ge(lo_ready, i + 1)
                if half == 0:
                    if g >= 1:
                        pe.wait_ge(dve_evac, 2 * min(g, NCH))
                    pe.wait_ge(mod_ready, ADA_BLOCKS + (g if g >= NCH else max(g - 1, 0)))
                hi, lo = (w.rearrange("p k c -> p (k c)").rearrange("p (k c) -> p k c", k=4) for w in parts(i))
                for k in range(4):
                    c = 4 * half + k
                    if half == 0:
                        mm(bk[0:18, 0:2 * P], cond_h[:, c, :], hi[:, k, :], start=k == 0, stop=False)
                        last = mm(bk[0:9, 0:2 * P], cond_h[:, c, 0:9], lo[:, k, :], start=False, stop=False)
                    else:
                        mm(bk[0:9, 0:2 * P], cond_h[:, c, 0:9], lo[:, k, :], start=False, stop=False)
                        last = mm(bk[0:18, 0:2 * P], cond_h[:, c, :], hi[:, k, :], start=False, stop=k == 3)
                last.then_inc(proj_done, 2)

            def ada_turn(g):
                pe.wait_ge(act_evac, 2 * T_WO + 4 * (g + 1))
                for u in range(2):
                    last = tr(ada_bank(g)[:, 2 * P + 18 * u:2 * P + 18 * u + 18], mod_row2[:, g % 2, u * P:(u + 1) * P], ident[0:18, 0:18])
                last.then_inc(mod_turned, 1)

            def scores(U):
                p, hh, qb = U // 8, U // 4 % 2, U % 4
                if U >= 2:
                    pe.wait_ge(lg_ready, U - 1)
                if U % 8 == 0:
                    pe.wait_ge(back_read, 2 * p + 2)
                mm(bank[4 + U % 2][:, 0:width(qb)], q_pad[:, p % 2, hh, qb * P:(qb + 1) * P],
                   k_fm[:, p % 2, 0:width(qb)], start=True, stop=True).then_inc(s_done, 1)

            def turn_probs(U):
                qb = U % 4
                pe.wait_ge(p_ready, U + 1)
                if U >= 1:
                    pe.wait_ge(pt_ready, U)
                for kb in range(qb + 1):
                    last = tr(bank[6][:, kb * P:(kb + 1) * P], lg[:, U % 3, kb * P:(kb + 1) * P], ident[:, :])
                last.then_inc(pt_done, 1)

            def values(p, hh):
                pe.wait_ge(pt_ready, 8 * p + 4 * hh + 4)
                pe.wait_ge(v_ready, p + 1)
                if p >= 1:
                    pe.wait_ge(o_lo_ready, p)
                for kb in range(QB):
                    last = mm(bank[7][64 * hh:64 * hh + 64, kb * P:SEQ], v_tok[:, p % 2, kb, 64 * hh:64 * hh + 64],
                              p_t[:, hh, kb, kb * P:SEQ], start=kb == 0, stop=kb == QB - 1)
                last.then_inc(pv_done, 1)

            def to_tokens(p, kd):
                pe.wait_ge(act_evac, act_evac_value(T_PAIR + 3 * p + kd, 1))
                if kd == 0:
                    if p == 0:
                        pe.wait_ge(smt_ready, 1)
                    else:
                        pe.wait_ge(v_ready, p)
                else:
                    pe.wait_ge(tok_read, 2 * p + kd)
                before = sum(at[0] < p or (kd == 2 and at[0] == p) for at in SIDE)
                if before:
                    pe.wait_ge(side_read, before)
                for t in range(QB):
                    last = tr(bank[2][:, t * P:(t + 1) * P], z[:, kd, t * P:(t + 1) * P], ident[:, :])
                last.then_inc(tok_done, 1)

            def to_features(p, kd):
                pe.wait_ge(tok_read if kd == 0 else tok_ready, 2 * p + 1 if kd == 0 else p + 1)
                if p == 0 and kd == 0:
                    pe.wait_ge(smt_ready, 1)
                if 2 * p + kd >= 1:
                    pe.wait_ge(back_read, 2 * p + kd)
                for t in range(QB):
                    last = tr(bank[3][:, t * P:(t + 1) * P], tok[:, kd, t * P:(t + 1) * P], ident[:, :])
                last.then_inc(back_done, 1)

            def index_scores(n):
                qb, h = 1 + n // H, n % H
                if n >= 2:
                    pe.wait_ge(idx_relu, n - 1)
                mm(bank[4 + n % 2][:, 0:width(qb)], q_idx[:, h, qb * P:(qb + 1) * P], ki2[:, 0:width(qb)],
                   start=True, stop=True).then_inc(idx_done, 1)

            def side_step(e):
                p, bk = SIDE[e][0], bank[2 + e % 2]
                if e >= 2:
                    pe.wait_ge(side_read, e - 1)
                if p == N_PAIRS:
                    pe.wait_ge(v_ready, p)
                elif e % 2:
                    pe.wait_ge(back_read, 2 * p + 2)
                else:
                    pe.wait_ge(tok_read, 2 * p + 2)
                if e < 4:
                    pe.wait_ge(kip_landed, 16 * 2 * NS * NPAGE)
                    for q in range(4):
                        last = tr(bk[:, q * P:(q + 1) * P], ki_pg[:, 4 * e + q].rearrange("p a d -> p (a d)"), ident[:, :])
                elif e == 4:
                    pe.wait_ge(side_read, 4)
                    pe.wait_ge(qzs_ready, 1)
                    for i in range(NS * NPAGE):
                        last = mm(bk[:, H * i:H * i + H], ki_pt[:, i, :], qzs[:, i // 2].rearrange("p c h -> p (c h)"),
                                  start=True, stop=True)
                elif e == 5:
                    pe.wait_ge(is_sum, 1)
                    for pg in range(NPAGE):
                        last = tr(bk[0:NS, pg * P:(pg + 1) * P], iss[:, :, pg], ident[:, :])
                else:
                    z0 = [0, 4, 24, 8, 12, 16, 20][e - 6]
                    for c in range(4):
                        last = tr(bk[0:NS, c * P:(c + 1) * P], z_s[:, z0 + c, :], ident[:, :])
                last.then_inc(side_done, 1)

            first_tiles(0, 0)
            for i in range(2, T_PAIR):
                project(i, 0)
                project(i, 1)
                if i == 2:
                    pe.wait_ge(sm_ready, 3)
                    for t in range(QB):
                        tr(bank[2][:, t * P:(t + 1) * P], zsm[:, t * P:(t + 1) * P], ident[:, :])
                    tr(bank[3][0:NS, 0:P], zsm[:, SEQ:T], ident[:, :]).then_inc(smt_done, 1)

            for p, s in ITERATIONS:
                U = SLOTS * (p - 1) + s
                if s in HALVES_AT and (p, s) < (N_PAIRS + 1, 4):
                    project(T_PAIR + 3 * p + HALVES_AT.index(s) // 2, HALVES_AT.index(s) % 2)
                if p < N_PAIRS:
                    if s == 2:
                        to_tokens(p, 0)
                    if s == 4:
                        to_tokens(p, 1)
                        to_features(p, 0)
                    if s == K_BACK:
                        to_features(p, 1)
                if s == 0 and 1 <= p <= N_PAIRS:
                    to_tokens(p - 1, 2)
                if p == 0:
                    if s == 0:
                        pe.wait_ge(act_evac, act_evac_value(T_PAIR - 1, 1))
                        pe.wait_ge(sm_ready, 3)
                    for n in range(3 * s, 3 * s + 3):
                        index_scores(n)
                if 0 <= U - 2 < N_UNITS:
                    turn_probs(U - 2)
                if 0 <= U < N_UNITS:
                    if U < 2:
                        pe.wait_ge(idx_relu, 24)
                    scores(U)
                if s == 6 and 1 <= p <= N_PAIRS:
                    values(p - 1, 0)
                if s == 2 and p >= 2:
                    values(p - 2, 1)
                if (p, s) in SIDE:
                    side_step(SIDE.index((p, s)))
            def spread_dist():
                pe.wait_ge(dist_ready, 1)
                mm(bank[6][0:64, 0:L], spread[:, :], srow[:, :], start=True, stop=True).then_inc(dist_spread, 1)

            def turn_rows():
                pe.wait_ge(prod_used, 2 * NS)
                pe.wait_ge(side_read, len(SIDE))
                pe.wait_ge(lfp_landed, 16 * NS * NPAGE)
                for m in range(2):
                    for pg in range(NPAGE):
                        tr(bank[2 + m][0:64, pg * P:(pg + 1) * P], lgs[:, m, pg, :], ident[:, :])
                for pg in range(NPAGE):
                    tr(bank[7][0:64, P + pg * P:2 * P + pg * P], lfp[:, pg, :], ident[:, :])
                mm(bank[7][0:64, 0:16], spread[:, :], s8[:, 9:11, :].rearrange("p a h -> p (a h)"), start=True, stop=True)
                mm(bank[7][0:64, 16:24], spread[:, :], sm_tok_s[:, ROW_FL:ROW_FL + H], start=True, stop=True).then_inc(rows_turned, 1)

            def turn_pts():
                for m in range(2):
                    pe.wait_ge(rows_p, m + 1)
                    for pg in range(NPAGE):
                        tr(bank[6][:, (2 * m + pg) * 64:(2 * m + pg + 1) * 64], rows_l[:, m, pg * P:(pg + 1) * P], ident[0:64, 0:64])
                pe.wait_ge(rows_p, 3)
                mm(bank[7][0:NS, 0:16], gather[:, :], pself[:, :, :].rearrange("p a h -> p (a h)"), start=True, stop=True)\
                    .then_inc(pts_turned, 1)

            def sample_values(v):
                m, b = v // NS, v % NS
                pe.wait_ge(val_landed[v % 4], 16 * NPAGE * (v // 4 + 1))
                for pg in range(NPAGE):
                    last = mm(bank[2 + m][0:64, :], ptz[:, NPAGE * m + pg, 64 * b:64 * b + 64], vbuf[v % 4][:, pg, :],
                              start=b == 0 and pg == 0, stop=b == NS - 1 and pg == NPAGE - 1)
                last.then_inc(pv_used, 1)

            def sample_outputs(m):
                pe.wait_ge(om_ready, m + 1)
                for c in range(4):
                    out = bank[6][:, 256 + (4 * m + c) * NS:256 + (4 * m + c + 1) * NS]
                    mm(out, om[:, m, c * P:(c + 1) * P], gather[:, :], start=True, stop=False)
                    last = mm(out, [ts_b, ts_a][m][:, 2, c * P:(c + 1) * P], ident[0:NS, 0:NS], start=False, stop=True)
                last.then_inc(os_done, 1)

            pe.wait_ge(o_hi_ready, N_PAIRS)
            pe.wait_ge(o_lo_ready, N_PAIRS)
            v = 0
            for i in range(T_GATE + 5, T_WO):
                if i == T_GATE + 5:
                    spread_dist()
                if i == T_GATE + 12:
                    turn_rows()
                if i == T_GATE + 14:
                    turn_pts()
                for _ in range(VALUES_AT.get(i - T_GATE, 0)):
                    if v == 0:
                        pe.wait_ge(pts_ready, 2)
                    sample_values(v)
                    v += 1
                project(i, 0)
                project(i, 1)
            sample_outputs(0)
            sample_outputs(1)

            pe.wait_ge(os_hi, 1)
            pe.wait_ge(os_lo, 1)
            pe.wait_ge(act_evac, act_evac_value(T_WO - 1, 1))
            for g in range(2 * NCH):
                i, b = T_WO + GROUP * g, 4 * (g % 2)
                if g == NCH:
                    pe.wait_ge(mf_hi, 2 * NCH)
                    pe.wait_ge(mf_lo, 2 * NCH)
                pe.wait_ge(hi_ready, i + 1)
                pe.wait_ge(lo_ready, i + 1)
                for half in range(2):
                    if g >= 2:
                        pe.wait_ge(dve_evac, 2 * (g - 2) + half + 1)
                    if g < NCH:
                        half_tile(i, half, bank[b + half][:, 0:HALF], range(0, 4), (o_hi, o_lo))
                        if half and g:
                            pe.wait_ge(mod_ready, ADA_BLOCKS + g)
                        half_tile(i, half, bank[b + half + 2][:, 0:HALF], range(4, 8), (o_hi, o_lo)).then_inc(proj_done, 1)
                    else:
                        half_tile(i, half, bank[b + half][:, 0:HALF]).then_inc(proj_done, 1)
                    if g and not half:
                        ada_turn(g - 1)
                ada_product(g, 0)
                ada_product(g, 1)
                if g > NCH:
                    norm_sum(1, g - NCH - 1)
            ada_turn(2 * NCH - 1)
            norm_sum(1, NCH - 1)
            def up_tile(q, b, it):
                i = T_MLP + 32 * q + b
                pe.wait_ge(hi_ready, it * 4 + (i + 1))
                pe.wait_ge(lo_ready, it * 4 + (i + 1))
                for half in range(2):
                    pe.wait_ge(act_evac, it * 8 + (2 * (T_WO + 4 * NCH) + 32 * q + 2 * (b - 2) + half + 1))
                    half_tile(i, half, bank[half + 4 * (i % 2)][:, 0:HALF]).then_inc(proj_done, 1)

            first_tiles(T_MLP, 1)
            up_tile(0, 2, 0)
            up_tile(0, 3, 0)
            for q in range(2):
                with pe.Fori(0 if q else 1, 4) as it:
                    for b in range(4):
                        up_tile(q, b, it)
                pe.wait_ge(u_hi_ready, 32 * (q + 1))
                pe.wait_ge(u_lo_ready, 32 * (q + 1))

                def down_tile(b, it):
                    i = T_MLP + 32 * q + 16 + b
                    kg, mb = b % 2, b // 2
                    pe.wait_ge(hi_ready, it * 4 + (i + 1))
                    pe.wait_ge(lo_ready, it * 4 + (i + 1))
                    for half in range(2):
                        if kg == 0:
                            pe.wait_ge(dve_evac, it * 4 + (32 + 16 * q + 2 * (mb - 2) + half + 1))
                        half_tile(i, half, bank[2 + half + 4 * mb][:, 0:HALF], src=(u_hi, u_lo), k0=8 * kg,
                                  first=kg == 0, last=kg == 1).then_inc(proj_done, 1)

                with pe.Fori(0, 3 if q else 4) as it:
                    for b in range(4):
                        down_tile(b, it)

            def turn_y(j):
                pe.wait_ge(dve_evac, 48 + 2 * (j + 1))
                if j >= 2:
                    pe.wait_ge([y_act, y_dve][j % 2], (j - 2) // 2 + 1)
                tr(bank[4 + j // 4][0:NS, (j % 4) * P:(j % 4 + 1) * P], x_t[:, j, SEQ:T], ident[:, :])
                for t in range(QB):
                    last = tr(bank[j % 2][:, t * P:(t + 1) * P], x_t[:, j, t * P:(t + 1) * P], ident[:, :])
                last.then_inc(y_done, 1)

            for b in range(4):
                down_tile(b, 3)
                if b < 3:
                    turn_y(2 * b)
                    turn_y(2 * b + 1)
            turn_y(6)
            turn_y(7)

        @block.scalar
        def _(act):
            A = nc.scalar.activation
            steps = [0]

            def link(ins):
                steps[0] += 1
                ins.then_inc(act_self, 1)
                act.wait_ge(act_self, steps[0])

            act.wait_ge(vec_done, 1)
            A(vec_t[:, :], bank[7][:, 0:64], ACT.Copy)
            A(sig[:, :], bank[7][:, 64:136], ACT.Sigmoid).then_inc(vec_ready, 1)
            for j in range(0, NCH, 2):
                act.wait_ge(xt_done, j + 1)
                A(x_t[:, j, 0:SEQ], bank[j % 4][:, :], ACT.Copy).then_inc(xt_act, 1)

            def square(n, j):
                if j >= 2 or n >= 1:
                    act.wait_ge(sq_used, NCH * n + j - 1)
                A(nrm[:, j % 2, :], x_t[:, j, :], ACT.Square).then_inc(sq_ready, 1)

            def inverse_root(n):
                if n == 0:
                    A(stat[0:1, 39:40], ones[0:1, 0:1], ACT.Ln)
                act.wait_ge(ms_ready, n + 1)
                link(A(nbuf[:, 1, :], nbuf[:, 0, :], ACT.Ln))
                A(nbuf[:, 1, :], nbuf[:, 1, :], ACT.Exp, scale=-0.5).then_inc(rs_ready, 1)

            act.wait_ge(cond_ready, 1)
            A(cond_h[:, :, 0:9], cond_t[:, :, :], ACT.Copy).then_inc(cond_hi, 1)
            act.wait_ge(xt_act, 4)
            act.wait_ge(xt_dve, 5)
            for j in range(NCH):
                square(0, j)
            act.wait_ge(consts, 2)
            inverse_root(0)

            def mod_rows(b, value):
                act.wait_ge(mod_done, value)
                A(mod_row[:, b, :], bank[b][0:9, :], ACT.Copy).then_inc(mod_row_ready, 1)

            for t in range(ADA_BLOCKS):
                if t >= 2:
                    act.wait_ge(mod_turned, t - 1)
                mod_rows(t % 2, t + 1)

            def round_h(n):
                act.wait_ge(nf_ready, (NCH + 1) * n + 1)
                A(h_hi[:, :, SEQ:T], nsm[:, 0], ACT.Copy).then_inc(h_hi_ready, 1)
                for j in range(NCH):
                    act.wait_ge(nf_ready, (NCH + 1) * n + j + 2)
                    A(h_hi[:, j, 0:SEQ], nrm[:, j % 2, 0:SEQ], ACT.Copy).then_inc(h_hi_ready, 1)

            def round_w(i):
                act.wait_ge(raw_landed[i % RAW], landed_value(i))
                if T_WO + 2 <= i < T_WO + 4:
                    act.wait_ge(pv_used, 2 * NS)
                elif i >= SPL:
                    act.wait_ge(proj_done, 2 * (i - (4 if T_WO + 4 <= i < T_MLP + 2 else SPL) + 1))
                A(parts(i)[0], raw[:, i % RAW], ACT.Copy).then_inc(hi_ready, 1)

            round_w(0)
            round_w(1)
            round_h(0)

            def store_z(p, kd, half):
                m, c = pair_mixer(p)
                i = T_PAIR + 3 * p + kd
                act.wait_ge(proj_done, 2 * i + half + 1)
                if half == 0:
                    if p >= 1:
                        act.wait_ge(tok_done, 3 * (p - 1) + kd + 1)
                    A(z[:, kd, 0:HALF], bank[0][:, 0:HALF], ACT.Copy).then_inc(act_evac, 1)
                else:
                    A(z[:, kd, HALF:SEQ], bank[1][:, 0:SEQ - HALF], ACT.Copy)
                    A(z_s[:, 12 * m + 4 * kd + c, :], bank[1][:, SEQ - HALF:HALF], ACT.Copy).then_inc(act_evac, 1)

            def store_gate(j, half):
                i = T_GATE + j
                act.wait_ge(proj_done, 2 * i + half + 1)
                if j < 5:
                    act.wait_ge(k_stored, 16 * N_PAIRS)
                A(gate[:, j, half * HALF:(half + 1) * HALF], bank[half + 4 * par(i)][:, 0:HALF], ACT.Copy).then_inc(act_evac, 1)

            def exps(U):
                w = width(U % 4)
                act.wait_ge(lg_ready, U + 1)
                A(lg[:, U % 3, 0:w], lg[:, U % 3, 0:w], ACT.Exp, bias=stat[:, 8 + U % 8:9 + U % 8],
                  accum_out=stat[:, 16 + U % 8:17 + U % 8]).then_inc(e_ready, 1)

            def store_pt(U):
                p, hh, qb = U // 8, U // 4 % 2, U % 4
                act.wait_ge(pt_done, U + 1)
                if p >= 1:
                    act.wait_ge(pv_done, 2 * (p - 1) + hh + 1)
                A(p_t[:, hh, 0:qb + 1, qb * P:(qb + 1) * P], bank[6][:, 0:width(qb)].rearrange("p (k c) -> p k c", k=qb + 1),
                  ACT.Copy).then_inc(pt_ready, 1)

            def square_tok(p, kd):
                act.wait_ge(tok_done, 3 * p + kd + 1)
                if 2 * p + kd >= 1:
                    act.wait_ge(ms_tok, 2 * p + kd)
                A(sq[:, :], bank[2][:, :], ACT.Square).then_inc(tok_sq, 1)

            def store_back(p, kd):
                m = pair_mixer(p)[0]
                act.wait_ge(back_done, 2 * p + kd + 1)
                if kd == 0:
                    if p == 0:
                        act.wait_ge(zeroed, 3)
                    if p >= 2:
                        act.wait_ge(s_done, 8 * (p - 1))
                    A(q_pad[0:64, p % 2, 0, :], bank[3][0:64, :], ACT.Copy, scale=gq[0:64, m:m + 1])
                    A(q_pad[64:128, p % 2, 1, :], bank[3][64:128, :], ACT.Copy, scale=gq[64:128, m:m + 1]).then_inc(back_read, 1)
                else:
                    A(k_fm[:, p % 2, :], bank[3][:, :], ACT.Copy).then_inc(back_read, 1)

            def store_v(p):
                act.wait_ge(tok_done, 3 * p + 3)
                if p >= 2:
                    act.wait_ge(v_stored, 16 * (p - 1))
                    act.wait_ge(pv_done, 2 * (p - 1))
                A(v_tok[:, p % 2], bank[2][:, :].rearrange("p (t c) -> p t c", t=QB), ACT.Copy).then_inc(v_ready, 1)

            def round_o(p):
                act.wait_ge(pv_done, 2 * p + 2)
                A(o_hi[:, p, 0:SEQ], bank[7][:, :], ACT.Copy).then_inc(o_hi_ready, 1)

            def relu_scores(n):
                w = width(1 + n // H)
                act.wait_ge(idx_done, n + 1)
                if n >= 2:
                    act.wait_ge(idx_sum, n - 1)
                if n < 2:
                    act.wait_ge(smt_done, 1)
                A(rbuf[:, n % 2, 0:w], bank[4 + n % 2][:, 0:w], ACT.Relu).then_inc(idx_relu, 1)

            def ada_rows(g):
                act.wait_ge(proj_done, 2 * (T_WO + GROUP * (g + 1)))
                act.wait_ge(mod_turned, ADA_BLOCKS + g - 1)
                A(mod_row2[:, g % 2, :], ada_bank(g)[0:18, 0:2 * P], ACT.Copy).then_inc(act_evac, 4)

            def side_store(e):
                bk = bank[2 + e % 2]
                act.wait_ge(side_done, e + 1)
                if e < 4:
                    ins = A(ki_pt[:, 4 * e:4 * e + 4, :], bk[:, :].rearrange("p (a c) -> p a c", a=4), ACT.Copy)
                elif e == 4:
                    ins = A(isr[:, :, :, :].rearrange("p b g h -> p (b g h)"), bk[:, 0:P], ACT.Relu)
                elif e == 5:
                    ins = A(srow[:, 0:PAST], bk[0:NS, 0:PAST], ACT.Copy)
                else:
                    ins = A(ts_b[:, [0, 1, 3, 2][e - 6], :] if e < 10 else ts_a[:, e - 10, :], bk[0:NS, :], ACT.Copy)
                ins.then_inc(side_read, 1)

            for i in range(T_PAIR):
                for half in range(2):
                    act.wait_ge(proj_done, 2 * i + half + 1)
                    lo, hi = half * HALF, min(half * HALF + HALF, SEQ)
                    if i == T_SMALL:
                        A(zsm[:, half * HALF:(half + 1) * HALF], bank[half][:, 0:HALF], ACT.Copy).then_inc(act_evac, 1)
                        continue
                    c = i - T_QI
                    if i == T_QI:
                        act.wait_ge(zeroed, 2)
                    A(q_idx[0:64, 2 * c, lo:hi], bank[half + 4 * par(i)][0:64, 0:hi - lo], ACT.Copy)
                    last = A(q_idx[64:128, 2 * c + 1, lo:hi], bank[half + 4 * par(i)][64:128, 0:hi - lo], ACT.Copy)
                    if half == 1:
                        last = A(z_s[:, 24 + c, :], bank[1 + 4 * par(i)][:, hi - lo:HALF], ACT.Copy)
                    last.then_inc(act_evac, 1)
                round_w(i + 2)
                if i == 1:
                    act.wait_ge(sm_ready, 1)
                    rows = slice(ROW_FL, ROW_FL + H)
                    link(A(lf[rows, 2, :], lf[rows, 1, :], ACT.Exp, scale=-1.0))
                    A(lf[rows, 3, :], lf[rows, 2, :], ACT.Ln, bias=1.0).then_inc(lf_step, 1)
                if i == 3:
                    act.wait_ge(smt_done, 1)
                    A(abias[:, :], bank[2][:, :], ACT.Copy)
                    A(sm_tok_s[:, :], bank[3][0:NS, 0:P], ACT.Copy).then_inc(smt_ready, 1)

            for p, s in ITERATIONS:
                U = SLOTS * (p - 1) + s
                before = slot_before(p, s)
                if before in SIDE:
                    side_store(SIDE.index(before))
                for i in split_at(p, s):
                    round_w(i)
                if s in HALVES_AT and (p, s) < (N_PAIRS + 1, 4):
                    kd, half = divmod(HALVES_AT.index(s), 2)
                    if p < N_PAIRS:
                        store_z(p, kd, half)
                    else:
                        store_gate(3 * (p - N_PAIRS) + kd, half)
                if p < N_PAIRS and s in (2, 4):
                    square_tok(p, s // 2 - 1)
                if p == 0:
                    for n in range(3 * s, 3 * s + 3):
                        relu_scores(n)
                if 0 <= U < N_UNITS:
                    exps(U)
                if 0 <= U - 2 < N_UNITS:
                    store_pt(U - 2)
                if s == 2 and p >= 2:
                    round_o(p - 2)
                if p < N_PAIRS:
                    if s == 4:
                        store_back(p, 0)
                    if s == K_BACK:
                        store_back(p, 1)
                if s == 0 and 1 <= p <= N_PAIRS:
                    store_v(p - 1)
            def row_exps():
                for m in range(2):
                    act.wait_ge(rows_lg, m + 1)
                    A(rows_l[:, m, :], rows_l[:, m, :], ACT.Exp, bias=col64[:, 2 + m:3 + m],
                      accum_out=col64[:, 4 + m:5 + m]).then_inc(rows_e, 1)

            def store_pts():
                act.wait_ge(pts_turned, 1)
                act.wait_ge(s_consts, 3)
                A(ptz[:, :, :].rearrange("p g (b x) -> p g b x", b=NS)[:, :, :, 0:H],
                  bank[6][:, 0:256].rearrange("p (g b h) -> p g b h", g=2 * NPAGE, b=NS), ACT.Copy).then_inc(pts_ready, 1)
                A(s8[:, 6:8, :].rearrange("p a h -> p (a h)"), bank[7][0:NS, 0:16], ACT.Copy).then_inc(pts_ready, 1)

            for i in range(T_GATE + 5, T_WO):
                if i == T_GATE + 13:
                    row_exps()
                if i == T_GATE + 14:
                    store_pts()
                for half in range(2):
                    store_gate(i - T_GATE, half)
                round_w(i + 2)
            for j in range(2 * NCH):
                if j == 0:
                    act.wait_ge(act_evac, act_evac_value(T_WO - 1, 1))
                A(gate[:, j, :], gate[:, j, :], ACT.Sigmoid).then_inc(gates_ready, 1)
            act.wait_ge(os_done, 2)
            A(o_hi[:, :, SEQ:T], bank[6][:, 256:256 + 8 * NS].rearrange("p (c b) -> p c b", b=NS), ACT.Copy).then_inc(os_hi, 1)

            round_w(T_WO + 2)
            round_w(T_WO + 3)
            def round_ahead(i):
                if i < T_MLP + 2:
                    round_w(i)

            for g in range(2 * NCH):
                i = T_WO + GROUP * g
                if g:
                    ada_rows(g - 1)
                    round_ahead(i - GROUP + 6)
                if g < NCH:
                    for half in range(2):
                        act.wait_ge(mf_ready, 2 * g + half + 1)
                        if g == 0 and half == 0:
                            act.wait_ge(proj_done, 2 * T_WO)
                        A(h_hi[:, g, half * HALF:(half + 1) * HALF], mix[:, half, 2, :], ACT.Copy).then_inc(mf_hi, 1)
                if g > NCH:
                    act.wait_ge(dve_evac, 2 * g)
                    square(1, g - NCH - 1)
                round_ahead(i + 4)
                round_ahead(i + 5)
            ada_rows(2 * NCH - 1)
            A(stat[0:1, 39:40], ones[0:1, 0:1], ACT.Ln)
            act.wait_ge(dve_evac, 4 * NCH)
            square(1, NCH - 1)
            inverse_root(1)
            round_h(1)

            def round_loop(i, it):
                act.wait_ge(raw_landed[i % RAW], it * 16 + landed_value(i))
                act.wait_ge(proj_done, it * 8 + 2 * (i - SPL + 1))
                A(w_hi[:, i % SPL], raw[:, i % RAW], ACT.Copy).then_inc(hi_ready, 1)

            def up_tile(q, b, it):
                n = 32 * q + 2 * b
                for half in range(2):
                    act.wait_ge(proj_done, it * 8 + (2 * (T_MLP + 32 * q + b) + half + 1))
                    if q or b >= 2:
                        act.wait_ge(u_lo_ready, it * 8 + (n + half - 3))
                    A(u_f[:, 2 * (b % 2) + half, :], bank[half + 4 * ((T_MLP + b) % 2)][:, 0:HALF], ACT.Relu).then_inc(act_evac, 1)
                round_loop(T_MLP + 32 * q + b + 2, it)
                for half in range(2):
                    act.wait_ge(u_sq, it * 8 + (n + half + 1))
                    A(u_hi[:, bass.ds(it * 4 + b, 1), half * HALF:(half + 1) * HALF], u_f[:, 2 * (b % 2) + half:2 * (b % 2) + half + 1, :],
                      ACT.Copy).then_inc(u_hi_ready, 1)

            for q in range(2):
                if q == 0:
                    for b in range(4):
                        up_tile(q, b, 0)
                    with act.Fori(1, 4) as it:
                        for b in range(4):
                            act.wait_ge(u_lo_ready, it * 8 + (2 * b - 2))
                            up_tile(q, b, it)
                else:
                    with act.Fori(0, 4) as it:
                        for b in range(4):
                            up_tile(q, b, it)
                last = 3 if q else 4
                with act.Fori(0, last) as it:
                    for b in range(4):
                        round_loop(T_MLP + 32 * q + 16 + b + 2, it)

            def store_y(j):
                act.wait_ge(y_done, j + 1)
                A(y_tok[:, :, j * P:(j + 1) * P], bank[j % 2][:, :].rearrange("p (t c) -> p t c", t=QB), ACT.Copy).then_inc(y_act, 1)

            round_loop(T_MLP + 32 + 16 + 2, 3)
            store_y(0)
            round_loop(T_MLP + 32 + 16 + 3, 3)
            for j in range(2, NCH, 2):
                store_y(j)
            act.wait_ge(y_done, NCH)
            A(y_stok[:, 0:SEQ], bank[4][0:NS, :], ACT.Copy)
            A(y_stok[:, SEQ:DM], bank[5][0:NS, :], ACT.Copy).then_inc(y_act, 1)

        @block.vector
        def _(dve):
            steps = [0]

            def link(ins):
                steps[0] += 1
                ins.then_inc(dve_self, 1)
                dve.wait_ge(dve_self, steps[0])

            dve.wait_ge(small_landed, 16 * N_SMALL)
            dve.tensor_scalar(gq[:, :], g_col[:, :], QK_SCALE, None, ALU.mult)
            dve.wait_ge(vec_ready, 1)
            dve.tensor_tensor(cond_t[:, :, :].rearrange("p k c -> p (k c)"), bank[7][:, 64:136], sig[:, :], ALU.mult).then_inc(cond_ready, 1)
            for j in range(1, NCH, 2):
                dve.wait_ge(xt_done, j + 1)
                dve.tensor_copy(x_t[:, j, 0:SEQ], bank[j % 4][:, :]).then_inc(xt_dve, 1)
            dve.tensor_copy(x_t[:, :, SEQ:T], bank[6][:, 0:64].rearrange("p (j c) -> p j c", c=NS)).then_inc(xt_dve, 1)

            def norm_root(n):
                dve.wait_ge(sq_used, NCH * (n + 1))
                dve.tensor_scalar(nbuf[:, 0, 0:HALF], bank[[4, 2][n]][:, 0:HALF], 1.0 / DM, EPS, ALU.mult, ALU.add)
                dve.tensor_scalar(nbuf[:, 0, HALF:T], bank[[5, 3][n]][:, 0:HALF], 1.0 / DM, EPS, ALU.mult, ALU.add).then_inc(ms_ready, 1)
                dve.wait_ge(rs_ready, n + 1)
                link(dve.tensor_tensor(nbuf[:, 2, :], nbuf[:, 0, :], nbuf[:, 1, :], ALU.mult))
                link(dve.tensor_tensor(nbuf[:, 2, :], nbuf[:, 2, :], nbuf[:, 1, :], ALU.mult))
                link(dve.tensor_scalar(nbuf[:, 2, :], nbuf[:, 2, :], -0.5, 1.5, ALU.mult, ALU.add))
                link(dve.tensor_tensor(nbuf[:, 1, :], nbuf[:, 1, :], nbuf[:, 2, :], ALU.mult))

            norm_root(0)

            dve.wait_ge(cond_hi, 1)
            dve.tensor_tensor(cond_h[:, :, 9:18], cond_t[:, :, :], cond_h[:, :, 0:9].bitcast(F32), ALU.subtract).then_inc(cond_lo, 1)

            def mod_add(b, block_at, value):
                dve.wait_ge(mod_turned, value)
                dve.tensor_tensor(mod_t[:, block_at, :], bank[2 + b][:, 0:36].rearrange("p (q c) -> p q c", c=9),
                                  vec_t[:, block_at].unsqueeze(2).to_broadcast([P, 4, 9]), ALU.add).then_inc(mod_ready, 1)

            for t in range(ADA_BLOCKS):
                mod_add(t % 2, slice(4 * t, 4 * t + 4), t + 1)

            def mod_pair(g):
                at = slice(4 * ADA_BLOCKS + 2 * g, 4 * ADA_BLOCKS + 2 * g + 2)
                turned = ada_bank(g)[:, 2 * P:2 * P + 36].rearrange("p (u c) -> p u c", u=2)
                dve.wait_ge(mod_turned, ADA_BLOCKS + g + 1)
                link(dve.tensor_tensor(mod_t[:, at, :], turned[:, :, 0:9], vec_t[:, at].unsqueeze(2).to_broadcast([P, 2, 9]), ALU.add))
                dve.tensor_tensor(mod_t[:, at, :], mod_t[:, at, :], turned[:, :, 9:18], ALU.add).then_inc(mod_ready, 1)

            def norm_apply(n):
                shift, scale = 24 * n, 24 * n + 8
                dve.wait_ge(mod_ready, ADA_BLOCKS + 12 * n)
                link(dve.tensor_scalar(amul[:, :, :], mod_t[:, scale:scale + NCH, :], 1.0, None, ALU.add))
                link(dve.tensor_tensor(amul[:, :, :], amul[:, :, :],
                                       vec_t[:, 48 + 8 * n:56 + 8 * n].unsqueeze(2).to_broadcast([P, NCH, 9]), ALU.mult))

                def rest(j):
                    dve.wait_ge(h_hi_ready, (NCH + 1) * n + j + 2)
                    dve.tensor_tensor(h_lo[:, j, 0:SEQ], nrm[:, j % 2, 0:SEQ], h_hi[:, j, 0:SEQ].bitcast(F32),
                                      ALU.subtract).then_inc(h_lo_ready, 1)

                link(dve.tensor_tensor(nsm[:, 0], x_t[:, :, SEQ:T], nbuf[:, 1, SEQ:T].unsqueeze(1).to_broadcast([P, NCH, NS]), ALU.mult))
                link(dve.tensor_tensor(nsm[:, 0], nsm[:, 0], amul[:, :, 1:9], ALU.mult))
                dve.tensor_tensor(nsm[:, 0], nsm[:, 0], mod_t[:, shift:shift + NCH, 1:9], ALU.add).then_inc(nf_ready, 1)
                dve.wait_ge(nf_ready, (NCH + 1) * n + 1)
                for j in range(NCH):
                    if j >= 2:
                        dve.wait_ge(h_lo_ready, (NCH + 1) * n + j)
                    link(dve.tensor_tensor(nrm[:, j % 2, 0:SEQ], x_t[:, j, 0:SEQ], nbuf[:, 1, 0:SEQ], ALU.mult))
                    dve.tensor_scalar(nrm[:, j % 2, 0:SEQ], nrm[:, j % 2, 0:SEQ], amul[:, j, 0:1],
                                      mod_t[:, shift + j, 0:1], ALU.mult, ALU.add).then_inc(nf_ready, 1)
                    if j == 0:
                        dve.wait_ge(h_hi_ready, (NCH + 1) * n + 1)
                        dve.tensor_tensor(h_lo[:, :, SEQ:T], nsm[:, 0], h_hi[:, :, SEQ:T].bitcast(F32), ALU.subtract).then_inc(h_lo_ready, 1)
                    else:
                        rest(j - 1)
                rest(NCH - 1)

            def rest_w(i):
                dve.wait_ge(hi_ready, i + 1)
                dve.tensor_tensor(parts(i)[1], raw[:, i % RAW], parts(i)[0].bitcast(F32), ALU.subtract).then_inc(lo_ready, 1)

            rest_w(0)
            rest_w(1)
            norm_apply(0)

            def index_sum(n):
                qb, h = 1 + n // H, n % H
                w = width(qb)
                dve.wait_ge(idx_relu, n + 1)
                out = sel[:, sel_at[qb]:sel_at[qb] + w]
                if h == 0:
                    ins = dve.tensor_scalar(out, rbuf[:, n % 2, 0:w], wi_tok[:, qb, h:h + 1], 0.0, ALU.mult, ALU.add)
                else:
                    dve.wait_ge(idx_sum, n)
                    ins = dve.scalar_tensor_tensor(out=out, in0=rbuf[:, n % 2, 0:w], scalar=wi_tok[:, qb, h:h + 1],
                                                   in1=out, op0=ALU.mult, op1=ALU.add)
                ins.then_inc(idx_sum, 1)

            def top_round(r):
                rounds = TOPK_P // 8
                blocks = (1, 3) if r < rounds else (2,)
                views = [(sel[:, sel_at[qb]:sel_at[qb] + width(qb)], top8) for qb, top8 in zip(blocks, (m8, m8b))]
                dve.wait_ge(sel_ready, 3)
                done = steps[0]
                for blk, top8 in views:
                    dve.max(out=top8[:, :], in_=blk).then_inc(dve_self, 1)
                for n, (blk, top8) in enumerate(views):
                    dve.wait_ge(dve_self, done + n + 1)
                    dve.match_replace(out=blk, in_to_replace=top8[:, :], in_values=blk, imm_value=TAKEN).then_inc(dve_self, 1)
                steps[0] += 2 * len(views)
                dve.wait_ge(dve_self, steps[0])
                if r % rounds == rounds - 1:
                    for (blk, _), qb in zip(views, blocks):
                        w = width(qb)
                        link(dve.tensor_scalar(blk, blk, TAKEN, 1.0, ALU.is_equal, ALU.subtract))
                        link(dve.scalar_tensor_tensor(out=blk, in0=blk, scalar=-MASK, in1=dist[:, SEQ - w:SEQ],
                                                      op0=ALU.mult, op1=ALU.add))

            def logits(U):
                p, hh, qb = U // 8, U // 4 % 2, U % 4
                m, c = pair_mixer(p)
                w = width(qb)
                out, s_bank = lg[:, U % 3, :], bank[4 + U % 2]
                mx, nm = stat[:, U % 8:U % 8 + 1], stat[:, 8 + U % 8:9 + U % 8]
                if U >= 3:
                    dve.wait_ge(pt_done, U - 2)
                if m == 1:
                    if U == 32:
                        dve.wait_ge(stored, 64)
                    src = sel[:, sel_at[qb]:sel_at[qb] + w] if qb else dist[:, SEQ - P:SEQ]
                    link(dve.tensor_scalar(abias[:, 0:w], src, SLOPES[2 * c + hh], None, ALU.mult))
                    dve.wait_ge(s_done, U + 1)
                    link(dve.tensor_tensor_reduce(out[:, 0:w], s_bank[:, 0:w], abias[:, 0:w], 1.0, TAKEN, ALU.add, ALU.max, mx))
                else:
                    dve.wait_ge(s_done, U + 1)
                    start = TAKEN
                    if qb:
                        link(dve.tensor_tensor_reduce(out[:, 0:w - P], s_bank[:, 0:w - P], fbc[:, p % 2, hh, 0:w - P], 1.0, TAKEN,
                                                      ALU.add, ALU.max, stat[:, 24:25]))
                        start = stat[:, 24:25]
                    link(dve.tensor_tensor_reduce(out[:, w - P:w], s_bank[:, w - P:w], fdiag[:, hh, w - P:w], 1.0, start,
                                                  ALU.add, ALU.max, mx))
                dve.tensor_scalar(nm, mx, -1.0, None, ALU.mult).then_inc(lg_ready, 1)

            def probs(U):
                w = width(U % 4)
                dve.wait_ge(e_ready, U + 1)
                link(dve.reciprocal(stat[:, 25:26], stat[:, 16 + U % 8:17 + U % 8]))
                dve.tensor_scalar(lg[:, U % 3, 0:w], lg[:, U % 3, 0:w], stat[:, 25:26], None, ALU.mult).then_inc(p_ready, 1)

            def mean_squares(p, kd):
                dve.wait_ge(tok_sq, 2 * p + kd + 1)
                link(dve.tensor_reduce(ms8[:, :], sq[:, :].rearrange("p (g d) -> p g d", d=HD), AX_X, ALU.add))
                dve.tensor_scalar(ms8[:, :], ms8[:, :], 1.0 / HD, EPS, ALU.mult, ALU.add).then_inc(ms_tok, 1)

            def normalize(p, kd):
                m = pair_mixer(p)[0]
                dve.wait_ge(rstd_tok, 2 * p + kd + 1)
                if p >= 1:
                    dve.wait_ge(back_done, 2 * (p - 1) + kd + 1)
                    if kd == 1:
                        dve.wait_ge(k_stored, 16 * p)
                out = tok[:, kd, :].rearrange("p (g d) -> p g d", d=HD)
                dve.tensor_tensor(out, bank[2][:, :].rearrange("p (g d) -> p g d", d=HD),
                                  rs8[:, :].unsqueeze(2).to_broadcast([P, 8, HD]), ALU.mult).then_inc(tok_read, 1)
                if kd == 1:
                    dve.wait_ge(tok_read, 2 * p + 2)
                    dve.tensor_tensor(out, out, gk_row[:, m, :].unsqueeze(1).to_broadcast([P, 8, HD]), ALU.mult).then_inc(tok_ready, 1)

            def rest_o(p):
                dve.wait_ge(o_hi_ready, p + 1)
                dve.tensor_tensor(o_lo[:, p, 0:SEQ], bank[7][:, :], o_hi[:, p, 0:SEQ].bitcast(F32), ALU.subtract).then_inc(o_lo_ready, 1)

            def padded_queries():
                dve.wait_ge(s_consts, 1)
                dve.tensor_copy(qzs[0:64, :, :, 0], z_s[0:64, 24:28, :].rearrange("p c b -> p b c"))
                dve.tensor_copy(qzs[64:128, :, :, 1], z_s[64:128, 24:28, :].rearrange("p c b -> p b c")).then_inc(qzs_ready, 1)
                dve.tensor_scalar(gq_row[:, :, :], gq_row[:, :, :], QK_SCALE, None, ALU.mult)
                dve.tensor_scalar(s8[:, 8, :], sm_tok_s[:, 64:64 + H], H ** -0.5, QK_SCALE, ALU.mult, ALU.mult).then_inc(wi_ready, 1)
                dve.wait_ge(wi_ready, 1)

            def index_sum_s():
                dve.wait_ge(side_read, 5)
                dve.wait_ge(wbc_landed, 16)
                link(dve.tensor_tensor(isr[:, :, :, :], isr[:, :, :, :], wbc[:, :, :].unsqueeze(2).to_broadcast([P, NS, NPAGE, H]), ALU.mult))
                dve.tensor_reduce(iss[:, :, :], isr[:, :, :, :], AX_X, ALU.add).then_inc(is_sum, 1)

            def heads(row):
                return row.rearrange("p (g d) -> p g d", d=HD)

            def sample_square(n):
                row = [ts_b, ts_a][n // 2][:, n % 2, :]
                dve.wait_ge(side_read, [7, 8, 11, 12][n])
                if n == 0:
                    dve.wait_ge(lg_ready, 8 * 4)
                link(dve.tensor_tensor(sqs[:, :], row, row, ALU.mult))
                link(dve.tensor_reduce(s8[:, n, :], heads(sqs[:, :]), AX_X, ALU.add))
                dve.tensor_scalar(s8[:, n, :], s8[:, n, :], 1.0 / HD, EPS, ALU.mult, ALU.add).then_inc(ts_ms, 1)

            def sample_norm(n):
                m = n // 2
                dve.wait_ge(ts_rs, n + 1)
                view = heads([ts_b, ts_a][m][:, n % 2, :])
                gain = (gk_row[0:NS, m, :] if n % 2 else gq_row[:, m, :]).unsqueeze(1).to_broadcast([NS, H, HD])
                link(dve.tensor_tensor(view, view, s8[:, 4 + n, :].unsqueeze(2).to_broadcast([NS, H, HD]), ALU.mult))
                dve.tensor_tensor(view, view, gain, ALU.mult).then_inc(ts_norm, 1)

            def own_key(m):
                ts = [ts_b, ts_a][m]
                dve.wait_ge(ts_norm, 2 * m + 2)
                link(dve.tensor_tensor(sqs[:, :], ts[:, 0, :], ts[:, 1, :], ALU.mult))
                dve.tensor_reduce(s8[:, 9 + m, :], heads(sqs[:, :]), AX_X, ALU.add).then_inc(own_done, 1)
                dve.wait_ge(own_done, m + 1)

            def own_index():
                dve.wait_ge(side_read, 9)
                link(dve.tensor_tensor(heads(sqs[:, :]), heads(ts_b[:, 3, :]), sm_tok_s[:, 0:HD].unsqueeze(1).to_broadcast([NS, H, HD]), ALU.mult))
                link(dve.tensor_reduce(s8[:, 11, :], heads(sqs[:, :]), AX_X, ALU.add))
                link(dve.scalar_tensor_tensor(out=s8[:, 11, :], in0=s8[:, 11, :], scalar=0.0, in1=s8[:, 8, :],
                                              op0=ALU.max, op1=ALU.mult))
                link(dve.tensor_reduce(srow[:, PAST:L], s8[:, 11, :], AX_X, ALU.add))

            def top_s(rounds, last):
                for _ in range(rounds):
                    link(dve.max(out=m8[0:NS, :], in_=srow[:, :]))
                    link(dve.match_replace(out=srow[:, :], in_to_replace=m8[0:NS, :], in_values=srow[:, :], imm_value=TAKEN))
                if last:
                    dve.wait_ge(s_consts, 2)
                    link(dve.tensor_scalar(srow[:, :], srow[:, :], TAKEN, 1.0, ALU.is_equal, ALU.subtract))
                    dve.scalar_tensor_tensor(out=srow[:, :], in0=srow[:, :], scalar=-MASK, in1=dist_s[:, :],
                                             op0=ALU.mult, op1=ALU.add).then_inc(dist_ready, 1)

            SAMPLE_STEPS = {
                (1, 6): padded_queries,
                (4, 0): index_sum_s,
                (5, 7): lambda: sample_square(0), (6, 0): lambda: sample_norm(0),
                (6, 1): lambda: sample_square(1), (6, 2): lambda: sample_norm(1),
                (6, 3): lambda: own_key(0), (7, 0): own_index,
                **{(7, s): lambda: top_s(1, False) for s in range(1, TOPK_S // 8)}, (8, 0): lambda: top_s(1, True),
                (8, 3): lambda: sample_square(2), (8, 4): lambda: sample_norm(2),
                (8, 5): lambda: sample_square(3), (8, 6): lambda: sample_norm(3), (8, 7): lambda: own_key(1),
            }

            rows = slice(ROW_FL, ROW_FL + H)
            dve.wait_ge(act_evac, 2)
            dve.tensor_copy(ki2[0:64, :], zsm[0:64, 0:SEQ])
            dve.tensor_copy(ki2[64:128, :], zsm[0:64, 0:SEQ])
            link(dve.tensor_scalar(lf[rows, 0, :], zsm[rows, :], bforget[rows, 0:1], None, ALU.add))
            link(dve.tensor_scalar(lf[rows, 1, :], lf[rows, 0, :], -1.0, None, ALU.mult))
            dve.tensor_tensor(lf[rows, 1, :], lf[rows, 1, :], lf[rows, 0, :], ALU.max).then_inc(sm_ready, 1)
            rest_w(2)
            rest_w(3)
            dve.wait_ge(lf_step, 1)
            dve.scalar_tensor_tensor(out=zsm[rows, :], in0=lf[rows, 0, :], scalar=0.0, in1=lf[rows, 3, :],
                                     op0=ALU.min, op1=ALU.subtract).then_inc(sm_ready, 2)
            dve.wait_ge(sm_ready, 3)
            link(dve.tensor_scalar(lf[rows, 0, :], zsm[rows, :], -1.0, None, ALU.mult))
            dve.tensor_tensor_scan(lf[rows, 1, 0:SEQ], ones[rows, 0:1].to_broadcast([H, SEQ]), lf[rows, 0, 0:SEQ], 0.0,
                                   ALU.mult, ALU.add).then_inc(negf_ready, 1)
            rest_w(4)
            dve.wait_ge(smt_ready, 1)
            dve.tensor_scalar(wi_tok[:, :, :], abias[:, :].rearrange("p (t c) -> p t c", t=QB)[:, :, 64:64 + H],
                              H ** -0.5, QK_SCALE, ALU.mult, ALU.mult).then_inc(sm_ready, 1)
            dve.wait_ge(sm_ready, 4)
            rest_w(5)
            rest_w(6)

            for p, s in ITERATIONS:
                U = SLOTS * (p - 1) + s
                if p == 0:
                    for n in range(3 * s, 3 * s + 3):
                        index_sum(n)
                if 1 <= p <= 4 and s == 0:
                    dve.wait_ge(fbc_landed[(p - 1) % 2], 32 * ((p - 1) // 2 + 1))
                    for hh in range(2):
                        link(dve.tensor_tensor(fdiag[:, hh, :].rearrange("p (t c) -> p t c", t=QB),
                                               fbc[:, (p - 1) % 2, hh, :].rearrange("p (t c) -> p t c", t=QB),
                                               cmask[:, :].unsqueeze(1).to_broadcast([P, QB, P]), ALU.add))
                if 0 <= U - 1 < N_UNITS:
                    probs(U - 1)
                if 0 <= U < N_UNITS:
                    logits(U)
                if p < N_PAIRS:
                    if s in (2, 4):
                        mean_squares(p, s // 2 - 1)
                    if s in (3, 5):
                        normalize(p, s // 2 - 1)
                if s == 3 and p >= 2:
                    rest_o(p - 2)
                if 0 <= U < 2 * TOPK_P // 8:
                    top_round(U)
                if (p, s) in SAMPLE_STEPS:
                    SAMPLE_STEPS[p, s]()
            def sample_keys(n):
                m, b = n // NS, n % NS
                if n % 2 == 0:
                    dve.wait_ge(kv_landed[0], kv_value(n))
                    if n >= 2:
                        dve.wait_ge(prod_used, n - 1)
                    dve.tensor_tensor(prod0[:, :, :], kv0[:, :, :], qbc0[:, :].unsqueeze(1).to_broadcast([P, NPAGE, SEQ]), ALU.mult)\
                        .then_inc(prod_dve, 1)
                dve.wait_ge([prod_dve, prod_pool][n % 2], n // 2 + 1)
                dve.tensor_reduce(lgs[:, m, :, H * b:H * b + H], prod[n % 2][:, :, :].rearrange("p g (h d) -> p g h d", d=HD), AX_X, ALU.add)\
                    .then_inc(prod_used, 1)

            def rows_logits():
                dve.wait_ge(rows_turned, 1)
                own = bank[7][0:64, 0:24]
                for j in range(3):
                    link(dve.tensor_tensor_reduce(pself[:, 0, :], own[:, 8 * j:8 * j + 8], pick[:, :], 1.0, 0.0, ALU.mult, ALU.add,
                                                  col64[:, 8 + j:9 + j]))
                link(dve.tensor_tensor_reduce(pself[:, 0, :], slope_rows[:, :], pick[:, :], 1.0, 0.0, ALU.mult, ALU.add, col64[:, 11:12]))
                dve.tensor_copy(rows_f[:, 0:PAST], bank[7][0:64, P:P + PAST])
                link(dve.tensor_copy(rows_f[:, PAST:L], col64[:, 10:11]))
                link(dve.tensor_tensor_scan(rows_l[:, 0, :], ones[0:64, 0:1].to_broadcast([64, L]), rows_f[:, :], 0.0, ALU.mult, ALU.add))
                dve.tensor_tensor(rows_f[:, 0:PAST], bank[2][0:64, 0:PAST], rows_l[:, 0, 0:PAST], ALU.subtract)
                link(dve.tensor_tensor(rows_f[:, PAST:L], col64[:, 8:9], rows_l[:, 0, PAST:L], ALU.subtract))
                dve.tensor_copy(rows_l[:, 0, :], rows_f[:, :])
                link(dve.tensor_reduce(col64[:, 0:1], rows_f[:, :], AX_X, ALU.max))
                dve.tensor_scalar(col64[:, 2:3], col64[:, 0:1], -1.0, None, ALU.mult).then_inc(rows_lg, 1)
                dve.wait_ge(dist_spread, 1)
                dve.tensor_copy(rows_f[:, 0:PAST], bank[3][0:64, 0:PAST])
                link(dve.tensor_copy(rows_f[:, PAST:L], col64[:, 9:10]))
                link(dve.scalar_tensor_tensor(out=rows_l[:, 1, :], in0=bank[6][0:64, 0:L], scalar=col64[:, 11:12], in1=rows_f[:, :],
                                              op0=ALU.mult, op1=ALU.add))
                link(dve.tensor_reduce(col64[:, 1:2], rows_l[:, 1, :], AX_X, ALU.max))
                dve.tensor_scalar(col64[:, 3:4], col64[:, 1:2], -1.0, None, ALU.mult).then_inc(rows_lg, 1)

            def rows_probs():
                for m in range(2):
                    dve.wait_ge(rows_e, m + 1)
                    link(dve.reciprocal(col64[:, 6 + m:7 + m], col64[:, 4 + m:5 + m]))
                    dve.tensor_scalar(rows_l[:, m, :], rows_l[:, m, :], col64[:, 6 + m:7 + m], None, ALU.mult).then_inc(rows_p, 1)
                    dve.wait_ge(rows_p, m + 1)
                    last = dve.tensor_scalar(pself[:, m, :], pick[:, :], rows_l[:, m, PAST:L], None, ALU.mult)
                last.then_inc(rows_p, 1)

            def own_value(m):
                row = heads([ts_b, ts_a][m][:, 2, :])
                if m == 0:
                    dve.wait_ge(pts_ready, 2)
                    dve.wait_ge(stored, 16 * 8)
                dve.tensor_tensor(row, row, s8[:, 6 + m, :].unsqueeze(2).to_broadcast([NS, H, HD]), ALU.mult)

            def own_features(m):
                dve.wait_ge(pv_used, NS * (m + 1))
                dve.tensor_tensor(heads(om[:, m, :]), heads(bank[2 + m][0:64, :]), pick[:, :].unsqueeze(2).to_broadcast([64, H, HD]), ALU.mult)\
                    .then_inc(om_ready, 1)

            dve.wait_ge(lo_ready, T_GATE + 7)
            n = 0
            for i in range(T_GATE + 5, T_WO):
                for _ in range(KEYS_AT[i - T_GATE - 5] if i - T_GATE - 5 < len(KEYS_AT) else 0):
                    sample_keys(n)
                    n += 1
                if i == T_GATE + 12:
                    rows_logits()
                if i == T_GATE + 13:
                    rows_probs()
                if i == T_GATE + 15:
                    own_value(0)
                    own_value(1)
                rest_w(i + 2)
            for m in range(2):
                own_features(m)
            dve.wait_ge(os_hi, 1)
            dve.tensor_tensor(o_lo[:, :, SEQ:T], bank[6][:, 256:256 + 8 * NS].rearrange("p (c b) -> p c b", b=NS),
                              o_hi[:, :, SEQ:T].bitcast(F32), ALU.subtract).then_inc(os_lo, 1)

            def rest_ahead(i):
                if i < T_MLP + 2:
                    dve.wait_ge(lo_ready, i)
                    rest_w(i)

            rest_w(T_WO + 2)
            rest_w(T_WO + 3)
            for g in range(NCH):
                dve.wait_ge(gates_ready, 2 * g + 2)
                if g:
                    mod_pair(g - 1)
                for half in range(2):
                    cols = slice(half * HALF, (half + 1) * HALF)
                    b = half + 4 * (g % 2)
                    dve.wait_ge(proj_done, 2 * (T_WO + GROUP * g) + half + 1)
                    dve.tensor_tensor(mix[:, half, 0, :], bank[b + 2][:, 0:HALF], gate[:, 2 * g, cols], ALU.mult)
                    dve.tensor_tensor(mix[:, half, 1, :], bank[b][:, 0:HALF], gate[:, 2 * g + 1, cols], ALU.mult).then_inc(dve_evac, 1)
                    dve.wait_ge(dve_evac, 2 * g + half + 1)
                    dve.tensor_tensor(mix[:, half, 2, :], mix[:, half, 0, :], mix[:, half, 1, :], ALU.add).then_inc(mf_ready, 1)
                for half in range(2):
                    cols = slice(half * HALF, (half + 1) * HALF)
                    dve.wait_ge(mf_hi, 2 * g + half + 1)
                    dve.tensor_tensor(h_lo[:, g, cols], mix[:, half, 2, :], h_hi[:, g, cols].bitcast(F32), ALU.subtract).then_inc(mf_lo, 1)
                rest_ahead(T_WO + GROUP * g + 4)
                rest_ahead(T_WO + GROUP * g + 5)

            def add_gated(bk, half, m, vec, done):
                n = HALF if half == 0 else SEQ - HALF
                xs = x_t[:, m, half * HALF:half * HALF + n]
                g = mod_t[:, vec, :]
                if half:
                    dve.wait_ge(dve_evac, done * 2 + (2 * NCH + 1))
                    dve.tensor_tensor(xs8[:, 0:1, :], bk[:, n:HALF].unsqueeze(1), g[:, :, 1:9], ALU.mult).then_inc(xs_ready, 1)
                last = dve.scalar_tensor_tensor(out=xs, in0=bk[:, 0:n].unsqueeze(1), scalar=g[:, 0, 0:1], in1=xs,
                                                op0=ALU.mult, op1=ALU.add)
                if half:
                    dve.wait_ge(xs_ready, done + 1)
                    last = dve.tensor_tensor(x_t[:, m, SEQ:T], x_t[:, m, SEQ:T], xs8[:, 0:1, :], ALU.add)
                last.then_inc(dve_evac, 1)

            for g in range(NCH, 2 * NCH):
                m = g - NCH
                mod_pair(g - 1)
                dve.wait_ge(mod_ready, ADA_BLOCKS + NCH - 1)
                for half in range(2):
                    dve.wait_ge(proj_done, 2 * (T_WO + GROUP * g) + half + 1)
                    add_gated(bank[half + 4 * (g % 2)], half, slice(m, m + 1), slice(16 + m, 17 + m), m)
                rest_ahead(T_WO + GROUP * g + 4)
                rest_ahead(T_WO + GROUP * g + 5)
            mod_pair(2 * NCH - 1)
            dve.wait_ge(mod_ready, ADA_BLOCKS + 2 * NCH)
            norm_root(1)
            norm_apply(1)

            def rest_loop(i, it):
                dve.wait_ge(hi_ready, it * 4 + (i + 1))
                dve.tensor_tensor(w_lo[:, i % SPL], raw[:, i % RAW], w_hi[:, i % SPL].bitcast(F32), ALU.subtract).then_inc(lo_ready, 1)

            for q in range(2):
                with dve.Fori(0, 4) as it:
                    for b in range(4):
                        n = 32 * q + 2 * b
                        for half in range(2):
                            uf = u_f[:, 2 * (b % 2) + half, :]
                            dve.wait_ge(act_evac, it * 8 + (2 * (T_WO + 4 * NCH) + n + half + 1))
                            dve.tensor_tensor(uf, uf, uf, ALU.mult).then_inc(u_sq, 1)
                        rest_loop(T_MLP + 32 * q + b + 2, it)
                        for half in range(2):
                            slot = 2 * (b % 2) + half
                            cols = slice(half * HALF, (half + 1) * HALF)
                            dve.wait_ge(u_hi_ready, it * 8 + (n + half + 1))
                            dve.tensor_tensor(u_lo[:, bass.ds(it * 4 + b, 1), cols], u_f[:, slot:slot + 1, :],
                                              u_hi[:, bass.ds(it * 4 + b, 1), cols].bitcast(F32), ALU.subtract).then_inc(u_lo_ready, 1)

                def down_add(it, mb):
                    for half in range(2):
                        dve.wait_ge(proj_done, it * 8 + (2 * (T_MLP + 32 * q + 16 + 2 * mb + 1) + half + 1))
                        add_gated(bank[2 + half + 4 * mb], half, bass.ds(it * 2 + mb, 1), bass.ds(it * 2 + (40 + mb), 1),
                                  it * 2 + (8 + 8 * q + mb))

                with dve.Fori(0, 3 if q else 4) as it:
                    for mb in range(2):
                        for kg in range(2):
                            rest_loop(T_MLP + 32 * q + 16 + 2 * mb + kg + 2, it)
                        down_add(it, mb)

            def store_y(j):
                dve.wait_ge(y_done, j + 1)
                dve.tensor_copy(y_tok[:, :, j * P:(j + 1) * P], bank[j % 2][:, :].rearrange("p (t c) -> p t c", t=QB)).then_inc(y_dve, 1)

            rest_loop(T_MLP + 32 + 16 + 2, 3)
            store_y(1)
            rest_loop(T_MLP + 32 + 16 + 3, 3)
            store_y(3)
            down_add(3, 0)
            store_y(5)
            down_add(3, 1)
            store_y(7)


_OUTS = [("y_p", (1, SEQ, DM)), ("y_s", (NS, 1, DM))] + [
    (name + group, (1, *lead, *shape)) for group, lead in (("_p", (1, SEQ)), ("_s", (NS, 1)))
    for name, shape in (("k_a", (H, HD)), ("v_a", (H, HD)), ("k_idx", (HD,)), ("k_b", (H, HD)), ("v_b", (H, HD)), ("logf", (H,)))]


def kernel(**inputs):
    import numpy as _np
    import concourse.bacc as _bacc
    from concourse import mybir as _mybir
    from concourse.bass_utils import run_bass_kernel_spmd as _run

    nc = _bacc.Bacc("TRN2", target_bir_lowering=False, num_devices=1)
    arrays, aps = {}, {}
    for name, value in inputs.items():
        v = _np.ascontiguousarray(value)
        arrays[f"in_{name}"] = v
        aps[name] = nc.dram_tensor(f"in_{name}", v.shape, _mybir.dt.from_np(v.dtype), kind="ExternalInput").ap()
    for name, shape in _OUTS:
        aps[name] = nc.dram_tensor(f"out_{name}", shape, F32, kind="ExternalOutput").ap()
    layer(nc, aps)
    r = _run(nc, [arrays], core_ids=[0])
    return tuple(r.results[0][f"out_{name}"] for name, _ in _OUTS)
```
